# Optimizing a Trainium2 kernel written in Bass

```python
import jax, jax.numpy as jnp
from jax import lax
import numpy as np

D_MODEL = 1024
BATCH = 1
SEQ = 256
DEPTH = 2

N_MIXERS = 2
N_HEADS = 16
HEAD_DIM = D_MODEL // N_HEADS
Q_BLOCK = 128
CONV_WIDTH = 31
D_FF = 7 * D_MODEL // 2
N_EXPERTS = 8
TOP_K = 2
EPS = 1e-6
N_EVEN = (DEPTH + 1) // 2
N_ODD = DEPTH // 2

kernel_name = "fox_conformer_moe_hybrid"

def rmsnorm(x, g):
    xf = x.astype(jnp.float32)
    y = xf * lax.rsqrt(jnp.mean(xf * xf, axis=-1, keepdims=True) + EPS)
    return (y * g.astype(jnp.float32)).astype(x.dtype)

def layernorm(x, g, b):
    xf = x.astype(jnp.float32)
    mu = jnp.mean(xf, axis=-1, keepdims=True)
    xc = xf - mu
    y = xc * lax.rsqrt(jnp.mean(xc * xc, axis=-1, keepdims=True) + EPS)
    return (y * g.astype(jnp.float32) + b.astype(jnp.float32)).astype(x.dtype)

def forgetting_attention(h, w_qkv, w_f, b_f, w_o):
    B, S, _ = h.shape
    q, k, v = jnp.split(h @ w_qkv, 3, axis=-1)
    to_heads = lambda t: t.reshape(B, S, N_HEADS, HEAD_DIM).transpose(0, 2, 1, 3)
    q, k, v = to_heads(q), to_heads(k), to_heads(v)
    log_f = jax.nn.log_sigmoid((h @ w_f + b_f).astype(jnp.float32))
    c = jnp.cumsum(log_f, axis=1).transpose(0, 2, 1)
    nb = S // Q_BLOCK
    qb = q.reshape(B, N_HEADS, nb, Q_BLOCK, HEAD_DIM).transpose(2, 0, 1, 3, 4)
    cb = c.reshape(B, N_HEADS, nb, Q_BLOCK).transpose(2, 0, 1, 3)
    starts = jnp.arange(nb, dtype=jnp.int32) * Q_BLOCK
    k_pos = jnp.arange(S, dtype=jnp.int32)
    scale = HEAD_DIM ** -0.5

    def one_block(args):
        q_i, c_i, start = args
        s = jnp.einsum('bhqd,bhkd->bhqk', q_i, k, preferred_element_type=jnp.float32) * scale
        s = s + (c_i[..., :, None] - c[..., None, :])
        q_pos = start + jnp.arange(Q_BLOCK, dtype=jnp.int32)
        s = jnp.where(k_pos[None, :] <= q_pos[:, None], s, -jnp.inf)
        p = jax.nn.softmax(s, axis=-1)
        return jnp.einsum('bhqk,bhkd->bhqd', p.astype(v.dtype), v)

    o = lax.map(one_block, (qb, cb, starts))
    o = o.transpose(1, 0, 3, 2, 4).reshape(B, S, D_MODEL)
    return o @ w_o

def conformer_conv(h, w_pw1, b_pw1, w_dw, b_dw, ln_g, ln_b, w_pw2, b_pw2):
    u = jax.nn.glu(h @ w_pw1 + b_pw1, axis=-1)
    u = lax.conv_general_dilated(
        u, w_dw[:, None, :].astype(u.dtype), window_strides=(1,),
        padding=[(CONV_WIDTH - 1, 0)],
        dimension_numbers=('NWC', 'WIO', 'NWC'),
        feature_group_count=D_MODEL) + b_dw
    u = jax.nn.silu(layernorm(u, ln_g, ln_b))
    return u @ w_pw2 + b_pw2

def swiglu(h, w_gate, w_up, w_down):
    return (jax.nn.silu(h @ w_gate) * (h @ w_up)) @ w_down

def moe_swiglu(h, w_router, w_gate, w_up, w_down):
    B, S, D = h.shape
    t = h.reshape(B * S, D)
    logits = (t @ w_router).astype(jnp.float32)
    top_v, top_i = lax.top_k(logits, TOP_K)
    gates = jax.nn.softmax(top_v, axis=-1)
    combine = jnp.sum(jax.nn.one_hot(top_i, N_EXPERTS, dtype=jnp.float32) * gates[..., None], axis=1)
    combine = combine.astype(t.dtype)
    out = jnp.zeros_like(t)
    for e in range(N_EXPERTS):
        out = out + combine[:, e:e + 1] * swiglu(t, w_gate[e], w_up[e], w_down[e])
    return out.reshape(B, S, D)

def setup_inputs(seed: int = 0) -> dict:
    key = jax.random.key(seed)
    ks = jax.random.split(key, 32)
    D, F, E, H, W = D_MODEL, D_FF, N_EXPERTS, N_HEADS, CONV_WIDTH
    nrm = lambda k, shape, fan_in: jax.random.normal(k, shape, jnp.float32) * (fan_in ** -0.5)
    gain = lambda k, shape: 1.0 + 0.02 * jax.random.normal(k, shape, jnp.float32)
    bias = lambda k, shape: 0.02 * jax.random.normal(k, shape, jnp.float32)
    return {
        "x": jax.random.normal(ks[0], (BATCH, SEQ, D), jnp.float32),
        "attn_norm": gain(ks[1], (N_EVEN, D)),
        "w_qkv": nrm(ks[2], (N_EVEN, D, 3 * D), D),
        "w_fgate": nrm(ks[3], (N_EVEN, D, H), D),
        "b_fgate": jax.random.uniform(ks[4], (N_EVEN, H), jnp.float32, 1.0, 4.0),
        "w_attn_out": nrm(ks[5], (N_EVEN, D, D), D),
        "conv_norm": gain(ks[6], (N_ODD, D)),
        "w_pw1": nrm(ks[7], (N_ODD, D, 2 * D), D),
        "b_pw1": bias(ks[8], (N_ODD, 2 * D)),
        "w_dw": nrm(ks[9], (N_ODD, W, D), W),
        "b_dw": bias(ks[10], (N_ODD, D)),
        "conv_ln_g": gain(ks[11], (N_ODD, D)),
        "conv_ln_b": bias(ks[12], (N_ODD, D)),
        "w_pw2": nrm(ks[13], (N_ODD, D, D), D),
        "b_pw2": bias(ks[14], (N_ODD, D)),
        "dense_norm": gain(ks[15], (N_EVEN, D)),
        "w_dense_gate": nrm(ks[16], (N_EVEN, D, F), D),
        "w_dense_up": nrm(ks[17], (N_EVEN, D, F), D),
        "w_dense_down": nrm(ks[18], (N_EVEN, F, D), F),
        "moe_norm": gain(ks[19], (N_ODD, D)),
        "w_router": nrm(ks[20], (N_ODD, D, E), D),
        "w_exp_gate": nrm(ks[21], (N_ODD, E, D, F), D),
        "w_exp_up": nrm(ks[22], (N_ODD, E, D, F), D),
        "w_exp_down": nrm(ks[23], (N_ODD, E, F, D), F),
        "final_norm": gain(ks[24], (D,)),
    }

def reference(x, attn_norm, w_qkv, w_fgate, b_fgate, w_attn_out,
              conv_norm, w_pw1, b_pw1, w_dw, b_dw, conv_ln_g, conv_ln_b, w_pw2, b_pw2,
              dense_norm, w_dense_gate, w_dense_up, w_dense_down,
              moe_norm, w_router, w_exp_gate, w_exp_up, w_exp_down,
              final_norm):
    for i in range(DEPTH):
        j = i // N_MIXERS
        if i % N_MIXERS == 0:
            x = x + forgetting_attention(rmsnorm(x, attn_norm[j]), w_qkv[j], w_fgate[j],
                                         b_fgate[j], w_attn_out[j])
            x = x + swiglu(rmsnorm(x, dense_norm[j]), w_dense_gate[j], w_dense_up[j], w_dense_down[j])
        else:
            x = x + conformer_conv(rmsnorm(x, conv_norm[j]), w_pw1[j], b_pw1[j], w_dw[j], b_dw[j],
                                   conv_ln_g[j], conv_ln_b[j], w_pw2[j], b_pw2[j])
            x = x + moe_swiglu(rmsnorm(x, moe_norm[j]), w_router[j], w_exp_gate[j],
                               w_exp_up[j], w_exp_down[j])
    return rmsnorm(x, final_norm)


_drawn_inputs = setup_inputs


def setup_inputs(seed=0):
    import zlib

    import numpy as np

    out = dict(_drawn_inputs(seed))
    spreads = {}
    factors = {'b_pw1': 3.569, 'conv_ln_b': 2.685, 'final_norm': 2.851}
    for name, (base, spread) in spreads.items():
        noise = np.random.default_rng([zlib.crc32(name.encode()), seed]).standard_normal(out[name].shape)
        drawn = base * np.exp(spread * noise) if base else spread * noise
        out[name] = __import__('jax').numpy.asarray(drawn.astype(out[name].dtype))
    for name, factor in factors.items():
        out[name] = (out[name] * factor).astype(out[name].dtype)
    return out
```

```python
from contextlib import ExitStack

import concourse.bass as bass
from concourse import mybir


def build_trunk(nc, x_in, attn_norm, w_qkv, w_fgate, b_fgate, w_attn_out, conv_norm, w_pw1, b_pw1, w_dw, b_dw,
                conv_ln_g, conv_ln_b, w_pw2, b_pw2, dense_norm, w_dense_gate, w_dense_up, w_dense_down,
                moe_norm, w_router, w_exp_gate, w_exp_up, w_exp_down, final_norm, out):
    f32, f32r, i32, u32 = mybir.dt.float32, mybir.dt.float32r, mybir.dt.int32, mybir.dt.uint32
    ALU, ACT, AX = mybir.AluOpType, mybir.ActivationFunctionType, mybir.AxisListType

    P = 128
    _, SEQ, D = x_in.shape
    T = SEQ // P
    KD = D // P
    H = w_fgate.shape[2]
    HD = D // H
    F = w_dense_gate.shape[2]
    E = w_exp_gate.shape[1]
    TAPS = w_dw.shape[1]
    EPS = 1e-6
    NC = 512
    UNIT = 4 * NC
    CH = F // NC
    RAW, SPLIT = 6, 3
    MASKED = -1e30
    CAP = P
    EXTRA = 4
    PASSES = E + EXTRA

    U_QKV = 0
    U_WO = U_QKV + 2 * (3 * D // NC)
    U_DENSE = U_WO + 2 * (D // NC)
    U_PW1 = U_DENSE + 6 * CH
    U_PW2 = U_PW1 + 2 * (2 * D // NC)
    U_EXP = U_PW2 + 2 * (D // NC)
    U_PASS = 6 * CH
    ROUNDS = U_PASS // RAW
    assert U_PASS % RAW == 0 and RAW % SPLIT == 0

    ctx = ExitStack()
    with ctx:
        def sb(name, shape, dt=f32, where=ctx):
            return where.enter_context(nc.sbuf_tensor(name, shape, dt))

        def sem(name):
            return ctx.enter_context(nc.semaphore(name))

        raw = sb("raw", [P, RAW, UNIT])
        w_hi = sb("w_hi", [P, SPLIT, UNIT], f32r)
        w_lo = sb("w_lo", [P, SPLIT, UNIT], f32r)
        x = sb("x", [P, T, D])
        rows = sb("rows", [P, T, D])
        c_hi = sb("c_hi", [P, KD, SEQ], f32r)
        c_lo = sb("c_lo", [P, KD, SEQ], f32r)
        gate = sb("gate", [P, T, NC])
        hid = sb("hid", [P, T, NC])
        h_hi = sb("h_hi", [P, T, 4, P], f32r)
        h_lo = sb("h_lo", [P, T, 4, P], f32r)
        bc = sb("bc", [P, 3, D])
        ident = sb("ident", [P, P])
        ones = sb("ones", [P, P])
        mean_w = sb("mean_w", [P, P])
        upto = sb("upto", [P, P])
        before = sb("before", [P, P])
        slot_row = sb("slot_row", [P, P])
        slot_col = sb("slot_col", [P, 1])
        iota_i = sb("iota_i", [P, P], i32)
        iota_c = sb("iota_c", [P, 1], i32)
        eight = sb("eight", [P, E])
        zero_r = sb("zero_r", [P, NC], f32r)
        ss = sb("ss", [P, T])
        ms = sb("ms", [P, T])
        rt = sb("rt", [P, T])
        rs = sb("rs", [P, T])
        rq = sb("rq", [P, T])
        wf = sb("wf", [P, KD, H])
        wf_hi = sb("wf_hi", [P, KD, H], f32r)
        wf_lo = sb("wf_lo", [P, KD, H], f32r)
        wr = sb("wr", [P, KD, E])
        wr_hi = sb("wr_hi", [P, KD, E], f32r)
        wr_lo = sb("wr_lo", [P, KD, E], f32r)
        bf_bc = sb("bf_bc", [P, H])

        sm, pr = gate[:, :, 0:3 * P], hid[:, :, 0:3 * P]

        with ExitStack() as region:
            q_even = sb("q_even", [P, KD, SEQ], f32, region)
            q_odd = sb("q_odd", [P, KD, SEQ], f32, region)
            k_T = sb("k_T", [P, KD, SEQ], f32, region)
            v_sb = sb("v_sb", [P, T, D], f32, region)
            pr_T = sb("pr_T", [P, 2, 3 * P], f32, region)
            mask = sb("mask", [P, 3 * P], f32, region)
            c_pad = sb("c_pad", [P, T, P], f32, region)
            neg_cT = sb("neg_cT", [P, SEQ], f32, region)
            nm = sb("nm", [P, H, T], f32, region)
            psum_rows = sb("psum_rows", [P, T, H], f32, region)
            inv_rows = sb("inv_rows", [P, T, H], f32, region)
            z = sb("z", [P, T, H], f32, region)
            z_min = sb("z_min", [P, T, H], f32, region)
            z_abs = sb("z_abs", [P, T, H], f32, region)
            z_exp = sb("z_exp", [P, T, H], f32, region)
            z_log = sb("z_log", [P, T, H], f32, region)
            log_f = sb("log_f", [P, T, H], f32, region)
        PAD = TAPS - 1
        with ExitStack() as region:
            glu = sb("glu", [P, KD, PAD + SEQ], f32, region)
            sig = sb("sig", [P, 4, SEQ], f32, region)
            cv = sb("cv", [P, KD, SEQ], f32, region)
            sq = sb("sq", [P, KD, SEQ], f32, region)
            prm = sb("prm", [P, 3, P], f32, region)
            prm_T = sb("prm_T", [P, 3 * P], f32, region)
            var_e = sb("var_e", [P, SEQ], f32, region)
            std = sb("std", [P, SEQ], f32, region)
            rstd = sb("rstd", [P, SEQ], f32, region)
        r_hi = sb("r_hi", [P, T, D], f32r)
        r_lo = sb("r_lo", [P, T, D], f32r)
        rank_T = sb("rank_T", [P, PASSES, SEQ])
        y_hi = sb("y_hi", [P, D], f32r)
        y_lo = sb("y_lo", [P, D], f32r)
        pick = sb("pick", [P, T, P], f32r)
        put = sb("put", [P, SEQ], f32r)
        slot_w = sb("slot_w", [P, 1])
        lg = sb("lg", [P, T, E])
        top = sb("top", [P, T, E])
        top_i = sb("top_i", [P, T, E], u32)
        top_f = sb("top_f", [P, T, E])
        dlt = sb("dlt", [P, T])
        ex = sb("ex", [P, T])
        p_top = sb("p_top", [P, 2, T])
        oh = sb("oh", [P, 2, T, E])
        chosen = sb("chosen", [P, T, E])
        comb = sb("comb", [P, T, PASSES])
        comb_2 = sb("comb_2", [P, T, E])
        rank = sb("rank", [P, T, PASSES])
        over = sb("over", [P, E])
        nth = sb("nth", [P, E])
        sel = sb("sel", [P, EXTRA, E])
        prod = sb("prod", [P, T, EXTRA, E])
        part = sb("part", [P, T, EXTRA])
        plan_f = sb("plan_f", [P, EXTRA + 1])
        plan = sb("plan", [P, EXTRA + 1], i32)
        comb_r = sb("comb_r", [P, PASSES, T, 2], f32r)

        ps = ctx.enter_context(nc.psum_tensor("ps", [P, 8, NC], f32))

        raw_in = [sem(f"raw_in{i}") for i in range(RAW)]
        hi_ready = sem("hi_ready")
        split_ready = sem("split_ready")
        unit_used = sem("unit_used")
        consts_ready = sem("consts_ready")
        gp_step = sem("gp_step")
        x_in_sem = sem("x_in_sem")
        small_in = [sem(f"small_in{i}") for i in range(3)]
        bc_in = [sem(f"bc_in{i}") for i in range(6)]
        dve_step = sem("dve_step")
        x_ready = sem("x_ready")
        ss_ready = sem("ss_ready")
        ms_ready = sem("ms_ready")
        rt_ready = sem("rt_ready")
        rows_ready = sem("rows_ready")
        turn_mm = sem("turn_mm")
        c_hi_ready = sem("c_hi_ready")
        c_ready = sem("c_ready")
        small_hi = sem("small_hi")
        small_split = sem("small_split")
        q_out = sem("q_out")
        k_out = sem("k_out")
        v_out = sem("v_out")
        fg_mm = sem("fg_mm")
        z_ready = sem("z_ready")
        z_exp_ready = sem("z_exp_ready")
        z_log_ready = sem("z_log_ready")
        log_f_ready = sem("log_f_ready")
        c_mm = sem("c_mm")
        c_out = sem("c_out")
        cT_mm = sem("cT_mm")
        cT_out = sem("cT_out")
        s_mm = sem("s_mm")
        sm_ready = sem("sm_ready")
        max_ready = sem("max_ready")
        exp_ready = sem("exp_ready")
        prT_mm = sem("prT_mm")
        prT_ready = sem("prT_ready")
        pv_mm = sem("pv_mm")
        silu_ready = sem("silu_ready")
        hid_ready = sem("hid_ready")
        hidT_mm = sem("hidT_mm")
        h_hi_ready = sem("h_hi_ready")
        h_ready = sem("h_ready")
        prm_in = sem("prm_in")
        prm_clear = sem("prm_clear")
        prm_mm = sem("prm_mm")
        prm_ready = sem("prm_ready")
        glu_clear = sem("glu_clear")
        sig_ready = sem("sig_ready")
        glu_ready = sem("glu_ready")
        conv_step = sem("conv_step")
        mean_mm = sem("mean_mm")
        dev_ready = sem("dev_ready")
        sq_ready = sem("sq_ready")
        var_mm = sem("var_mm")
        var_ready = sem("var_ready")
        std_ready = sem("std_ready")
        ln_ready = sem("ln_ready")
        act_ready = sem("act_ready")
        r_hi_ready = sem("r_hi_ready")
        r_ready = sem("r_ready")
        lg_mm = sem("lg_mm")
        dlt_ready = sem("dlt_ready")
        ex_ready = sem("ex_ready")
        chosen_ready = sem("chosen_ready")
        rank_mm = sem("rank_mm")
        rank_ready = sem("rank_ready")
        comb_hi_ready = sem("comb_hi_ready")
        comb_ready = sem("comb_ready")
        rankT_mm = sem("rankT_mm")
        rankT_a = sem("rankT_a")
        rankT_b = sem("rankT_b")
        plan_ready = sem("plan_ready")
        pick_ready = sem("pick_ready")
        put_ready = sem("put_ready")
        gather_mm = sem("gather_mm")
        gather_a = sem("gather_a")
        gather_v = sem("gather_v")
        slot_w_mm = sem("slot_w_mm")
        slot_w_ready = sem("slot_w_ready")
        y_hi_ready = sem("y_hi_ready")
        y_ready = sem("y_ready")
        scatter_mm = sem("scatter_mm")
        moe_mm = sem("moe_mm")
        stored = sem("stored")

        DENSE = dict(tiles=T, gate=0, up=2, y=4)
        EXPERT = dict(tiles=1, gate=0, up=1, y=2)
        SUM = 4
        WD = w_dw.shape[1] * KD
        A_PW1, A_DW, A_G, A_B = 2 * P, 2 * P + 2 * KD, 2 * P + 3 * KD, 2 * P + 4 * KD

        block = ctx.enter_context(nc.Block())

        @block.sync
        def _(sp):
            def load(s, src, r=0):
                if s >= RAW or not isinstance(r, int):
                    sp.wait_ge(split_ready, s - RAW + 1 + RAW * r)
                k = src.shape[0] // P
                sp.dma_start(raw[:, s % RAW, :].rearrange("p (k n) -> p k n", k=k),
                             src.rearrange("(k p) n -> p k n", p=P)).then_inc(raw_in[s % RAW], 16)

            def load_columns(s, w, c, r=0):
                for half in range(2):
                    load(s + half, w[half * D // 2:(half + 1) * D // 2, bass.ds(c * NC, NC)], r)

            def load_swiglu(s, wg, wu, wd, r=0):
                def down(s, c, r):
                    for half in range(2):
                        load(s + half, wd[bass.ds(c * NC + half * (NC // 2), NC // 2), :], r)
                load_columns(s, wg, 0, r)
                load_columns(s + 2, wu, 0, r)
                with sp.Fori(0, CH - 1) as i:
                    load_columns(s + 4, wg, i + 1, r + i)
                    load_columns(s + 6, wu, i + 1, r + i)
                    down(s + 8, i, r + i)
                down(s + 6 * CH - 2, CH - 1, r)

            for c in range(3 * D // NC):
                load_columns(U_QKV + 2 * c, w_qkv[0], c)
            for c in range(D // NC):
                load_columns(U_WO + 2 * c, w_attn_out[0], c)
            load_swiglu(U_DENSE, w_dense_gate[0], w_dense_up[0], w_dense_down[0])
            for g, c in enumerate((0, 2, 1, 3)):
                load_columns(U_PW1 + 2 * g, w_pw1[0], c)
            for c in range(D // NC):
                load_columns(U_PW2 + 2 * c, w_pw2[0], c)

            def load_expert(e, p):
                load_swiglu(U_EXP, w_exp_gate[0, e], w_exp_up[0, e], w_exp_down[0, e], ROUNDS * p)

            with sp.Fori(0, E) as p:
                load_expert(p, p)
            sp.wait_ge(plan_ready, 1)
            extra = sp.value_load(plan[0:1, EXTRA:EXTRA + 1], min_val=0, max_val=EXTRA - 1)
            with sp.If(extra > 0):
                with sp.Fori(0, extra) as j:
                    e = sp.value_load(plan[0:1, bass.ds(j, 1)], min_val=0, max_val=E - 1)
                    load_expert(e, j + E)
            load_columns(U_EXP, w_exp_gate[0, 0], 0, ROUNDS * (extra + E))

            for t in range(T):
                sp.wait_ge(rows_ready, 5 * T + t + 1)
                sp.dma_start(out[0, t * P:(t + 1) * P, :], rows[:, t, :]).then_inc(stored, 16)
            sp.wait_ge(stored, 16 * T)

        @block.gpsimd
        def _(gp):
            def triangle(tile, fill, op, row=-1, column=1):
                return nc.gpsimd.affine_select(out=tile, in_=tile, compare_op=op, fill=fill, base=0,
                                               pattern=[[column, P]], channel_multiplier=row)
            for i, row in enumerate((attn_norm[0], dense_norm[0], conv_norm[0])):
                gp.dma_start(bc[:, i, :], row.partition_broadcast(P)).then_inc(bc_in[i], 16)
            gp.dma_start(wf[:, :, :], w_fgate[0].rearrange("(k p) n -> p k n", p=P)).then_inc(small_in[0], 16)
            gp.dma_start(bf_bc[:, :], b_fgate[0].partition_broadcast(P)).then_inc(small_in[1], 16)
            gp.dma_start(wr[:, :, :], w_router[0].rearrange("(k p) n -> p k n", p=P)).then_inc(small_in[2], 16)
            for i, (tile, value) in enumerate((
                    (ident[:, :], 0.0), (ones[:, :], 1.0), (mean_w[:, :], 1.0 / D), (upto[:, :], 1.0),
                    (before[:, :], 1.0), (mask[:, :], 0.0), (c_pad[:, :, :], 0.0), (zero_r[:, :].bitcast(f32), 0.0),
                    (q_even[P // 2:P, :, :], 0.0), (q_odd[0:P // 2, :, :], 0.0))):
                if i:
                    gp.wait_ge(gp_step, i)
                nc.gpsimd.memset(tile, value).then_inc(gp_step, 1)
            gp.wait_ge(gp_step, 10)
            nc.gpsimd.iota(iota_i[:, :], [[1, P]], base=1, channel_multiplier=0).then_inc(gp_step, 1)
            gp.wait_ge(gp_step, 11)
            nc.gpsimd.iota(iota_c[:, :], [[0, 1]], base=1, channel_multiplier=1).then_inc(gp_step, 1)
            gp.wait_ge(gp_step, 12)
            triangle(ident[:, :], 1.0, ALU.not_equal).then_inc(consts_ready, 1)
            gp.wait_ge(consts_ready, 1)
            triangle(upto[:, :], 0.0, ALU.is_ge).then_inc(consts_ready, 1)
            gp.wait_ge(consts_ready, 2)
            triangle(before[:, :], 0.0, ALU.is_gt).then_inc(consts_ready, 1)
            for i, at in enumerate((0, 2 * P)):
                gp.wait_ge(consts_ready, 3 + i)
                triangle(mask[:, at:at + P], MASKED, ALU.is_ge, row=1, column=-1).then_inc(consts_ready, 1)
            gp.wait_ge(consts_ready, 5)
            nc.gpsimd.tensor_copy(slot_row[:, :], iota_i[:, :]).then_inc(consts_ready, 1)
            gp.wait_ge(consts_ready, 6)
            nc.gpsimd.tensor_copy(slot_col[:, :], iota_c[:, :]).then_inc(consts_ready, 1)
            gp.wait_ge(consts_ready, 7)

            gp.wait_ge(rows_ready, 2 * T)
            nc.gpsimd.memset(prm[:, :, :], 0.0).then_inc(prm_clear, 1)
            gp.wait_ge(prm_clear, 1)
            nc.gpsimd.memset(glu[:, :, 0:PAD], 0.0).then_inc(glu_clear, 1)
            taps = w_dw[0].rearrange("a (b c) -> (a b) c", c=P)
            gp.dma_start(prm[:, 0, :], taps[0:P, :]).then_inc(prm_in, 16)
            gp.dma_start(prm[0:WD - P, 1, :], taps[P:WD, :]).then_inc(prm_in, 16)
            at = 0
            for v, n in ((b_pw1, 2 * KD), (b_dw, KD), (conv_ln_g, KD), (conv_ln_b, KD)):
                gp.dma_start(prm[at:at + n, 2, :], v[0].rearrange("(b c) -> b c", c=P)).then_inc(prm_in, 16)
                at += n
            gp.dma_start(bc[:, 0, :], moe_norm[0].partition_broadcast(P)).then_inc(bc_in[3], 16)
            gp.wait_ge(rows_ready, 3 * T)
            gp.dma_start(bc[:, 1, :], final_norm.partition_broadcast(P)).then_inc(bc_in[4], 16)
            gp.wait_ge(rows_ready, 4 * T)
            gp.dma_start(bc[:, 2, :], b_pw2[0].partition_broadcast(P)).then_inc(bc_in[5], 16)

        @block.scalar
        def _(act):
            def high(s, r=0):
                act.wait_ge(raw_in[s % RAW], 16 * (s // RAW + 1) + 16 * r)
                if s >= SPLIT or not isinstance(r, int):
                    act.wait_ge(unit_used, s - SPLIT + 1 + RAW * r)
                nc.scalar.copy(w_hi[:, s % SPLIT, :], raw[:, s % RAW, :]).then_inc(hi_ready, 1)

            def norm_sums(k):
                for t in range(T):
                    if k == 0:
                        act.wait_ge(x_in_sem, 16)
                    else:
                        act.wait_ge(x_ready, 2 * k)
                    nc.scalar.activation(rows[:, t, :], x[:, t, :], ACT.Square,
                                         accum_out=ss[:, t:t + 1]).then_inc(ss_ready, 1)
                act.wait_ge(ms_ready, k + 1)
                nc.scalar.activation(rt[:, :], ms[:, :], ACT.Sqrt).then_inc(rt_ready, 1)

            def turned_high(k):
                for g in range(4):
                    t, half = g // 2, g % 2
                    act.wait_ge(turn_mm, 4 * k + g + 1)
                    nc.scalar.copy(c_hi[:, 4 * half:4 * half + 4, t * P:(t + 1) * P],
                                   ps[:, g, :].rearrange("p (b m) -> p b m", b=4)).then_inc(c_hi_ready, 1)

            def hid_high(q, tiles, up):
                act.wait_ge(hidT_mm, q + 1)
                nc.scalar.copy(h_hi[:, 0:tiles].rearrange("p t b m -> p t (b m)"),
                               ps[:, up:up + tiles, :]).then_inc(h_hi_ready, 1)

            def silu(s, tiles, gate_bank, r):
                act.wait_ge(unit_used, s + 2 + RAW * r)
                nc.scalar.activation(gate[:, 0:tiles, :], ps[:, gate_bank:gate_bank + tiles, :],
                                     ACT.Silu).then_inc(silu_ready, 1)

            def swiglu_first(s, q, L, r=0):
                high(s + 2, r)
                high(s + 3, r)
                silu(s, L["tiles"], L["gate"], r)
                high(s + 4, r)
                high(s + 5, r)

            def swiglu_loop(s, q, L, r=0):
                with act.Fori(0, CH - 1) as i:
                    hid_high(q + i, L["tiles"], L["up"])
                    high(s + 6, r + i)
                    high(s + 7, r + i)
                    silu(s + 4, L["tiles"], L["gate"], r + i)
                    for j in range(8, 12):
                        high(s + j, r + i)

            act.dma_start(x[:, :, :], x_in[0].rearrange("(t p) d -> p t d", p=P)).then_inc(x_in_sem, 16)
            norm_sums(0)
            for s in range(3):
                high(s)
            turned_high(0)
            act.wait_ge(small_in[0], 16)
            nc.scalar.copy(wf_hi[:, :, :], wf[:, :, :]).then_inc(small_hi, 1)
            act.wait_ge(small_in[2], 16)
            nc.scalar.copy(wr_hi[:, :, :], wr[:, :, :]).then_inc(small_hi, 1)

            for g in range(6):
                if g:
                    high(2 * g + 1)
                    high(2 * g + 2)
                if g < 2:
                    act.wait_ge(unit_used, U_QKV + 2 * g + 2)
                    if g == 0:
                        act.wait_ge(gp_step, 12)
                    cols = slice(4 * g, 4 * g + 4)
                    banks = slice(4 * (g % 2), 4 * (g % 2) + 4)
                    nc.scalar.activation(q_even[0:HD, cols, :], ps[0:HD, banks, 0:SEQ], ACT.Copy,
                                         scale=HD ** -0.5)
                    nc.scalar.activation(q_odd[HD:P, cols, :], ps[HD:P, banks, 0:SEQ], ACT.Copy,
                                         scale=HD ** -0.5).then_inc(q_out, 1)
                if g >= 4:
                    act.wait_ge(unit_used, U_QKV + 2 * g + 2)
                    h = g - 4
                    nc.scalar.copy(v_sb[:, :, h * NC:(h + 1) * NC], ps[:, 2 * h:2 * h + 2, :]).then_inc(v_out, 1)
            high(U_WO + 1)
            high(U_WO + 2)

            act.wait_ge(z_ready, 1)
            nc.scalar.activation(z_exp[:, :, :], z_abs[:, :, :], ACT.Exp, scale=-1.0).then_inc(z_exp_ready, 1)
            act.wait_ge(z_exp_ready, 1)
            nc.scalar.activation(z_log[:, :, :], z_exp[:, :, :], ACT.Ln, bias=1.0).then_inc(z_log_ready, 1)

            def prob_T(h):
                act.wait_ge(prT_mm, h + 1)
                if h >= 2:
                    act.wait_ge(pv_mm, h - 1)
                nc.scalar.copy(pr_T[:, h % 2, :], ps[:, 2 + h % 2, 0:3 * P]).then_inc(prT_ready, 1)

            for h in range(H):
                act.wait_ge(max_ready, h + 1)
                if h >= 2:
                    act.wait_ge(prT_mm, h - 1)
                nc.scalar.activation(pr[:, h % 2, 0:P], sm[:, h % 2, 0:P], ACT.Exp, bias=nm[:, h, 0:1],
                                     accum_out=psum_rows[:, 0, h:h + 1])
                nc.scalar.activation(pr[:, h % 2, P:3 * P], sm[:, h % 2, P:3 * P], ACT.Exp, bias=nm[:, h, 1:2],
                                     accum_out=psum_rows[:, 1, h:h + 1]).then_inc(exp_ready, 1)
                if h:
                    prob_T(h - 1)
            prob_T(H - 1)
            turned_high(1)
            high(U_WO + 3)
            for s in range(U_WO + 4, U_WO + 6):
                high(s)

            norm_sums(1)
            turned_high(2)
            swiglu_first(U_DENSE, 0, DENSE)
            swiglu_loop(U_DENSE, 0, DENSE)
            hid_high(CH - 1, T, DENSE["up"])
            high(U_PW1)
            high(U_PW1 + 1)

            norm_sums(2)
            turned_high(3)
            high(U_PW1 + 2)
            for j in range(2):
                for s in range(U_PW1 + 4 * j + 3, U_PW1 + 4 * j + 6):
                    high(s)
                act.wait_ge(unit_used, U_PW1 + 4 * j + 4)
                if j == 0:
                    act.wait_ge(prm_ready, 1)
                else:
                    act.wait_ge(glu_ready, 4)
                for c in range(4):
                    ch = A_PW1 + KD + 4 * j + c
                    nc.scalar.activation(sig[:, c, :], ps[:, 4 + c, 0:SEQ], ACT.Sigmoid,
                                         bias=prm_T[:, ch:ch + 1]).then_inc(sig_ready, 1)
                high(U_PW1 + 4 * j + 6)
            for c in range(KD):
                act.wait_ge(dev_ready, c + 1)
                nc.scalar.activation(sq[:, c, :], cv[:, c, :], ACT.Square).then_inc(sq_ready, 1)
            act.wait_ge(var_ready, 1)
            nc.scalar.activation(std[:, :], var_e[:, :], ACT.Sqrt).then_inc(std_ready, 1)
            for c in range(KD):
                act.wait_ge(ln_ready, c + 1)
                nc.scalar.activation(sq[:, c, :], cv[:, c, :], ACT.Silu, bias=prm_T[:, A_B + c:A_B + c + 1],
                                     scale=prm_T[:, A_G + c:A_G + c + 1]).then_inc(act_ready, 1)
            for c in range(KD):
                act.wait_ge(act_ready, c + 1)
                nc.scalar.copy(c_hi[:, c, :], sq[:, c, :]).then_inc(c_hi_ready, 1)
            for s in range(U_PW2 + 3, U_EXP + 2):
                high(s)

            norm_sums(3)
            for t in range(T):
                act.wait_ge(rows_ready, 4 * T + t + 1)
                nc.scalar.copy(r_hi[:, t, :], rows[:, t, :]).then_inc(r_hi_ready, 1)
            turned_high(4)
            act.wait_ge(dlt_ready, 1)
            nc.scalar.activation(ex[:, :], dlt[:, :], ACT.Exp).then_inc(ex_ready, 1)
            act.wait_ge(rankT_mm, 1)
            nc.scalar.copy(rank_T[:, 0:8, :], ps[:, 0:4, :].rearrange("p b (e s) -> p b e s", e=2)
                           .rearrange("p b e s -> p (b e) s")).then_inc(rankT_a, 1)

            def gathered(p, quarter):
                act.wait_ge(gather_mm, 4 * p + quarter + 1)
                dst = c_hi if quarter == 0 else c_lo
                nc.scalar.copy(dst[:, 0:4, 0:P], ps[:, 0, :].rearrange("p (b m) -> p b m", b=4)).then_inc(gather_a, 1)

            gathered(0, 0)
            gathered(0, 2)

            def expert_pass(p):
                r, q = ROUNDS * p, CH + CH * p
                swiglu_first(U_EXP, q, EXPERT, r)
                swiglu_loop(U_EXP, q, EXPERT, r)
                hid_high(q + CH - 1, 1, EXPERT["up"])
                gathered(p + 1, 0)
                high(U_EXP + U_PASS, r)
                gathered(p + 1, 2)
                high(U_EXP + U_PASS + 1, r)
                act.wait_ge(unit_used, U_EXP + U_PASS + RAW * r)
                act.wait_ge(slot_w_ready, p + 1)
                nc.scalar.activation(y_hi[:, :], ps[:, 2:4, :].rearrange("p b n -> p (b n)"), ACT.Copy,
                                     scale=slot_w[:, 0:1]).then_inc(y_hi_ready, 1)

            with act.Fori(0, E) as p:
                expert_pass(p)
            act.wait_ge(plan_ready, 1)
            extra = act.value_load(plan[0:1, EXTRA:EXTRA + 1], min_val=0, max_val=EXTRA - 1)
            with act.If(extra > 0):
                with act.Fori(0, extra) as j:
                    expert_pass(j + E)
            norm_sums(4)

        @block.vector
        def _(dve):
            chain = [0]

            def link(ins):
                chain[0] += 1
                ins.then_inc(dve_step, 1)
                dve.wait_ge(dve_step, chain[0])

            def low(s, r=0):
                dve.wait_ge(hi_ready, s + 1 + RAW * r)
                nc.vector.tensor_tensor(w_lo[:, s % SPLIT, :], raw[:, s % RAW, :], w_hi[:, s % SPLIT, :],
                                        ALU.subtract).then_inc(split_ready, 1)

            def norm(k, slot, gain_in):
                dve.wait_ge(ss_ready, T * (k + 1))
                nc.vector.tensor_scalar(ms[:, :], ss[:, :], 1.0 / D, EPS, ALU.mult, ALU.add).then_inc(ms_ready, 1)
                dve.wait_ge(rt_ready, k + 1)
                dve.wait_ge(ms_ready, k + 1)
                link(nc.vector.reciprocal(rs[:, :], rt[:, :]))
                link(nc.vector.tensor_tensor(rq[:, :], rs[:, :], rs[:, :], ALU.mult))
                link(nc.vector.tensor_tensor(rq[:, :], rq[:, :], ms[:, :], ALU.mult))
                link(nc.vector.tensor_scalar(rq[:, :], rq[:, :], -0.5, 1.5, ALU.mult, ALU.add))
                link(nc.vector.tensor_tensor(rs[:, :], rs[:, :], rq[:, :], ALU.mult))
                dve.wait_ge(gain_in, 16)
                for t in range(T):
                    nc.vector.scalar_tensor_tensor(rows[:, t, :], x[:, t, :], rs[:, t:t + 1], bc[:, slot, :],
                                                   ALU.mult, ALU.mult).then_inc(rows_ready, 1)

            def turned_low(k, base):
                for g in range(4):
                    t, half = g // 2, g % 2
                    dve.wait_ge(c_hi_ready, base + g + 1)
                    nc.vector.tensor_tensor(c_lo[:, 4 * half:4 * half + 4, t * P:(t + 1) * P],
                                            ps[:, g, :].rearrange("p (b m) -> p b m", b=4),
                                            c_hi[:, 4 * half:4 * half + 4, t * P:(t + 1) * P],
                                            ALU.subtract).then_inc(c_ready, 1)

            def add_projection(s, h):
                dve.wait_ge(unit_used, s + 2 * h + 2)
                return nc.vector.tensor_tensor(x[:, :, h * NC:(h + 1) * NC], x[:, :, h * NC:(h + 1) * NC],
                                               ps[:, 4 + 2 * h:6 + 2 * h, :], ALU.add).then_inc(x_ready, 1)

            def hid_low(q, tiles, up):
                dve.wait_ge(h_hi_ready, q + 1)
                nc.vector.tensor_tensor(h_lo[:, 0:tiles].rearrange("p t b m -> p t (b m)"),
                                        ps[:, up:up + tiles, :],
                                        h_hi[:, 0:tiles].rearrange("p t b m -> p t (b m)"),
                                        ALU.subtract).then_inc(h_ready, 1)

            def hidden(s, q, tiles, up, r):
                dve.wait_ge(unit_used, s + 2 + RAW * r)
                dve.wait_ge(silu_ready, q + 1)
                nc.vector.tensor_tensor(hid[:, 0:tiles, :], gate[:, 0:tiles, :], ps[:, up:up + tiles, :],
                                        ALU.mult).then_inc(hid_ready, 1)

            def swiglu_first(s, q, L, r=0):
                for j in range(2, 6):
                    low(s + j, r)
                hidden(s + 2, q, L["tiles"], L["up"], r)

            def swiglu_loop(s, q, L, r=0):
                with dve.Fori(0, CH - 1) as i:
                    hid_low(q + i, L["tiles"], L["up"])
                    for j in range(6, 10):
                        low(s + j, r + i)
                    hidden(s + 6, q + 1 + i, L["tiles"], L["up"], r + i)
                    low(s + 10, r + i)
                    low(s + 11, r + i)

            norm(0, 0, bc_in[0])
            for s in range(3):
                low(s)
            turned_low(0, 0)
            dve.wait_ge(small_hi, 1)
            nc.vector.tensor_tensor(wf_lo[:, :, :], wf[:, :, :], wf_hi[:, :, :], ALU.subtract).then_inc(small_split, 1)
            dve.wait_ge(small_hi, 2)
            nc.vector.tensor_tensor(wr_lo[:, :, :], wr[:, :, :], wr_hi[:, :, :], ALU.subtract).then_inc(small_split, 1)

            for g in range(6):
                if g:
                    low(2 * g + 1)
                    low(2 * g + 2)
                if g in (2, 3):
                    dve.wait_ge(unit_used, U_QKV + 2 * g + 2)
                    banks = slice(4 * (g % 2), 4 * (g % 2) + 4)
                    nc.vector.tensor_copy(k_T[:, 4 * (g - 2):4 * (g - 2) + 4, :],
                                          ps[:, banks, 0:SEQ]).then_inc(k_out, 1)
            low(U_WO + 1)
            low(U_WO + 2)

            dve.wait_ge(fg_mm, 1)
            dve.wait_ge(small_in[1], 16)
            link(nc.vector.tensor_tensor(z[:, :, :], ps[:, 4, 0:T * H].rearrange("p (t h) -> p t h", t=T),
                                         bf_bc[:, None, :].to_broadcast([P, T, H]), ALU.add))
            nc.vector.tensor_scalar(z_min[:, :, :], z[:, :, :], 0.0, None, ALU.min)
            nc.vector.scalar_tensor_tensor(z_abs[:, :, :], z[:, :, :], -1.0, z[:, :, :],
                                           ALU.mult, ALU.max).then_inc(z_ready, 1)
            dve.wait_ge(z_log_ready, 1)
            dve.wait_ge(z_ready, 1)
            nc.vector.tensor_tensor(log_f[:, :, :], z_min[:, :, :], z_log[:, :, :],
                                    ALU.subtract).then_inc(log_f_ready, 1)
            dve.wait_ge(c_mm, 1)
            dve.wait_ge(gp_step, 12)
            nc.vector.tensor_copy(c_pad[:, :, 0:H], ps[:, 5, 0:T * H].rearrange("p (t h) -> p t h", t=T))\
              .then_inc(c_out, 1)
            dve.wait_ge(cT_mm, 1)
            nc.vector.tensor_scalar(neg_cT[:, :], ps[:, 6, 0:SEQ], -1.0, None, ALU.mult).then_inc(cT_out, 1)
            dve.wait_ge(c_out, 1)
            dve.wait_ge(consts_ready, 7)
            for h in range(H):
                dve.wait_ge(s_mm, h + 1)
                if h >= 2:
                    dve.wait_ge(exp_ready, h - 1)
                nc.vector.scalar_tensor_tensor(sm[:, h % 2, 0:P], ps[:, h % 2, 0:P], c_pad[:, 0, h:h + 1],
                                               mask[:, 0:P], ALU.add, ALU.add)
                nc.vector.scalar_tensor_tensor(sm[:, h % 2, P:3 * P], ps[:, h % 2, P:3 * P], c_pad[:, 1, h:h + 1],
                                               mask[:, P:3 * P], ALU.add, ALU.add).then_inc(sm_ready, 1)
                dve.wait_ge(sm_ready, h + 1)
                nc.vector.tensor_reduce(nm[:, h, 0:1], sm[:, h % 2, 0:P], AX.X, ALU.max, negate=True)
                nc.vector.tensor_reduce(nm[:, h, 1:2], sm[:, h % 2, P:3 * P], AX.X, ALU.max,
                                        negate=True).then_inc(max_ready, 1)
            dve.wait_ge(exp_ready, H)
            link(nc.vector.reciprocal(inv_rows[:, :, :], psum_rows[:, :, :]))
            dve.wait_ge(pv_mm, H)
            for t in range(T):
                nc.vector.tensor_tensor(rows[:, t, :].rearrange("p (h d) -> p h d", h=H),
                                        ps[:, 4 + 2 * t:6 + 2 * t, :].rearrange("p b (h d) -> p (b h) d", d=HD),
                                        inv_rows[:, t, :, None].to_broadcast([P, H, HD]),
                                        ALU.mult).then_inc(rows_ready, 1)
            turned_low(1, 4)
            low(U_WO + 3)
            low(U_WO + 4)
            add_projection(U_WO, 0)
            low(U_WO + 5)
            add_projection(U_WO, 1)

            norm(1, 1, bc_in[1])
            turned_low(2, 8)
            swiglu_first(U_DENSE, 0, DENSE)
            swiglu_loop(U_DENSE, 0, DENSE)
            hid_low(CH - 1, T, DENSE["up"])
            low(U_PW1)
            low(U_PW1 + 1)
            dve.wait_ge(unit_used, U_DENSE + U_PASS)
            for t in range(T):
                nc.vector.tensor_tensor(x[:, t, :], x[:, t, :],
                                        ps[:, 4 + 2 * t:6 + 2 * t, :].rearrange("p b n -> p (b n)"),
                                        ALU.add).then_inc(x_ready, 1)

            norm(2, 2, bc_in[2])
            turned_low(3, 12)
            dve.wait_ge(prm_mm, 1)
            nc.vector.tensor_copy(prm_T[:, :], ps[:, 7, 0:3 * P]).then_inc(prm_ready, 1)
            low(U_PW1 + 2)
            dve.wait_ge(prm_ready, 1)
            dve.wait_ge(glu_clear, 1)
            for j in range(2):
                for s in range(U_PW1 + 4 * j + 3, U_PW1 + 4 * j + 6):
                    low(s)
                for c in range(4):
                    ch = A_PW1 + 4 * j + c
                    dve.wait_ge(sig_ready, 4 * j + c + 1)
                    nc.vector.scalar_tensor_tensor(glu[:, 4 * j + c, PAD:PAD + SEQ], ps[:, c, 0:SEQ],
                                                   prm_T[:, ch:ch + 1], sig[:, c, :],
                                                   ALU.add, ALU.mult).then_inc(glu_ready, 1)
                low(U_PW1 + 4 * j + 6)
            dve.wait_ge(glu_ready, KD)
            for tap in range(TAPS):
                for c in range(KD):
                    src = glu[:, c, tap:tap + SEQ]
                    wt = prm_T[:, tap * KD + c:tap * KD + c + 1]
                    if tap == 0:
                        nc.vector.tensor_scalar(cv[:, c, :], src, wt, prm_T[:, A_DW + c:A_DW + c + 1],
                                                ALU.mult, ALU.add).then_inc(conv_step, 1)
                    else:
                        dve.wait_ge(conv_step, (tap - 1) * KD + c + 1)
                        nc.vector.scalar_tensor_tensor(cv[:, c, :], src, wt, cv[:, c, :],
                                                       ALU.mult, ALU.add).then_inc(conv_step, 1)
            dve.wait_ge(mean_mm, 1)
            for c in range(KD):
                nc.vector.tensor_tensor(cv[:, c, :], cv[:, c, :], ps[:, 0, 0:SEQ],
                                        ALU.subtract).then_inc(dev_ready, 1)
            dve.wait_ge(var_mm, 1)
            nc.vector.tensor_scalar(var_e[:, :], ps[:, 1, 0:SEQ], EPS, None, ALU.add).then_inc(var_ready, 1)
            dve.wait_ge(std_ready, 1)
            link(nc.vector.reciprocal(rstd[:, :], std[:, :]))
            for c in range(KD):
                nc.vector.tensor_tensor(cv[:, c, :], cv[:, c, :], rstd[:, :], ALU.mult).then_inc(ln_ready, 1)
            dve.wait_ge(bc_in[5], 16)
            link(nc.vector.tensor_tensor(x[:, :, :], x[:, :, :], bc[:, 2:3, :].to_broadcast([P, T, D]), ALU.add))
            for c in range(KD):
                dve.wait_ge(c_hi_ready, 16 + c + 1)
                nc.vector.tensor_tensor(c_lo[:, c, :], sq[:, c, :], c_hi[:, c, :], ALU.subtract).then_inc(c_ready, 1)
            low(U_PW2 + 3)
            low(U_PW2 + 4)
            add_projection(U_PW2, 0)
            low(U_PW2 + 5)
            add_projection(U_PW2, 1)

            norm(3, 0, bc_in[3])
            turned_low(4, 24)
            for t in range(T):
                dve.wait_ge(r_hi_ready, t + 1)
                nc.vector.tensor_tensor(r_lo[:, t, :], rows[:, t, :], r_hi[:, t, :], ALU.subtract).then_inc(r_ready, 1)
            dve.wait_ge(consts_ready, 7)
            link(nc.vector.tensor_scalar(eight[:, :], slot_row[:, 0:E], -1.0, None, ALU.add))
            dve.wait_ge(lg_mm, 1)
            link(nc.vector.tensor_copy(lg[:, :, :], ps[:, 4, 0:T * E].rearrange("p (t e) -> p t e", t=T)))
            for t in range(T):
                link(nc.vector.max(top[:, t, :], lg[:, t, :]))
                link(nc.vector.max_index(top_i[:, t, :], top[:, t, :], lg[:, t, :]))
            nc.vector.tensor_tensor(dlt[:, :], top[:, :, 1], top[:, :, 0], ALU.subtract).then_inc(dlt_ready, 1)
            link(nc.vector.tensor_copy(top_f[:, :, :], top_i[:, :, :]))
            for j in range(2):
                nc.vector.tensor_tensor(oh[:, j], eight[:, None, :].to_broadcast([P, T, E]),
                                        top_f[:, :, j:j + 1].to_broadcast([P, T, E]), ALU.is_equal)
            dve.wait_ge(ex_ready, 1)
            link(nc.vector.tensor_scalar(p_top[:, 1, :], ex[:, :], 1.0, None, ALU.add))
            link(nc.vector.reciprocal(p_top[:, 0, :], p_top[:, 1, :]))
            link(nc.vector.tensor_tensor(p_top[:, 1, :], p_top[:, 0, :], ex[:, :], ALU.mult))
            nc.vector.tensor_tensor(chosen[:, :, :], oh[:, 0], oh[:, 1], ALU.add).then_inc(chosen_ready, 1)
            nc.vector.tensor_tensor(comb[:, :, 0:E], oh[:, 0], p_top[:, 0, :, None].to_broadcast([P, T, E]), ALU.mult)
            link(nc.vector.tensor_tensor(comb_2[:, :, :], oh[:, 1], p_top[:, 1, :, None].to_broadcast([P, T, E]),
                                         ALU.mult))
            link(nc.vector.tensor_tensor(comb[:, :, 0:E], comb[:, :, 0:E], comb_2[:, :, :], ALU.add))
            dve.wait_ge(rank_mm, 1)
            dve.wait_ge(chosen_ready, 1)
            link(nc.vector.scalar_tensor_tensor(rank[:, :, 0:E],
                                                ps[:, 5, 0:T * E].rearrange("p (t e) -> p t e", t=T), 1.0,
                                                chosen[:, :, :], ALU.add, ALU.mult))
            link(nc.vector.tensor_scalar(over[:, :], ps[:, 5, T * E:(T + 1) * E], float(CAP), None, ALU.is_gt))
            link(nc.vector.tensor_tensor_scan(nth[:, :], ones[:, 0:E], over[:, :], 0.0, ALU.mult, ALU.add))
            for j in range(EXTRA):
                nc.vector.scalar_tensor_tensor(sel[:, j, :], nth[:, :], float(j + 1), over[:, :],
                                               ALU.is_equal, ALU.mult)
            link(nc.vector.tensor_reduce(plan_f[:, EXTRA:EXTRA + 1], over[:, :], AX.X, ALU.add))
            link(nc.vector.tensor_tensor(prod[:, 0], sel[:, :, :], eight[:, None, :].to_broadcast([P, EXTRA, E]),
                                         ALU.mult))
            link(nc.vector.tensor_reduce(plan_f[:, 0:EXTRA], prod[:, 0], AX.X, ALU.add))
            nc.vector.tensor_copy(plan[:, :], plan_f[:, :]).then_inc(plan_ready, 1)
            for table in (rank, comb):
                for t in range(T):
                    link(nc.vector.tensor_tensor(prod[:, t], sel[:, :, :],
                                                 table[:, t, None, 0:E].to_broadcast([P, EXTRA, E]), ALU.mult))
                link(nc.vector.tensor_reduce(part[:, :, :], prod[:, :, :, :], AX.X, ALU.add))
                link(nc.vector.tensor_scalar(table[:, :, E:PASSES], part[:, :, :],
                                             -float(CAP) if table is rank else 0.0, None, ALU.add))
            link(nc.vector.tensor_copy(comb_r[:, :, :, 0].rearrange("p e t -> p t e"), comb[:, :, :]))
            nc.vector.tensor_tensor(comb_r[:, :, :, 1].rearrange("p e t -> p t e"), comb[:, :, :],
                                    comb_r[:, :, :, 0].rearrange("p e t -> p t e"), ALU.subtract).then_inc(rank_ready, 1)
            nc.vector.memset(y_hi[:, :].bitcast(f32), 0.0)
            nc.vector.memset(y_lo[:, :].bitcast(f32), 0.0).then_inc(y_ready, 1)

            def make_pick(p):
                for t in range(T):
                    ins = nc.vector.tensor_scalar(pick[:, t, :], slot_row[:, :], rank[:, t, bass.ds(p, 1)], None,
                                                  ALU.is_equal)
                ins.then_inc(pick_ready, 1)

            def make_put(p):
                nc.vector.tensor_scalar(put[:, :], rank_T[:, bass.ds(p, 1), :].rearrange("p a s -> p (a s)"),
                                        slot_col[:, 0:1], None, ALU.is_equal).then_inc(put_ready, 1)

            def gathered(p, quarter):
                dve.wait_ge(gather_mm, 4 * p + quarter + 1)
                dst = c_hi if quarter == 1 else c_lo
                nc.vector.tensor_copy(dst[:, 4:8, 0:P],
                                      ps[:, 1, :].rearrange("p (b m) -> p b m", b=4)).then_inc(gather_v, 1)

            nc.vector.memset(put[:, :].bitcast(f32), 0.0).then_inc(put_ready, 1)
            dve.wait_ge(rank_ready, 1)
            make_pick(0)
            dve.wait_ge(rankT_mm, 1)
            nc.vector.tensor_copy(rank_T[:, 8:PASSES, :], ps[:, 6:8, :].rearrange("p b (e s) -> p (b e) s", e=2))\
              .then_inc(rankT_b, 1)
            dve.wait_ge(rankT_a, 1)
            dve.wait_ge(rankT_b, 1)
            gathered(0, 1)
            gathered(0, 3)

            def expert_pass(p):
                r, q = ROUNDS * p, CH + CH * p
                swiglu_first(U_EXP, q, EXPERT, r)
                dve.wait_ge(slot_w_mm, p + 1)
                nc.vector.tensor_reduce(slot_w[:, 0:1], ps[:, 2, 0:2], AX.X, ALU.add).then_inc(slot_w_ready, 1)
                make_pick(p + 1)
                dve.wait_ge(scatter_mm, p + 1)
                make_put(p)
                swiglu_loop(U_EXP, q, EXPERT, r)
                hid_low(q + CH - 1, 1, EXPERT["up"])
                low(U_EXP + U_PASS, r)
                gathered(p + 1, 1)
                low(U_EXP + U_PASS + 1, r)
                gathered(p + 1, 3)
                dve.wait_ge(y_hi_ready, p + 1)
                nc.vector.scalar_tensor_tensor(y_lo[:, :], ps[:, 2:4, :].rearrange("p b n -> p (b n)"),
                                               slot_w[:, 0:1], y_hi[:, :], ALU.mult, ALU.subtract)\
                  .then_inc(y_ready, 1)

            with dve.Fori(0, E) as p:
                expert_pass(p)
            extra = dve.value_load(plan[0:1, EXTRA:EXTRA + 1], min_val=0, max_val=EXTRA - 1)
            with dve.If(extra > 0):
                with dve.Fori(0, extra) as j:
                    expert_pass(j + E)
            dve.wait_ge(moe_mm, 1)
            for t in range(T):
                nc.vector.tensor_tensor(x[:, t, :], x[:, t, :],
                                        ps[:, SUM + 2 * t:SUM + 2 * t + 2, :].rearrange("p b n -> p (b n)"),
                                        ALU.add).then_inc(x_ready, 1)
            norm(4, 1, bc_in[4])

        @block.tensor
        def _(pe):
            mm = nc.tensor.matmul

            def moving(dst, hi, lo, s, at, start, stop):
                wh, wl = w_hi[:, s % SPLIT, at:at + NC], w_lo[:, s % SPLIT, at:at + NC]
                mm(dst, hi, wh, start=start, stop=False, skip_group_check=True)
                mm(dst, hi, wl, start=False, stop=False, skip_group_check=True)
                return mm(dst, lo, wh, start=False, stop=stop, skip_group_check=True)

            def turn_rows(k, first):
                for g in range(4):
                    t, half = g // 2, g % 2
                    if half == 0:
                        pe.wait_ge(rows_ready, first + t + 1)
                    for b in range(4):
                        at = (4 * half + b) * P
                        last = nc.tensor.transpose(ps[:, g, b * P:(b + 1) * P], rows[:, t, at:at + P], ident[:, :])
                    last.then_inc(turn_mm, 1)

            def column_unit(s, half, bank, tiles, r=0):
                pe.wait_ge(split_ready, s + 1 + RAW * r)
                for k in range(4):
                    for t in range(tiles):
                        kk = 4 * half + k
                        last = moving(ps[:, bank + t, :], c_hi[:, kk, t * P:(t + 1) * P],
                                      c_lo[:, kk, t * P:(t + 1) * P], s, k * NC, kk == 0, kk == KD - 1)
                return last.then_inc(unit_used, 1)

            def feature_unit(s, half, bank):
                pe.wait_ge(split_ready, s + 1)
                for k in range(4):
                    kk = 4 * half + k
                    for b in range(4):
                        at = k * NC + b * P
                        wh, wl = w_hi[:, s % SPLIT, at:at + P], w_lo[:, s % SPLIT, at:at + P]
                        dst = ps[:, bank + b, 0:SEQ]
                        mm(dst, wh, c_hi[:, kk, :], start=kk == 0, stop=False)
                        mm(dst, wh, c_lo[:, kk, :], start=False, stop=False)
                        last = mm(dst, wl, c_hi[:, kk, :], start=False, stop=kk == KD - 1)
                return last.then_inc(unit_used, 1)

            def small_products(bank, wh, wl, n):
                for t in range(T):
                    dst = ps[:, bank, t * n:(t + 1) * n]
                    for k in range(KD):
                        a, b = c_hi[:, k, t * P:(t + 1) * P], c_lo[:, k, t * P:(t + 1) * P]
                        mm(dst, a, wh[:, k, :], start=k == 0, stop=False)
                        mm(dst, a, wl[:, k, :], start=False, stop=False)
                        mm(dst, b, wh[:, k, :], start=False, stop=False)
                        last = mm(dst, b, wl[:, k, :], start=False, stop=k == KD - 1)
                return last

            def clear(bank, n):
                for b in range(n):
                    last = mm(ps[:, bank + b, :], zero_r[:, 0:P], zero_r[:, :], start=True, stop=False,
                              skip_group_check=True)
                return last

            def gate_products(s, q, L, r=0):
                column_unit(s, 0, L["gate"], L["tiles"], r)
                column_unit(s + 1, 1, L["gate"], L["tiles"], r)

            def up_products(s, q, L, r=0):
                column_unit(s, 0, L["up"], L["tiles"], r)
                column_unit(s + 1, 1, L["up"], L["tiles"], r)

            def down(s, half, L, r=0, stop=False):
                pe.wait_ge(split_ready, s + 1 + RAW * r)
                for k in range(2):
                    for t in range(L["tiles"]):
                        hi, lo = h_hi[:, t, 2 * half + k, :], h_lo[:, t, 2 * half + k, :]
                        for n in range(2):
                            last = moving(ps[:, L["y"] + 2 * t + n, :], hi, lo, s, k * D + n * NC, False,
                                          stop and k == 1)
                return last.then_inc(unit_used, 1)

            def turn_hidden(q, L):
                pe.wait_ge(hid_ready, q + 1)
                for t in range(L["tiles"]):
                    for b in range(4):
                        last = nc.tensor.transpose(ps[:, L["up"] + t, b * P:(b + 1) * P],
                                                   hid[:, t, b * P:(b + 1) * P], ident[:, :])
                last.then_inc(hidT_mm, 1)

            def swiglu_loop(s, q, L, r=0):
                with pe.Fori(0, CH - 1) as i:
                    gate_products(s + 4, q + 1 + i, L, r + i)
                    pe.wait_ge(h_ready, q + 1 + i)
                    up_products(s + 6, q + 1 + i, L, r + i)
                    down(s + 8, 0, L, r + i)
                    down(s + 9, 1, L, r + i)
                    turn_hidden(q + 1 + i, L)

            pe.wait_ge(consts_ready, 7)
            pe.wait_ge(gp_step, 12)
            turn_rows(0, 0)
            pe.wait_ge(c_ready, 4)
            for g in range(4):
                if g >= 2:
                    pe.wait_ge(q_out, g - 1)
                for half in range(2):
                    feature_unit(U_QKV + 2 * g + half, half, 4 * (g % 2))
            for h in range(2):
                if h == 0:
                    pe.wait_ge(k_out, 1)
                for half in range(2):
                    column_unit(U_QKV + 8 + 2 * h + half, half, 2 * h, T)
            pe.wait_ge(k_out, 2)
            pe.wait_ge(small_split, 2)
            small_products(4, wf_hi, wf_lo, H).then_inc(fg_mm, 1)
            pe.wait_ge(log_f_ready, 1)
            for t in range(T):
                dst = ps[:, 5, t * H:(t + 1) * H]
                for u in range(t):
                    mm(dst, ones[:, :], log_f[:, u, :], start=u == 0, stop=False)
                last = mm(dst, upto[:, :], log_f[:, t, :], start=t == 0, stop=True)
            last.then_inc(c_mm, 1)
            pe.wait_ge(c_out, 1)
            for t in range(T):
                last = nc.tensor.transpose(ps[:, 6, t * P:(t + 1) * P], c_pad[:, t, :], ident[:, :])
            last.then_inc(cT_mm, 1)
            pe.wait_ge(cT_out, 1)
            pe.wait_ge(v_out, 2)

            def scores(h):
                q = (q_even, q_odd)[h % 2]
                if h >= 2:
                    pe.wait_ge(sm_ready, h - 1)
                pick_c = ident[:, h:h + 1].to_broadcast([P, P])
                for t in range(T):
                    at = P if t else 0
                    n = (t + 1) * P
                    dst = ps[:, h % 2, at:at + n]
                    mm(dst, q[:, h // 2, t * P:(t + 1) * P], k_T[:, h // 2, 0:n], start=True, stop=False)
                    last = mm(dst, pick_c, neg_cT[:, 0:n], start=False, stop=True)
                last.then_inc(s_mm, 1)

            def turn_probs(h):
                pe.wait_ge(exp_ready, h + 1)
                if h >= 2:
                    pe.wait_ge(prT_ready, h - 1)
                for b in range(3):
                    last = nc.tensor.transpose(ps[:, 2 + h % 2, b * P:(b + 1) * P],
                                               pr[:, h % 2, b * P:(b + 1) * P], ident[:, :])
                last.then_inc(prT_mm, 1)

            def values(h):
                pe.wait_ge(prT_ready, h + 1)
                at = (h * HD) % NC
                for t in range(T):
                    dst = ps[:, 4 + 2 * t + h * HD // NC, at:at + HD]
                    for u in range(t + 1):
                        b = (u + 1) if t else 0
                        last = mm(dst, pr_T[:, h % 2, b * P:(b + 1) * P], v_sb[:, u, h * HD:(h + 1) * HD],
                                  start=u == 0, stop=u == t)
                last.then_inc(pv_mm, 1)

            for step in range(H + 2):
                if step < H:
                    scores(step)
                if 1 <= step <= H:
                    turn_probs(step - 1)
                if step >= 2:
                    values(step - 2)

            def projection(s):
                for h in range(2):
                    for half in range(2):
                        column_unit(s + 2 * h + half, half, 4 + 2 * h, T)

            turn_rows(1, T)
            pe.wait_ge(c_ready, 8)
            projection(U_WO)

            turn_rows(2, 2 * T)
            pe.wait_ge(c_ready, 12)
            gate_products(U_DENSE, 0, DENSE)
            up_products(U_DENSE + 2, 0, DENSE)
            clear(DENSE["y"], 2 * T)
            turn_hidden(0, DENSE)
            swiglu_loop(U_DENSE, 0, DENSE)
            pe.wait_ge(h_ready, CH)
            down(U_DENSE + U_PASS - 2, 0, DENSE)
            down(U_DENSE + U_PASS - 1, 1, DENSE, stop=True)

            pe.wait_ge(x_ready, 4)
            pe.wait_ge(prm_in, 6 * 16)
            for b in range(3):
                last = nc.tensor.transpose(ps[:, 7, b * P:(b + 1) * P], prm[:, b, :], ident[:, :])
            last.then_inc(prm_mm, 1)
            turn_rows(3, 3 * T)
            pe.wait_ge(c_ready, 16)
            for g in range(4):
                if g == 1:
                    pe.wait_ge(prm_ready, 1)
                if g == 2:
                    pe.wait_ge(glu_ready, 4)
                if g == 3:
                    pe.wait_ge(sig_ready, 4)
                for half in range(2):
                    feature_unit(U_PW1 + 2 * g + half, half, 4 * (g % 2))
            for c in range(KD):
                pe.wait_ge(conv_step, (TAPS - 1) * KD + c + 1)
                last = mm(ps[:, 0, 0:SEQ], mean_w[:, :], cv[:, c, :], start=c == 0, stop=c == KD - 1)
            last.then_inc(mean_mm, 1)
            for c in range(KD):
                pe.wait_ge(sq_ready, c + 1)
                last = mm(ps[:, 1, 0:SEQ], mean_w[:, :], sq[:, c, :], start=c == 0, stop=c == KD - 1)
            last.then_inc(var_mm, 1)
            pe.wait_ge(c_ready, 16 + KD)
            projection(U_PW2)

            turn_rows(4, 4 * T)
            pe.wait_ge(c_ready, 16 + KD + 4)
            small_products(4, wr_hi, wr_lo, E).then_inc(lg_mm, 1)
            pe.wait_ge(chosen_ready, 1)
            for t in range(T):
                dst = ps[:, 5, t * E:(t + 1) * E]
                for u in range(t):
                    mm(dst, ones[:, :], chosen[:, u, :], start=u == 0, stop=False)
                mm(dst, before[:, :], chosen[:, t, :], start=t == 0, stop=True)
            for t in range(T):
                last = mm(ps[:, 5, T * E:(T + 1) * E], ones[:, :], chosen[:, t, :], start=t == 0, stop=t == T - 1)
            last.then_inc(rank_mm, 1)
            pe.wait_ge(rank_ready, 1)
            for j in range(PASSES):
                bank = j // 2 if j < E else 6 + (j - E) // 2
                for t in range(T):
                    at = (j % 2) * SEQ + t * P
                    last = mm(ps[:, bank, at:at + P], rank[:, t, j:j + 1].to_broadcast([P, P]), ident[:, :],
                              start=True, stop=True)
            last.then_inc(rankT_mm, 1)

            def gather(p, quarter):
                src = r_hi if quarter < 2 else r_lo
                bank = quarter % 2
                for b in range(4):
                    at = (4 * (quarter % 2) + b) * P
                    for t in range(T):
                        last = mm(ps[:, bank, b * P:(b + 1) * P], src[:, t, at:at + P], pick[:, t, :],
                                  start=t == 0, stop=t == T - 1)
                last.then_inc(gather_mm, 1)

            pe.wait_ge(rankT_a, 1)
            pe.wait_ge(rankT_b, 1)
            clear(SUM, 2 * T)
            pe.wait_ge(r_ready, T)
            pe.wait_ge(pick_ready, 1)
            gather(0, 0)
            gather(0, 1)
            pe.wait_ge(gather_a, 1)
            gather(0, 2)
            pe.wait_ge(gather_v, 1)
            gather(0, 3)

            def scatter(n):
                pe.wait_ge(y_ready, n + 1)
                pe.wait_ge(put_ready, n + 1)
                for t in range(T):
                    for h in range(2):
                        dst = ps[:, SUM + 2 * t + h, :]
                        mm(dst, put[:, t * P:(t + 1) * P], y_hi[:, h * NC:(h + 1) * NC], start=False, stop=False,
                           skip_group_check=True)
                        last = mm(dst, put[:, t * P:(t + 1) * P], y_lo[:, h * NC:(h + 1) * NC], start=False,
                                  stop=False, skip_group_check=True)
                return last.then_inc(scatter_mm, 1)

            def expert_pass(p):
                r, q = ROUNDS * p, CH + CH * p
                pe.wait_ge(gather_a, 2 * p + 2)
                pe.wait_ge(gather_v, 2 * p + 2)
                gate_products(U_EXP, q, EXPERT, r)
                up_products(U_EXP + 2, q, EXPERT, r)
                pe.wait_ge(y_ready, p + 1)
                for t in range(T):
                    last = mm(ps[:, EXPERT["y"], 0:2], pick[:, t, :],
                              comb_r[:, bass.ds(p, 1), t, :].rearrange("p a b -> p (a b)"),
                              start=t == 0, stop=t == T - 1)
                last.then_inc(slot_w_mm, 1)
                scatter(p)
                turn_hidden(q, EXPERT)
                pe.wait_ge(slot_w_ready, p + 1)
                clear(EXPERT["y"], 2)
                swiglu_loop(U_EXP, q, EXPERT, r)
                pe.wait_ge(pick_ready, p + 2)
                gather(p + 1, 0)
                pe.wait_ge(h_ready, q + CH)
                down(U_EXP + U_PASS - 2, 0, EXPERT, r)
                gather(p + 1, 1)
                pe.wait_ge(gather_a, 2 * p + 3)
                gather(p + 1, 2)
                down(U_EXP + U_PASS - 1, 1, EXPERT, r, stop=True)
                pe.wait_ge(gather_v, 2 * p + 3)
                gather(p + 1, 3)

            with pe.Fori(0, E) as p:
                expert_pass(p)
            pe.wait_ge(plan_ready, 1)
            extra = pe.value_load(plan[0:1, EXTRA:EXTRA + 1], min_val=0, max_val=EXTRA - 1)
            with pe.If(extra > 0):
                with pe.Fori(0, extra) as j:
                    expert_pass(j + E)
            scatter(extra + E)
            for b in range(2 * T):
                last = mm(ps[:, SUM + b, :], zero_r[:, 0:P], zero_r[:, :], start=False, stop=True,
                          skip_group_check=True)
            last.then_inc(moe_mm, 1)


_INS = ['x', 'attn_norm', 'w_qkv', 'w_fgate', 'b_fgate', 'w_attn_out', 'conv_norm', 'w_pw1', 'b_pw1', 'w_dw', 'b_dw',
        'conv_ln_g', 'conv_ln_b', 'w_pw2', 'b_pw2', 'dense_norm', 'w_dense_gate', 'w_dense_up', 'w_dense_down',
        'moe_norm', 'w_router', 'w_exp_gate', 'w_exp_up', 'w_exp_down', 'final_norm']


def kernel(**inputs):
    import numpy as _np
    import concourse.bacc as _bacc
    from concourse import mybir as _mybir
    from concourse.bass_utils import run_bass_kernel_spmd as _run

    nc = _bacc.Bacc("TRN2", target_bir_lowering=False, num_devices=1)
    arrays, args = {}, []
    for name in _INS:
        a = _np.ascontiguousarray(inputs[name])
        arrays[f"in_{name}_dram"] = a
        args.append(nc.dram_tensor(f"in_{name}_dram", a.shape, _mybir.dt.from_np(a.dtype), kind="ExternalInput").ap())
    args.append(nc.dram_tensor("out_0_dram", inputs['x'].shape, _mybir.dt.float32, kind="ExternalOutput").ap())
    build_trunk(nc, *args)
    r = _run(nc, [arrays], core_ids=[0])
    return r.results[0]["out_0_dram"]
```

```python
from contextlib import ExitStack

import concourse.bass as bass
from concourse import mybir


def build_trunk(nc, x_in, attn_norm, w_qkv, w_fgate, b_fgate, w_attn_out, conv_norm, w_pw1, b_pw1, w_dw, b_dw,
                conv_ln_g, conv_ln_b, w_pw2, b_pw2, dense_norm, w_dense_gate, w_dense_up, w_dense_down,
                moe_norm, w_router, w_exp_gate, w_exp_up, w_exp_down, final_norm, out):
    f32, f32r, i32, u32 = mybir.dt.float32, mybir.dt.float32r, mybir.dt.int32, mybir.dt.uint32
    ALU, ACT, AX = mybir.AluOpType, mybir.ActivationFunctionType, mybir.AxisListType

    P = 128
    _, SEQ, D = x_in.shape
    T = SEQ // P
    KD = D // P
    H = w_fgate.shape[2]
    HD = D // H
    F = w_dense_gate.shape[2]
    E = w_exp_gate.shape[1]
    TAPS = w_dw.shape[1]
    EPS = 1e-6
    NC = 512
    UNIT = 4 * NC
    CH = F // NC
    RAW, SPLIT = 6, 3
    MASKED = -1e30
    CAP = P
    EXTRA = 4
    PASSES = E + EXTRA

    U_QKV = 0
    U_WO = U_QKV + 2 * (3 * D // NC)
    U_DENSE = U_WO + 2 * (D // NC)
    U_PW1 = U_DENSE + 6 * CH
    U_PW2 = U_PW1 + 2 * (2 * D // NC)
    U_EXP = U_PW2 + 2 * (D // NC)
    U_PASS = 6 * CH
    ROUNDS = U_PASS // RAW
    assert U_PASS % RAW == 0 and RAW % SPLIT == 0

    ctx = ExitStack()
    with ctx:
        def sb(name, shape, dt=f32, where=ctx):
            return where.enter_context(nc.sbuf_tensor(name, shape, dt))

        def sem(name):
            return ctx.enter_context(nc.semaphore(name))

        raw = sb("raw", [P, RAW, UNIT])
        w_hi = sb("w_hi", [P, SPLIT, UNIT], f32r)
        w_lo = sb("w_lo", [P, SPLIT, UNIT], f32r)
        x = sb("x", [P, T, D])
        rows = sb("rows", [P, T, D])
        c_hi = sb("c_hi", [P, KD, SEQ], f32r)
        c_lo = sb("c_lo", [P, KD, SEQ], f32r)
        gate = sb("gate", [P, T, NC])
        hid = sb("hid", [P, T, NC])
        h_hi = sb("h_hi", [P, T, 4, P], f32r)
        h_lo = sb("h_lo", [P, T, 4, P], f32r)
        bc = sb("bc", [P, 3, D])
        ident = sb("ident", [P, P])
        ones = sb("ones", [P, P])
        mean_w = sb("mean_w", [P, P])
        upto = sb("upto", [P, P])
        before = sb("before", [P, P])
        slot_row = sb("slot_row", [P, P])
        slot_col = sb("slot_col", [P, 1])
        iota_i = sb("iota_i", [P, P], i32)
        iota_c = sb("iota_c", [P, 1], i32)
        eight = sb("eight", [P, E])
        zero_r = sb("zero_r", [P, NC], f32r)
        ss = sb("ss", [P, T, 2])
        ones_r = sb("ones_r", [P, P], f32r)
        tick = sb("tick", [P, 2])
        narrow = sb("narrow", [P, SEQ])
        ms = sb("ms", [P, T])
        rt = sb("rt", [P, T])
        rs = sb("rs", [P, T])
        rq = sb("rq", [P, T])
        wf = sb("wf", [P, KD, H])
        wf_cat = sb("wf_cat", [P, KD * 2 * H + P], f32r)
        wr = sb("wr", [P, KD, E])
        wr_cat = sb("wr_cat", [P, KD * 2 * E + P], f32r)
        bf_bc = sb("bf_bc", [P, H])

        wf_parts = wf_cat[:, 0:KD * 2 * H].rearrange("p (k c n) -> p k c n", k=KD, c=2)
        wr_parts = wr_cat[:, 0:KD * 2 * E].rearrange("p (k c n) -> p k c n", k=KD, c=2)
        sm, pr = gate[:, :, 0:3 * P], hid[:, :, 0:3 * P]

        with ExitStack() as region:
            q_even = sb("q_even", [P, KD, SEQ], f32, region)
            q_odd = sb("q_odd", [P, KD, SEQ], f32, region)
            k_T = sb("k_T", [P, KD, SEQ], f32, region)
            v_sb = sb("v_sb", [P, T, D], f32, region)
            pr_T = sb("pr_T", [P, 2, 3 * P], f32, region)
            mask = sb("mask", [P, 3 * P], f32, region)
            c_pad = sb("c_pad", [P, T, P], f32, region)
            neg_cT = sb("neg_cT", [P, SEQ], f32, region)
            nm = sb("nm", [P, H, T], f32, region)
            psum_rows = sb("psum_rows", [P, T, H], f32, region)
            inv_rows = sb("inv_rows", [P, T, H], f32, region)
            z = sb("z", [P, T, H], f32, region)
            z_min = sb("z_min", [P, T, H], f32, region)
            z_abs = sb("z_abs", [P, T, H], f32, region)
            z_exp = sb("z_exp", [P, T, H], f32, region)
            z_log = sb("z_log", [P, T, H], f32, region)
            log_f = sb("log_f", [P, T, H], f32, region)
        PAD = TAPS - 1
        with ExitStack() as region:
            glu = sb("glu", [P, KD, PAD + SEQ], f32, region)
            sig = sb("sig", [P, 4, SEQ], f32, region)
            cv = sb("cv", [P, KD, SEQ], f32, region)
            sq = sb("sq", [P, KD, SEQ], f32, region)
            prm = sb("prm", [P, 3, P], f32, region)
            prm_T = sb("prm_T", [P, 3 * P], f32, region)
            var_e = sb("var_e", [P, SEQ], f32, region)
            std = sb("std", [P, SEQ], f32, region)
            rstd = sb("rstd", [P, SEQ], f32, region)
        DIAG = KD * SEQ // P
        diag = sq[:, :, :].rearrange("p c s -> p (c s)").rearrange("p (i m) -> p i m", m=P)
        r_hi = sb("r_hi", [P, T, D], f32r)
        r_lo = sb("r_lo", [P, T, D], f32r)
        rank_d = sb("rank_d", [P, T, P], f32r)
        y_hi = sb("y_hi", [P, D], f32r)
        y_lo = sb("y_lo", [P, D], f32r)
        pick = sb("pick", [P, T, P], f32r)
        put = sb("put", [P, SEQ], f32r)
        slot_w = sb("slot_w", [P, 1])
        lg = sb("lg", [P, T, E])
        top = sb("top", [P, T, E])
        below = sb("below", [P, E, E])
        better = sb("better", [P, T, E, E])
        equal = sb("equal", [P, T, E, E])
        place = sb("place", [P, T, E])
        dlt = sb("dlt", [P, T])
        ex = sb("ex", [P, T])
        p_top = sb("p_top", [P, 2, T])
        oh = sb("oh", [P, 2, T, E])
        chosen = sb("chosen", [P, T, E])
        comb = sb("comb", [P, T, PASSES])
        comb_2 = sb("comb_2", [P, T, E])
        rank = sb("rank", [P, T, PASSES])
        over = sb("over", [P, E])
        nth = sb("nth", [P, E])
        sel = sb("sel", [P, EXTRA, E])
        prod = sb("prod", [P, T, EXTRA, E])
        part = sb("part", [P, T, EXTRA])
        plan_f = sb("plan_f", [P, EXTRA + 1])
        plan = sb("plan", [P, EXTRA + 1], i32)
        comb_r = sb("comb_r", [P, PASSES, T, 2], f32r)

        ps = ctx.enter_context(nc.psum_tensor("ps", [P, 8, NC], f32))

        raw_in = [sem(f"raw_in{i}") for i in range(RAW)]
        hi_ready = sem("hi_ready")
        split_ready = sem("split_ready")
        unit_used = sem("unit_used")
        consts_ready = sem("consts_ready")
        gp_step = sem("gp_step")
        x_in_sem = [sem(f"x_in_sem{t}") for t in range(T)]
        tick_ready = sem("tick_ready")
        bank_done = sem("bank_done")
        narrow_mm = sem("narrow_mm")
        narrow_out = sem("narrow_out")
        small_in = [sem(f"small_in{i}") for i in range(3)]
        bc_in = [sem(f"bc_in{i}") for i in range(6)]
        dve_step = sem("dve_step")
        x_ready = sem("x_ready")
        ss_ready = sem("ss_ready")
        ms_ready = sem("ms_ready")
        rt_ready = sem("rt_ready")
        rows_ready = sem("rows_ready")
        turn_mm = sem("turn_mm")
        c_hi_ready = sem("c_hi_ready")
        c_ready = sem("c_ready")
        small_hi = sem("small_hi")
        small_split = sem("small_split")
        q_out = sem("q_out")
        k_out = sem("k_out")
        v_out = sem("v_out")
        fg_mm = sem("fg_mm")
        z_ready = sem("z_ready")
        z_exp_ready = sem("z_exp_ready")
        z_log_ready = sem("z_log_ready")
        log_f_ready = sem("log_f_ready")
        c_mm = sem("c_mm")
        c_out = sem("c_out")
        cT_mm = sem("cT_mm")
        cT_out = sem("cT_out")
        s_mm = sem("s_mm")
        sm_ready = sem("sm_ready")
        max_ready = sem("max_ready")
        exp_ready = sem("exp_ready")
        prT_mm = sem("prT_mm")
        prT_ready = sem("prT_ready")
        pv_mm = sem("pv_mm")
        silu_ready = sem("silu_ready")
        hid_ready = sem("hid_ready")
        hidT_mm = sem("hidT_mm")
        h_hi_ready = sem("h_hi_ready")
        h_ready = sem("h_ready")
        prm_in = sem("prm_in")
        prm_clear = sem("prm_clear")
        prm_mm = sem("prm_mm")
        prm_ready = sem("prm_ready")
        glu_clear = sem("glu_clear")
        sig_ready = sem("sig_ready")
        glu_ready = sem("glu_ready")
        conv_step = sem("conv_step")
        diag_ready = sem("diag_ready")
        diag_used = sem("diag_used")
        base_ready = sem("base_ready")
        conv_out = sem("conv_out")
        mean_mm = sem("mean_mm")
        dev_ready = sem("dev_ready")
        sq_ready = sem("sq_ready")
        var_mm = sem("var_mm")
        var_ready = sem("var_ready")
        std_ready = sem("std_ready")
        ln_ready = sem("ln_ready")
        act_ready = sem("act_ready")
        r_hi_ready = sem("r_hi_ready")
        r_ready = sem("r_ready")
        lg_mm = sem("lg_mm")
        dlt_ready = sem("dlt_ready")
        ex_ready = sem("ex_ready")
        chosen_ready = sem("chosen_ready")
        rank_mm = sem("rank_mm")
        comb_hi_ready = sem("comb_hi_ready")
        comb_ready = sem("comb_ready")
        rank_d_ready = sem("rank_d_ready")
        rank_row_mm = sem("rank_row_mm")
        zeros_ready = sem("zeros_ready")
        plan_ready = sem("plan_ready")
        pick_ready = sem("pick_ready")
        put_ready = sem("put_ready")
        gather_mm = sem("gather_mm")
        gather_a = sem("gather_a")
        gather_v = sem("gather_v")
        slot_w_mm = sem("slot_w_mm")
        slot_w_ready = sem("slot_w_ready")
        y_hi_ready = sem("y_hi_ready")
        y_ready = sem("y_ready")
        scatter_mm = sem("scatter_mm")
        moe_mm = sem("moe_mm")
        stored = sem("stored")

        PE_TAPS = 12
        DVE_TAPS = TAPS - PE_TAPS
        BY_HALF = ((0, 0), (1, 0), (0, 1), (1, 1))
        BY_TILE = ((0, 0), (0, 1), (1, 0), (1, 1))

        DENSE = dict(tiles=T, gate=0, up=2, y=4)
        EXPERT = dict(tiles=1, gate=0, up=1, y=2)
        SUM = 4
        WD = w_dw.shape[1] * KD
        A_PW1, A_DW, A_G, A_B = 2 * P, 2 * P + 2 * KD, 2 * P + 3 * KD, 2 * P + 4 * KD

        block = ctx.enter_context(nc.Block())

        @block.sync
        def _(sp):
            def load(s, src, r=0):
                if s >= RAW or not isinstance(r, int):
                    sp.wait_ge(split_ready, s - RAW + 1 + RAW * r)
                k = src.shape[0] // P
                sp.dma_start(raw[:, s % RAW, :].rearrange("p (k n) -> p k n", k=k),
                             src.rearrange("(k p) n -> p k n", p=P)).then_inc(raw_in[s % RAW], 16)

            def load_columns(s, w, c, r=0):
                for half in range(2):
                    load(s + half, w[half * D // 2:(half + 1) * D // 2, bass.ds(c * NC, NC)], r)

            def load_swiglu(s, wg, wu, wd, r=0):
                def down(s, c, r):
                    for half in range(2):
                        load(s + half, wd[bass.ds(c * NC + half * (NC // 2), NC // 2), :], r)
                load_columns(s, wg, 0, r)
                load_columns(s + 2, wu, 0, r)
                with sp.Fori(0, CH - 1) as i:
                    load_columns(s + 4, wg, i + 1, r + i)
                    load_columns(s + 6, wu, i + 1, r + i)
                    down(s + 8, i, r + i)
                down(s + 6 * CH - 2, CH - 1, r)

            for t in range(T):
                sp.dma_start(x[:, t, :], x_in[0, t * P:(t + 1) * P, :]).then_inc(x_in_sem[t], 16)
            for c in range(3 * D // NC):
                load_columns(U_QKV + 2 * c, w_qkv[0], c)
            for c in range(D // NC):
                load_columns(U_WO + 2 * c, w_attn_out[0], c)
            load_swiglu(U_DENSE, w_dense_gate[0], w_dense_up[0], w_dense_down[0])
            for g, c in enumerate((0, 2, 1, 3)):
                load_columns(U_PW1 + 2 * g, w_pw1[0], c)
            for c in range(D // NC):
                load_columns(U_PW2 + 2 * c, w_pw2[0], c)

            def load_expert(e, p):
                load_swiglu(U_EXP, w_exp_gate[0, e], w_exp_up[0, e], w_exp_down[0, e], ROUNDS * p)

            with sp.Fori(0, E) as p:
                load_expert(p, p)
            sp.wait_ge(plan_ready, 1)
            extra = sp.value_load(plan[0:1, EXTRA:EXTRA + 1], min_val=0, max_val=EXTRA - 1)
            with sp.If(extra > 0):
                with sp.Fori(0, extra) as j:
                    e = sp.value_load(plan[0:1, bass.ds(j, 1)], min_val=0, max_val=E - 1)
                    load_expert(e, j + E)
            load_columns(U_EXP, w_exp_gate[0, 0], 0, ROUNDS * (extra + E))

            for i, (t, h) in enumerate(BY_HALF):
                sp.wait_ge(rows_ready, 20 + i + 1)
                sp.dma_start(out[0, t * P:(t + 1) * P, h * NC:(h + 1) * NC],
                             rows[:, t, h * NC:(h + 1) * NC]).then_inc(stored, 16)
            sp.wait_ge(stored, 16 * 4)

        @block.gpsimd
        def _(gp):
            def triangle(tile, fill, op, row=-1, column=1):
                return nc.gpsimd.affine_select(out=tile, in_=tile, compare_op=op, fill=fill, base=0,
                                               pattern=[[column, P]], channel_multiplier=row)
            for i, row in enumerate((attn_norm[0], dense_norm[0], conv_norm[0])):
                gp.dma_start(bc[:, i, :], row.partition_broadcast(P)).then_inc(bc_in[i], 16)
            gp.dma_start(wf[:, :, :], w_fgate[0].rearrange("(k p) n -> p k n", p=P)).then_inc(small_in[0], 16)
            gp.dma_start(bf_bc[:, :], b_fgate[0].partition_broadcast(P)).then_inc(small_in[1], 16)
            gp.dma_start(wr[:, :, :], w_router[0].rearrange("(k p) n -> p k n", p=P)).then_inc(small_in[2], 16)
            for i, (tile, value) in enumerate((
                    (ident[:, :], 0.0), (ones[:, :], 1.0), (mean_w[:, :], 1.0 / D), (upto[:, :], 1.0),
                    (before[:, :], 1.0), (mask[:, :], 0.0), (c_pad[:, :, :], 0.0), (zero_r[:, :].bitcast(f32), 0.0),
                    (ones_r[:, :].bitcast(f32), 1.0), (wf_cat[:, KD * 2 * H:].bitcast(f32), 0.0),
                    (wr_cat[:, KD * 2 * E:].bitcast(f32), 0.0),
                    (q_even[P // 2:P, :, :], 0.0), (q_odd[0:P // 2, :, :], 0.0))):
                if i:
                    gp.wait_ge(gp_step, i)
                nc.gpsimd.memset(tile, value).then_inc(gp_step, 1)
            gp.wait_ge(gp_step, 13)
            nc.gpsimd.iota(iota_i[:, :], [[1, P]], base=1, channel_multiplier=0).then_inc(gp_step, 1)
            gp.wait_ge(gp_step, 14)
            nc.gpsimd.iota(iota_c[:, :], [[0, 1]], base=1, channel_multiplier=1).then_inc(gp_step, 1)
            gp.wait_ge(gp_step, 15)
            triangle(ident[:, :], 1.0, ALU.not_equal).then_inc(consts_ready, 1)
            gp.wait_ge(consts_ready, 1)
            triangle(upto[:, :], 0.0, ALU.is_ge).then_inc(consts_ready, 1)
            gp.wait_ge(consts_ready, 2)
            triangle(before[:, :], 0.0, ALU.is_gt).then_inc(consts_ready, 1)
            for i, at in enumerate((0, 2 * P)):
                gp.wait_ge(consts_ready, 3 + i)
                triangle(mask[:, at:at + P], MASKED, ALU.is_ge, row=1, column=-1).then_inc(consts_ready, 1)
            gp.wait_ge(consts_ready, 5)
            nc.gpsimd.tensor_copy(slot_row[:, :], iota_i[:, :]).then_inc(consts_ready, 1)
            gp.wait_ge(consts_ready, 6)
            nc.gpsimd.tensor_copy(slot_col[:, :], iota_c[:, :]).then_inc(consts_ready, 1)
            gp.wait_ge(consts_ready, 7)

            gp.wait_ge(rows_ready, 8)
            nc.gpsimd.memset(prm[:, :, :], 0.0).then_inc(prm_clear, 1)
            gp.wait_ge(prm_clear, 1)
            nc.gpsimd.memset(glu[:, :, 0:PAD], 0.0).then_inc(glu_clear, 1)
            taps = w_dw[0].rearrange("a (b c) -> (a b) c", c=P)
            gp.dma_start(prm[:, 0, :], taps[0:P, :]).then_inc(prm_in, 16)
            gp.dma_start(prm[0:WD - P, 1, :], taps[P:WD, :]).then_inc(prm_in, 16)
            at = 0
            for v, n in ((b_pw1, 2 * KD), (b_dw, KD), (conv_ln_g, KD), (conv_ln_b, KD)):
                gp.dma_start(prm[at:at + n, 2, :], v[0].rearrange("(b c) -> b c", c=P)).then_inc(prm_in, 16)
                at += n
            gp.dma_start(bc[:, 0, :], moe_norm[0].partition_broadcast(P)).then_inc(bc_in[3], 16)
            gp.wait_ge(rows_ready, 12)
            gp.dma_start(bc[:, 1, :], final_norm.partition_broadcast(P)).then_inc(bc_in[4], 16)
            gp.wait_ge(rows_ready, 16)
            gp.dma_start(bc[:, 2, :], b_pw2[0].partition_broadcast(P)).then_inc(bc_in[5], 16)

            gp.wait_ge(c_ready, 20)
            gp.wait_ge(glu_clear, 1)
            nc.gpsimd.memset(y_hi[:, :].bitcast(f32), 0.0).then_inc(zeros_ready, 1)
            gp.wait_ge(zeros_ready, 1)
            nc.gpsimd.memset(y_lo[:, :].bitcast(f32), 0.0).then_inc(zeros_ready, 1)
            gp.wait_ge(zeros_ready, 2)
            nc.gpsimd.memset(put[:, :].bitcast(f32), 0.0).then_inc(y_ready, 1)

        @block.scalar
        def _(act):
            def high(s, r=0):
                act.wait_ge(raw_in[s % RAW], 16 * (s // RAW + 1) + 16 * r)
                if s >= SPLIT or not isinstance(r, int):
                    act.wait_ge(unit_used, s - SPLIT + 1 + RAW * r)
                nc.scalar.copy(w_hi[:, s % SPLIT, :], raw[:, s % RAW, :]).then_inc(hi_ready, 1)

            def norm_sums(k, order):
                nc.scalar.activation(tick[:, 1:2], tick[:, 0:1], ACT.Sqrt)
                for i, (t, h) in enumerate(order):
                    if k == 0:
                        act.wait_ge(x_in_sem[t], 16)
                    else:
                        act.wait_ge(x_ready, 4 * (k - 1) + i + 1)
                    nc.scalar.activation(rows[:, t, h * NC:(h + 1) * NC], x[:, t, h * NC:(h + 1) * NC], ACT.Square,
                                         accum_out=ss[:, t, h:h + 1]).then_inc(ss_ready, 1)
                act.wait_ge(ms_ready, k + 1)
                nc.scalar.activation(rt[:, :], ms[:, :], ACT.Sqrt).then_inc(rt_ready, 1)

            def turned_high(k, bank):
                for g, (t, half) in enumerate(BY_HALF):
                    act.wait_ge(turn_mm, 4 * k + g + 1)
                    nc.scalar.copy(c_hi[:, 4 * half:4 * half + 4, t * P:(t + 1) * P],
                                   ps[:, bank + g, :].rearrange("p (b m) -> p b m", b=4)).then_inc(c_hi_ready, 1)

            def hid_high(q, tiles, up):
                act.wait_ge(hidT_mm, q + 1)
                nc.scalar.copy(h_hi[:, 0:tiles].rearrange("p t b m -> p t (b m)"),
                               ps[:, up:up + tiles, :]).then_inc(h_hi_ready, 1)

            def silu(s, tiles, gate_bank, r):
                act.wait_ge(unit_used, s + 2 + RAW * r)
                nc.scalar.activation(gate[:, 0:tiles, :], ps[:, gate_bank:gate_bank + tiles, :],
                                     ACT.Silu).then_inc(silu_ready, 1)

            def swiglu_first(s, q, L, r=0):
                high(s + 2, r)
                high(s + 3, r)
                silu(s, L["tiles"], L["gate"], r)
                high(s + 4, r)
                high(s + 5, r)

            def swiglu_loop(s, q, L, r=0):
                with act.Fori(0, CH - 1) as i:
                    hid_high(q + i, L["tiles"], L["up"])
                    high(s + 6, r + i)
                    high(s + 7, r + i)
                    silu(s + 4, L["tiles"], L["gate"], r + i)
                    for j in range(8, 12):
                        high(s + j, r + i)

            act.wait_ge(tick_ready, 1)
            norm_sums(0, BY_TILE)
            high(0)
            turned_high(0, 4)
            high(1)
            high(2)
            act.wait_ge(small_in[0], 16)
            nc.scalar.copy(wf_parts[:, :, 0, :], wf[:, :, :]).then_inc(small_hi, 1)
            act.wait_ge(small_in[2], 16)
            nc.scalar.copy(wr_parts[:, :, 0, :], wr[:, :, :]).then_inc(small_hi, 1)

            for g in range(4):
                if g:
                    high(2 * g + 1)
                    high(2 * g + 2)
                if g < 2:
                    act.wait_ge(unit_used, U_QKV + 2 * g + 2)
                    if g == 0:
                        act.wait_ge(gp_step, 15)
                    cols = slice(4 * g, 4 * g + 4)
                    banks = slice(4 * g, 4 * g + 4)
                    nc.scalar.activation(q_even[0:HD, cols, :], ps[0:HD, banks, 0:SEQ], ACT.Copy,
                                         scale=HD ** -0.5)
                    nc.scalar.activation(q_odd[HD:P, cols, :], ps[HD:P, banks, 0:SEQ], ACT.Copy,
                                         scale=HD ** -0.5).then_inc(q_out, 1)
            for s in range(U_QKV + 9, U_QKV + 12):
                high(s)
            act.wait_ge(z_ready, 1)
            nc.scalar.activation(z_exp[:, :, :], z_abs[:, :, :], ACT.Exp, scale=-1.0).then_inc(z_exp_ready, 1)
            act.wait_ge(z_exp_ready, 1)
            nc.scalar.activation(z_log[:, :, :], z_exp[:, :, :], ACT.Ln, bias=1.0).then_inc(z_log_ready, 1)
            for h in range(2):
                act.wait_ge(unit_used, U_QKV + 10 + 2 * h)
                nc.scalar.copy(v_sb[:, :, h * NC:(h + 1) * NC], ps[:, 2 * h:2 * h + 2, :]).then_inc(v_out, 1)
                if h == 0:
                    high(U_WO)
                    high(U_WO + 1)
                else:
                    high(U_WO + 2)

            def prob_T(h):
                act.wait_ge(prT_mm, h + 1)
                if h >= 2:
                    act.wait_ge(pv_mm, h - 1)
                nc.scalar.copy(pr_T[:, h % 2, :], ps[:, 2 + h % 2, 0:3 * P]).then_inc(prT_ready, 1)

            for h in range(H):
                act.wait_ge(max_ready, h + 1)
                if h >= 2:
                    act.wait_ge(prT_mm, h - 1)
                nc.scalar.activation(pr[:, h % 2, 0:P], sm[:, h % 2, 0:P], ACT.Exp, bias=nm[:, h, 0:1],
                                     accum_out=psum_rows[:, 0, h:h + 1])
                nc.scalar.activation(pr[:, h % 2, P:3 * P], sm[:, h % 2, P:3 * P], ACT.Exp, bias=nm[:, h, 1:2],
                                     accum_out=psum_rows[:, 1, h:h + 1]).then_inc(exp_ready, 1)
                if h:
                    prob_T(h - 1)
            prob_T(H - 1)
            turned_high(1, 0)
            high(U_WO + 3)
            for s in range(U_WO + 4, U_WO + 6):
                high(s)

            norm_sums(1, BY_HALF)
            turned_high(2, 4)
            swiglu_first(U_DENSE, 0, DENSE)
            swiglu_loop(U_DENSE, 0, DENSE)
            hid_high(CH - 1, T, DENSE["up"])
            high(U_PW1)
            high(U_PW1 + 1)

            norm_sums(2, BY_TILE)
            turned_high(3, 4)
            high(U_PW1 + 2)

            def tap_diagonals(first, count):
                for i in range(first, first + count):
                    c = (i // PE_TAPS + KD // 2) % KD
                    col = (DVE_TAPS + i % PE_TAPS) * KD + c
                    if i >= DIAG:
                        act.wait_ge(diag_used, i - DIAG + 1)
                    nc.scalar.activation(diag[:, i % DIAG, :], ident[:, :], ACT.Copy,
                                         scale=prm_T[:, col:col + 1]).then_inc(diag_ready, 1)

            for j in range(2):
                for i, s in enumerate(range(U_PW1 + 4 * j + 3, U_PW1 + 4 * j + 6)):
                    high(s)
                    if j == 1:
                        tap_diagonals(4 * i, 4)
                act.wait_ge(unit_used, U_PW1 + 4 * j + 4)
                if j == 0:
                    act.wait_ge(prm_ready, 1)
                else:
                    act.wait_ge(glu_ready, 4)
                for c in range(4):
                    ch = A_PW1 + KD + 4 * j + c
                    nc.scalar.activation(sig[:, c, :], ps[:, 4 + c, 0:SEQ], ACT.Sigmoid,
                                         bias=prm_T[:, ch:ch + 1]).then_inc(sig_ready, 1)
                high(U_PW1 + 4 * j + 6)
            for b in range(1, KD):
                tap_diagonals(b * PE_TAPS, PE_TAPS)
                if b <= 4:
                    c = b + 3
                    act.wait_ge(diag_used, b * PE_TAPS)
                    nc.scalar.activation(cv[:, c, :], ps[:, c, 0:SEQ], ACT.Identity,
                                         bias=prm_T[:, A_DW + c:A_DW + c + 1]).then_inc(base_ready, 1)
            nc.scalar.activation(tick[:, 1:2], tick[:, 0:1], ACT.Sqrt)
            for i in range(KD // 2):
                act.wait_ge(dev_ready, i + 1)
                nc.scalar.activation(sq[:, 2 * i:2 * i + 2, :], cv[:, 2 * i:2 * i + 2, :],
                                     ACT.Square).then_inc(sq_ready, 1)
            act.wait_ge(var_ready, 1)
            nc.scalar.activation(std[:, :], var_e[:, :], ACT.Sqrt).then_inc(std_ready, 1)
            for c in range(KD):
                act.wait_ge(ln_ready, c // 2 + 1)
                nc.scalar.activation(sq[:, c, :], cv[:, c, :], ACT.Silu, bias=prm_T[:, A_B + c:A_B + c + 1],
                                     scale=prm_T[:, A_G + c:A_G + c + 1]).then_inc(act_ready, 1)
                if c % 2:
                    act.wait_ge(act_ready, c + 1)
                    nc.scalar.copy(c_hi[:, c - 1:c + 1, :], sq[:, c - 1:c + 1, :]).then_inc(c_hi_ready, 1)
            for s in range(U_PW2 + 3, U_EXP + 2):
                high(s)

            norm_sums(3, BY_HALF)
            turned_high(4, 0)
            for t in range(T):
                act.wait_ge(rows_ready, 20)
                nc.scalar.copy(r_hi[:, t, :], rows[:, t, :]).then_inc(r_hi_ready, 1)
            act.wait_ge(dlt_ready, 1)
            nc.scalar.activation(ex[:, :], dlt[:, :], ACT.Exp).then_inc(ex_ready, 1)

            def gathered(p, quarter):
                act.wait_ge(gather_mm, 4 * p + quarter + 1)
                dst = c_hi if quarter == 0 else c_lo
                nc.scalar.copy(dst[:, 0:4, 0:P], ps[:, 0, :].rearrange("p (b m) -> p b m", b=4)).then_inc(gather_a, 1)

            gathered(0, 0)
            gathered(0, 2)

            def expert_pass(p):
                r, q = ROUNDS * p, CH + CH * p
                swiglu_first(U_EXP, q, EXPERT, r)
                swiglu_loop(U_EXP, q, EXPERT, r)
                hid_high(q + CH - 1, 1, EXPERT["up"])
                gathered(p + 1, 0)
                high(U_EXP + U_PASS, r)
                gathered(p + 1, 2)
                high(U_EXP + U_PASS + 1, r)
                act.wait_ge(unit_used, U_EXP + U_PASS + RAW * r)
                act.wait_ge(slot_w_ready, p + 1)
                nc.scalar.activation(y_hi[:, :], ps[:, 2:4, :].rearrange("p b n -> p (b n)"), ACT.Copy,
                                     scale=slot_w[:, 0:1]).then_inc(y_hi_ready, 1)

            with act.Fori(0, E) as p:
                expert_pass(p)
            act.wait_ge(plan_ready, 1)
            extra = act.value_load(plan[0:1, EXTRA:EXTRA + 1], min_val=0, max_val=EXTRA - 1)
            with act.If(extra > 0):
                with act.Fori(0, extra) as j:
                    expert_pass(j + E)
            norm_sums(4, BY_TILE)

        @block.vector
        def _(dve):
            chain = [0]

            def link(ins):
                chain[0] += 1
                ins.then_inc(dve_step, 1)
                dve.wait_ge(dve_step, chain[0])

            def low(s, r=0):
                dve.wait_ge(hi_ready, s + 1 + RAW * r)
                nc.vector.tensor_tensor(w_lo[:, s % SPLIT, :], raw[:, s % RAW, :], w_hi[:, s % SPLIT, :],
                                        ALU.subtract).then_inc(split_ready, 1)

            def norm(k, slot, gain_in):
                dve.wait_ge(ss_ready, 4 * (k + 1))
                link(nc.vector.tensor_tensor(ms[:, :], ss[:, :, 0], ss[:, :, 1], ALU.add))
                nc.vector.tensor_scalar(ms[:, :], ms[:, :], 1.0 / D, EPS, ALU.mult, ALU.add).then_inc(ms_ready, 1)
                dve.wait_ge(rt_ready, k + 1)
                dve.wait_ge(ms_ready, k + 1)
                link(nc.vector.reciprocal(rs[:, :], rt[:, :]))
                link(nc.vector.scalar_tensor_tensor(rq[:, :], rs[:, :], -0.5, rs[:, :], ALU.mult, ALU.mult))
                link(nc.vector.tensor_tensor(rq[:, :], rq[:, :], ms[:, :], ALU.mult))
                link(nc.vector.scalar_tensor_tensor(rs[:, :], rq[:, :], 1.5, rs[:, :], ALU.add, ALU.mult))
                dve.wait_ge(gain_in, 16)
                for t, h in BY_HALF:
                    at = slice(h * NC, (h + 1) * NC)
                    nc.vector.scalar_tensor_tensor(rows[:, t, at], x[:, t, at], rs[:, t:t + 1], bc[:, slot, at],
                                                   ALU.mult, ALU.mult).then_inc(rows_ready, 1)

            def turned_low(k, bank, base):
                for g, (t, half) in enumerate(BY_HALF):
                    dve.wait_ge(c_hi_ready, base + g + 1)
                    nc.vector.tensor_tensor(c_lo[:, 4 * half:4 * half + 4, t * P:(t + 1) * P],
                                            ps[:, bank + g, :].rearrange("p (b m) -> p b m", b=4),
                                            c_hi[:, 4 * half:4 * half + 4, t * P:(t + 1) * P],
                                            ALU.subtract).then_inc(c_ready, 1)

            def add_quarter(t, h, bank):
                nc.vector.tensor_tensor(x[:, t, h * NC:(h + 1) * NC], x[:, t, h * NC:(h + 1) * NC], ps[:, bank, :],
                                        ALU.add).then_inc(x_ready, 1)

            def add_projection(s, h, done):
                if h == 0:
                    dve.wait_ge(unit_used, s + 2)
                    add_quarter(0, 0, 4)
                    add_quarter(1, 0, 5)
                else:
                    dve.wait_ge(bank_done, done)
                    add_quarter(0, 1, 6)
                    dve.wait_ge(unit_used, s + 4)
                    add_quarter(1, 1, 7)

            def hid_low(q, tiles, up):
                dve.wait_ge(h_hi_ready, q + 1)
                nc.vector.tensor_tensor(h_lo[:, 0:tiles].rearrange("p t b m -> p t (b m)"),
                                        ps[:, up:up + tiles, :],
                                        h_hi[:, 0:tiles].rearrange("p t b m -> p t (b m)"),
                                        ALU.subtract).then_inc(h_ready, 1)

            def hidden(s, q, tiles, up, r):
                dve.wait_ge(unit_used, s + 2 + RAW * r)
                dve.wait_ge(silu_ready, q + 1)
                nc.vector.tensor_tensor(hid[:, 0:tiles, :], gate[:, 0:tiles, :], ps[:, up:up + tiles, :],
                                        ALU.mult).then_inc(hid_ready, 1)

            def swiglu_first(s, q, L, r=0):
                for j in range(2, 6):
                    low(s + j, r)
                hidden(s + 2, q, L["tiles"], L["up"], r)

            def swiglu_loop(s, q, L, r=0):
                with dve.Fori(0, CH - 1) as i:
                    hid_low(q + i, L["tiles"], L["up"])
                    for j in range(6, 10):
                        low(s + j, r + i)
                    hidden(s + 6, q + 1 + i, L["tiles"], L["up"], r + i)
                    low(s + 10, r + i)
                    low(s + 11, r + i)

            nc.vector.memset(tick[:, :], 1.0).then_inc(tick_ready, 1)
            norm(0, 0, bc_in[0])
            low(0)
            turned_low(0, 4, 0)
            low(1)
            low(2)
            dve.wait_ge(small_hi, 1)
            nc.vector.tensor_tensor(wf_parts[:, :, 1, :], wf[:, :, :], wf_parts[:, :, 0, :],
                                    ALU.subtract).then_inc(small_split, 1)
            dve.wait_ge(small_hi, 2)
            nc.vector.tensor_tensor(wr_parts[:, :, 1, :], wr[:, :, :], wr_parts[:, :, 0, :],
                                    ALU.subtract).then_inc(small_split, 1)

            for g in range(5):
                if g:
                    low(2 * g + 1)
                    low(2 * g + 2)
                if g in (2, 3):
                    dve.wait_ge(unit_used, U_QKV + 2 * g + 2)
                    banks = slice(4 * (g % 2), 4 * (g % 2) + 4)
                    nc.vector.tensor_copy(k_T[:, 4 * (g - 2):4 * (g - 2) + 4, :],
                                          ps[:, banks, 0:SEQ]).then_inc(k_out, 1)

            dve.wait_ge(narrow_mm, 1)
            nc.vector.tensor_copy(narrow[0:2 * H, :], ps[0:2 * H, 4, 0:SEQ]).then_inc(narrow_out, 1)
            low(U_QKV + 11)
            dve.wait_ge(fg_mm, 1)
            dve.wait_ge(small_in[1], 16)
            link(nc.vector.tensor_tensor(z[:, :, :], ps[:, 5, 0:T * H].rearrange("p (t h) -> p t h", t=T),
                                         bf_bc[:, None, :].to_broadcast([P, T, H]), ALU.add))
            nc.vector.tensor_scalar(z_min[:, :, :], z[:, :, :], 0.0, None, ALU.min)
            nc.vector.scalar_tensor_tensor(z_abs[:, :, :], z[:, :, :], -1.0, z[:, :, :],
                                           ALU.mult, ALU.max).then_inc(z_ready, 1)
            low(U_WO)
            dve.wait_ge(z_log_ready, 1)
            dve.wait_ge(z_ready, 1)
            nc.vector.tensor_tensor(log_f[:, :, :], z_min[:, :, :], z_log[:, :, :],
                                    ALU.subtract).then_inc(log_f_ready, 1)
            low(U_WO + 1)
            dve.wait_ge(c_mm, 1)
            dve.wait_ge(gp_step, 15)
            nc.vector.tensor_copy(c_pad[:, :, 0:H], ps[:, 6, 0:T * H].rearrange("p (t h) -> p t h", t=T))\
              .then_inc(c_out, 1)
            dve.wait_ge(cT_mm, 1)
            nc.vector.tensor_scalar(neg_cT[:, :], ps[:, 7, 0:SEQ], -1.0, None, ALU.mult).then_inc(cT_out, 1)
            low(U_WO + 2)
            dve.wait_ge(c_out, 1)
            dve.wait_ge(consts_ready, 7)
            for h in range(H):
                dve.wait_ge(s_mm, h + 1)
                if h >= 2:
                    dve.wait_ge(exp_ready, h - 1)
                nc.vector.scalar_tensor_tensor(sm[:, h % 2, 0:P], ps[:, h % 2, 0:P], c_pad[:, 0, h:h + 1],
                                               mask[:, 0:P], ALU.add, ALU.add)
                nc.vector.scalar_tensor_tensor(sm[:, h % 2, P:3 * P], ps[:, h % 2, P:3 * P], c_pad[:, 1, h:h + 1],
                                               mask[:, P:3 * P], ALU.add, ALU.add).then_inc(sm_ready, 1)
                dve.wait_ge(sm_ready, h + 1)
                nc.vector.tensor_reduce(nm[:, h, 0:1], sm[:, h % 2, 0:P], AX.X, ALU.max, negate=True)
                nc.vector.tensor_reduce(nm[:, h, 1:2], sm[:, h % 2, P:3 * P], AX.X, ALU.max,
                                        negate=True).then_inc(max_ready, 1)
            dve.wait_ge(exp_ready, H)
            link(nc.vector.reciprocal(inv_rows[:, :, :], psum_rows[:, :, :]))
            dve.wait_ge(pv_mm, H)
            for t, h in BY_HALF:
                heads = slice(h * H // 2, (h + 1) * H // 2)
                nc.vector.tensor_tensor(rows[:, t, h * NC:(h + 1) * NC].rearrange("p (h d) -> p h d", d=HD),
                                        ps[:, 4 + 2 * t + h, :].rearrange("p (h d) -> p h d", d=HD),
                                        inv_rows[:, t, heads, None].to_broadcast([P, H // 2, HD]),
                                        ALU.mult).then_inc(rows_ready, 1)
            turned_low(1, 0, 4)
            low(U_WO + 3)
            low(U_WO + 4)
            add_projection(U_WO, 0, 0)
            low(U_WO + 5)
            add_projection(U_WO, 1, 1)

            norm(1, 1, bc_in[1])
            turned_low(2, 4, 8)
            low(U_DENSE + 2)
            dve.wait_ge(prm_mm, 1)
            nc.vector.tensor_copy(prm_T[:, :], ps[:, 4, 0:3 * P]).then_inc(prm_ready, 1)
            for s in range(U_DENSE + 3, U_DENSE + 6):
                low(s)
            hidden(U_DENSE + 2, 0, T, DENSE["up"], 0)
            swiglu_loop(U_DENSE, 0, DENSE)
            hid_low(CH - 1, T, DENSE["up"])
            low(U_PW1)
            low(U_PW1 + 1)
            for i, (t, h) in enumerate(BY_TILE):
                if i < 3:
                    dve.wait_ge(bank_done, 1 + i + 1)
                else:
                    dve.wait_ge(unit_used, U_DENSE + U_PASS)
                add_quarter(t, h, DENSE["y"] + i)

            norm(2, 2, bc_in[2])
            turned_low(3, 4, 12)
            low(U_PW1 + 2)
            dve.wait_ge(prm_ready, 1)
            dve.wait_ge(glu_clear, 1)
            steps, step_of = [0], {}

            def conv_tap(c, tap):
                src = glu[:, c, tap:tap + SEQ]
                wt = prm_T[:, tap * KD + c:tap * KD + c + 1]
                if tap:
                    dve.wait_ge(conv_step, step_of[c])
                elif c >= KD // 2:
                    dve.wait_ge(base_ready, c - KD // 2 + 1)
                if tap == 0 and c < KD // 2:
                    ins = nc.vector.tensor_scalar(cv[:, c, :], src, wt, prm_T[:, A_DW + c:A_DW + c + 1],
                                                  ALU.mult, ALU.add)
                else:
                    ins = nc.vector.scalar_tensor_tensor(cv[:, c, :], src, wt, cv[:, c, :], ALU.mult, ALU.add)
                if c >= KD // 2 and tap == DVE_TAPS - 1:
                    ins.then_inc(conv_out, 1)
                else:
                    ins.then_inc(conv_step, 1)
                    steps[0] += 1
                    step_of[c] = steps[0]

            def conv_taps(blocks, first, last):
                for tap in range(first, last):
                    for c in blocks:
                        conv_tap(c, tap)

            for j in range(2):
                for i, s in enumerate(range(U_PW1 + 4 * j + 3, U_PW1 + 4 * j + 6)):
                    low(s)
                    if j == 1:
                        if i == 0:
                            dve.wait_ge(glu_ready, KD // 2)
                        conv_taps(range(KD // 2), 2 * i, 2 * i + 2)
                for c in range(4):
                    ch = A_PW1 + 4 * j + c
                    dve.wait_ge(sig_ready, 4 * j + c + 1)
                    nc.vector.scalar_tensor_tensor(glu[:, 4 * j + c, PAD:PAD + SEQ], ps[:, c, 0:SEQ],
                                                   prm_T[:, ch:ch + 1], sig[:, c, :],
                                                   ALU.add, ALU.mult).then_inc(glu_ready, 1)
                low(U_PW1 + 4 * j + 6)
            conv_taps(range(KD // 2), 6, DVE_TAPS)
            dve.wait_ge(glu_ready, KD)
            conv_taps(range(KD // 2, KD), 0, DVE_TAPS)
            for c in range(KD // 2):
                dve.wait_ge(diag_used, (KD // 2 + c + 1) * PE_TAPS)
                dve.wait_ge(conv_step, step_of[c])
                nc.vector.tensor_tensor(cv[:, c, :], cv[:, c, :], ps[:, c, 0:SEQ], ALU.add).then_inc(conv_out, 1)

            dve.wait_ge(mean_mm, 1)
            dve.wait_ge(conv_out, KD)
            for i in range(KD // 2):
                two = cv[:, 2 * i:2 * i + 2, :]
                nc.vector.tensor_tensor(two, two, ps[:, 4:5, 0:SEQ].to_broadcast([P, 2, SEQ]),
                                        ALU.subtract).then_inc(dev_ready, 1)
            dve.wait_ge(var_mm, 1)
            nc.vector.tensor_scalar(var_e[:, :], ps[:, 5, 0:SEQ], EPS, None, ALU.add).then_inc(var_ready, 1)
            dve.wait_ge(std_ready, 1)
            link(nc.vector.reciprocal(rstd[:, :], std[:, :]))
            dve.wait_ge(dev_ready, KD // 2)
            for i in range(KD // 2):
                two = cv[:, 2 * i:2 * i + 2, :]
                nc.vector.tensor_tensor(two, two, rstd[:, None, :].to_broadcast([P, 2, SEQ]),
                                        ALU.mult).then_inc(ln_ready, 1)
            for i in range(KD // 2):
                dve.wait_ge(c_hi_ready, 16 + i + 1)
                nc.vector.tensor_tensor(c_lo[:, 2 * i:2 * i + 2, :], sq[:, 2 * i:2 * i + 2, :],
                                        c_hi[:, 2 * i:2 * i + 2, :], ALU.subtract).then_inc(c_ready, 1)
            dve.wait_ge(bc_in[5], 16)
            link(nc.vector.tensor_tensor(x[:, :, :], x[:, :, :], bc[:, 2:3, :].to_broadcast([P, T, D]), ALU.add))
            low(U_PW2 + 3)
            low(U_PW2 + 4)
            add_projection(U_PW2, 0, 0)
            low(U_PW2 + 5)
            add_projection(U_PW2, 1, 5)

            dve.wait_ge(consts_ready, 7)
            nc.vector.tensor_scalar(eight[:, :], slot_row[:, 0:E], -1.0, None, ALU.add)
            link(nc.vector.tensor_tensor(below[:, :, :], slot_row[:, None, 0:E].to_broadcast([P, E, E]),
                                         slot_row[:, 0:E, None].to_broadcast([P, E, E]), ALU.is_lt))

            norm(3, 0, bc_in[3])
            turned_low(4, 0, 20)
            for t in range(T):
                dve.wait_ge(r_hi_ready, t + 1)
                nc.vector.tensor_tensor(r_lo[:, t, :], rows[:, t, :], r_hi[:, t, :], ALU.subtract).then_inc(r_ready, 1)
                if t == 0:
                    dve.wait_ge(narrow_mm, 2)
                    nc.vector.tensor_copy(narrow[0:2 * E, :], ps[0:2 * E, 4, 0:SEQ]).then_inc(narrow_out, 1)
            dve.wait_ge(lg_mm, 1)
            link(nc.vector.tensor_copy(lg[:, :, :], ps[:, 5, 0:T * E].rearrange("p (t e) -> p t e", t=T)))
            for t in range(T):
                one, other = (lg[:, t, None, :].to_broadcast([P, E, E]), lg[:, t, :, None].to_broadcast([P, E, E]))
                nc.vector.tensor_tensor(better[:, t], one, other, ALU.is_gt)
                ins = nc.vector.tensor_tensor(equal[:, t], one, other, ALU.is_equal)
            link(ins)
            for t in range(T):
                ins = nc.vector.tensor_tensor(equal[:, t], equal[:, t], below[:, :, :], ALU.mult)
            link(ins)
            for t in range(T):
                ins = nc.vector.tensor_tensor(better[:, t], better[:, t], equal[:, t], ALU.add)
            link(ins)
            link(nc.vector.tensor_reduce(place[:, :, :], better[:, :, :, :], AX.X, ALU.add))
            nc.vector.tensor_scalar(chosen[:, :, :], place[:, :, :], 2.0, None, ALU.is_lt).then_inc(chosen_ready, 1)
            for j in range(2):
                nc.vector.tensor_scalar(oh[:, j], place[:, :, :], float(j), None, ALU.is_equal)
            for t in range(T):
                ins = nc.vector.max(top[:, t, :], lg[:, t, :])
            link(ins)
            nc.vector.tensor_tensor(dlt[:, :], top[:, :, 1], top[:, :, 0], ALU.subtract).then_inc(dlt_ready, 1)
            dve.wait_ge(rank_mm, 1)
            dve.wait_ge(chosen_ready, 1)
            nc.vector.scalar_tensor_tensor(rank[:, :, 0:E],
                                           ps[:, 6, 0:T * E].rearrange("p (t e) -> p t e", t=T), 1.0,
                                           chosen[:, :, :], ALU.add, ALU.mult)
            link(nc.vector.tensor_scalar(over[:, :], ps[:, 6, T * E:(T + 1) * E], float(CAP), None, ALU.is_gt))

            def make_pick(p):
                for t in range(T):
                    ins = nc.vector.tensor_scalar(pick[:, t, :], slot_row[:, :], rank[:, t, bass.ds(p, 1)], None,
                                                  ALU.is_equal)
                ins.then_inc(pick_ready, 1)

            def make_rank_diagonals(p):
                for t in range(T):
                    ins = nc.vector.tensor_scalar(rank_d[:, t, :], ident[:, :], rank[:, t, bass.ds(p, 1)], None,
                                                  ALU.mult)
                ins.then_inc(rank_d_ready, 1)

            def make_put(p):
                dve.wait_ge(rank_row_mm, p + 1)
                nc.vector.tensor_scalar(put[:, :], ps[:, EXPERT["y"] + 1, 0:SEQ],
                                        slot_col[:, 0:1], None, ALU.is_equal).then_inc(put_ready, 1)

            def gathered(p, quarter):
                dve.wait_ge(gather_mm, 4 * p + quarter + 1)
                dst = c_hi if quarter == 1 else c_lo
                nc.vector.tensor_copy(dst[:, 4:8, 0:P],
                                      ps[:, 1, :].rearrange("p (b m) -> p b m", b=4)).then_inc(gather_v, 1)

            make_pick(0)
            dve.wait_ge(ex_ready, 1)
            link(nc.vector.tensor_scalar(p_top[:, 1, :], ex[:, :], 1.0, None, ALU.add))
            link(nc.vector.reciprocal(p_top[:, 0, :], p_top[:, 1, :]))
            link(nc.vector.tensor_tensor(p_top[:, 1, :], p_top[:, 0, :], ex[:, :], ALU.mult))
            nc.vector.tensor_tensor(comb[:, :, 0:E], oh[:, 0], p_top[:, 0, :, None].to_broadcast([P, T, E]), ALU.mult)
            link(nc.vector.tensor_tensor(comb_2[:, :, :], oh[:, 1], p_top[:, 1, :, None].to_broadcast([P, T, E]),
                                         ALU.mult))
            link(nc.vector.tensor_tensor(comb[:, :, 0:E], comb[:, :, 0:E], comb_2[:, :, :], ALU.add))
            gathered(0, 1)
            link(nc.vector.tensor_tensor_scan(nth[:, :], ones[:, 0:E], over[:, :], 0.0, ALU.mult, ALU.add))
            for j in range(EXTRA):
                nc.vector.scalar_tensor_tensor(sel[:, j, :], nth[:, :], float(j + 1), over[:, :],
                                               ALU.is_equal, ALU.mult)
            link(nc.vector.tensor_reduce(plan_f[:, EXTRA:EXTRA + 1], over[:, :], AX.X, ALU.add))
            link(nc.vector.tensor_tensor(prod[:, 0], sel[:, :, :], eight[:, None, :].to_broadcast([P, EXTRA, E]),
                                         ALU.mult))
            link(nc.vector.tensor_reduce(plan_f[:, 0:EXTRA], prod[:, 0], AX.X, ALU.add))
            nc.vector.tensor_copy(plan[:, :], plan_f[:, :]).then_inc(plan_ready, 1)
            gathered(0, 3)
            for table in (rank, comb):
                for t in range(T):
                    link(nc.vector.tensor_tensor(prod[:, t], sel[:, :, :],
                                                 table[:, t, None, 0:E].to_broadcast([P, EXTRA, E]), ALU.mult))
                link(nc.vector.tensor_reduce(part[:, :, :], prod[:, :, :, :], AX.X, ALU.add))
                link(nc.vector.tensor_scalar(table[:, :, E:PASSES], part[:, :, :],
                                             -float(CAP) if table is rank else 0.0, None, ALU.add))
            link(nc.vector.tensor_copy(comb_r[:, :, :, 0].rearrange("p e t -> p t e"), comb[:, :, :]))
            nc.vector.tensor_tensor(comb_r[:, :, :, 1].rearrange("p e t -> p t e"), comb[:, :, :],
                                    comb_r[:, :, :, 0].rearrange("p e t -> p t e"), ALU.subtract).then_inc(comb_ready, 1)

            def expert_pass(p):
                r, q = ROUNDS * p, CH + CH * p
                swiglu_first(U_EXP, q, EXPERT, r)
                make_rank_diagonals(p)
                dve.wait_ge(slot_w_mm, p + 1)
                nc.vector.tensor_reduce(slot_w[:, 0:1], ps[:, 2, 0:2], AX.X, ALU.add).then_inc(slot_w_ready, 1)
                make_pick(p + 1)
                dve.wait_ge(scatter_mm, p + 1)
                make_put(p)
                swiglu_loop(U_EXP, q, EXPERT, r)
                hid_low(q + CH - 1, 1, EXPERT["up"])
                low(U_EXP + U_PASS, r)
                gathered(p + 1, 1)
                low(U_EXP + U_PASS + 1, r)
                gathered(p + 1, 3)
                dve.wait_ge(y_hi_ready, p + 1)
                nc.vector.scalar_tensor_tensor(y_lo[:, :], ps[:, 2:4, :].rearrange("p b n -> p (b n)"),
                                               slot_w[:, 0:1], y_hi[:, :], ALU.mult, ALU.subtract)\
                  .then_inc(y_ready, 1)

            with dve.Fori(0, E) as p:
                expert_pass(p)
            extra = dve.value_load(plan[0:1, EXTRA:EXTRA + 1], min_val=0, max_val=EXTRA - 1)
            with dve.If(extra > 0):
                with dve.Fori(0, extra) as j:
                    expert_pass(j + E)
            for i, (t, h) in enumerate(BY_TILE):
                dve.wait_ge(moe_mm, i + 1)
                add_quarter(t, h, SUM + i)
            norm(4, 1, bc_in[4])

        @block.tensor
        def _(pe):
            mm = nc.tensor.matmul

            def moving(dst, hi, lo, s, at, start, stop):
                wh, wl = w_hi[:, s % SPLIT, at:at + NC], w_lo[:, s % SPLIT, at:at + NC]
                mm(dst, hi, wh, start=start, stop=False, skip_group_check=True)
                mm(dst, hi, wl, start=False, stop=False, skip_group_check=True)
                return mm(dst, lo, wh, start=False, stop=stop, skip_group_check=True)

            def turn_rows(k, bank):
                for g, (t, half) in enumerate(BY_HALF):
                    pe.wait_ge(rows_ready, 4 * k + g + 1)
                    for b in range(4):
                        at = (4 * half + b) * P
                        last = nc.tensor.transpose(ps[:, bank + g, b * P:(b + 1) * P], rows[:, t, at:at + P], ident[:, :])
                    last.then_inc(turn_mm, 1)

            def column_unit(s, half, bank, tiles, r=0, tell=False):
                pe.wait_ge(split_ready, s + 1 + RAW * r)
                for t in range(tiles):
                    for k in range(4):
                        kk = 4 * half + k
                        last = moving(ps[:, bank + t, :], c_hi[:, kk, t * P:(t + 1) * P],
                                      c_lo[:, kk, t * P:(t + 1) * P], s, k * NC, kk == 0, kk == KD - 1)
                    if tell and t < tiles - 1:
                        last.then_inc(bank_done, 1)
                return last.then_inc(unit_used, 1)

            def feature_unit(s, half, bank):
                pe.wait_ge(split_ready, s + 1)
                for k in range(4):
                    kk = 4 * half + k
                    for b in range(4):
                        at = k * NC + b * P
                        wh, wl = w_hi[:, s % SPLIT, at:at + P], w_lo[:, s % SPLIT, at:at + P]
                        dst = ps[:, bank + b, 0:SEQ]
                        mm(dst, wh, c_hi[:, kk, :], start=kk == 0, stop=False)
                        mm(dst, wh, c_lo[:, kk, :], start=False, stop=False)
                        last = mm(dst, wl, c_hi[:, kk, :], start=False, stop=kk == KD - 1)
                return last.then_inc(unit_used, 1)

            def narrow_product(cat, n):
                for k in range(KD):
                    for part in (c_hi, c_lo):
                        last = mm(ps[:, 4, 0:SEQ], cat[:, 2 * n * k:2 * n * k + P], part[:, k, :],
                                  start=k == 0 and part is c_hi, stop=k == KD - 1 and part is c_lo)
                last.then_inc(narrow_mm, 1)

            def narrow_rows(n):
                for t in range(T):
                    for part in range(2):
                        last = mm(ps[:, 5, t * n:(t + 1) * n], narrow[0:2 * n, t * P:(t + 1) * P],
                                  ident[0:2 * n, part * n:(part + 1) * n], start=part == 0, stop=part == 1)
                return last

            def clear(bank, n):
                for b in range(n):
                    last = mm(ps[:, bank + b, :], zero_r[:, 0:P], zero_r[:, :], start=True, stop=False,
                              skip_group_check=True)
                return last

            def gate_products(s, q, L, r=0):
                column_unit(s, 0, L["gate"], L["tiles"], r)
                column_unit(s + 1, 1, L["gate"], L["tiles"], r)

            def up_products(s, q, L, r=0):
                column_unit(s, 0, L["up"], L["tiles"], r)
                column_unit(s + 1, 1, L["up"], L["tiles"], r)

            def down(s, half, L, r=0, stop=False, tell=False):
                pe.wait_ge(split_ready, s + 1 + RAW * r)
                for i, (t, n) in enumerate(BY_TILE[0:2 * L["tiles"]]):
                    for k in range(2):
                        hi, lo = h_hi[:, t, 2 * half + k, :], h_lo[:, t, 2 * half + k, :]
                        last = moving(ps[:, L["y"] + i, :], hi, lo, s, k * D + n * NC, False, stop and k == 1)
                    if tell and i < 2 * L["tiles"] - 1:
                        last.then_inc(bank_done, 1)
                return last.then_inc(unit_used, 1)

            def turn_hidden(q, L):
                pe.wait_ge(hid_ready, q + 1)
                for t in range(L["tiles"]):
                    for b in range(4):
                        last = nc.tensor.transpose(ps[:, L["up"] + t, b * P:(b + 1) * P],
                                                   hid[:, t, b * P:(b + 1) * P], ident[:, :])
                last.then_inc(hidT_mm, 1)

            def swiglu_loop(s, q, L, r=0):
                with pe.Fori(0, CH - 1) as i:
                    gate_products(s + 4, q + 1 + i, L, r + i)
                    pe.wait_ge(h_ready, q + 1 + i)
                    up_products(s + 6, q + 1 + i, L, r + i)
                    down(s + 8, 0, L, r + i)
                    down(s + 9, 1, L, r + i)
                    turn_hidden(q + 1 + i, L)

            pe.wait_ge(consts_ready, 7)
            pe.wait_ge(gp_step, 15)
            turn_rows(0, 4)
            for g in range(4):
                if g >= 2:
                    pe.wait_ge(q_out, g - 1)
                for half in range(2):
                    if g == 0:
                        pe.wait_ge(c_ready, 2 * half + 2)
                    feature_unit(U_QKV + 2 * g + half, half, 4 * (g % 2))
            pe.wait_ge(k_out, 1)
            column_unit(U_QKV + 8, 0, 0, T)
            pe.wait_ge(k_out, 2)
            pe.wait_ge(small_split, 2)
            narrow_product(wf_cat, H)
            column_unit(U_QKV + 9, 1, 0, T)
            pe.wait_ge(narrow_out, 1)
            narrow_rows(H).then_inc(fg_mm, 1)
            column_unit(U_QKV + 10, 0, 2, T)
            pe.wait_ge(log_f_ready, 1)
            for t in range(T):
                dst = ps[:, 6, t * H:(t + 1) * H]
                for u in range(t):
                    mm(dst, ones[:, :], log_f[:, u, :], start=u == 0, stop=False)
                last = mm(dst, upto[:, :], log_f[:, t, :], start=t == 0, stop=True)
            last.then_inc(c_mm, 1)
            column_unit(U_QKV + 11, 1, 2, T)
            pe.wait_ge(c_out, 1)
            for t in range(T):
                last = nc.tensor.transpose(ps[:, 7, t * P:(t + 1) * P], c_pad[:, t, :], ident[:, :])
            last.then_inc(cT_mm, 1)
            pe.wait_ge(cT_out, 1)
            pe.wait_ge(v_out, 2)

            def scores(h):
                q = (q_even, q_odd)[h % 2]
                if h >= 2:
                    pe.wait_ge(sm_ready, h - 1)
                pick_c = ident[:, h:h + 1].to_broadcast([P, P])
                for t in range(T):
                    at = P if t else 0
                    n = (t + 1) * P
                    dst = ps[:, h % 2, at:at + n]
                    mm(dst, q[:, h // 2, t * P:(t + 1) * P], k_T[:, h // 2, 0:n], start=True, stop=False)
                    last = mm(dst, pick_c, neg_cT[:, 0:n], start=False, stop=True)
                last.then_inc(s_mm, 1)

            def turn_probs(h):
                pe.wait_ge(exp_ready, h + 1)
                if h >= 2:
                    pe.wait_ge(prT_ready, h - 1)
                for b in range(3):
                    last = nc.tensor.transpose(ps[:, 2 + h % 2, b * P:(b + 1) * P],
                                               pr[:, h % 2, b * P:(b + 1) * P], ident[:, :])
                last.then_inc(prT_mm, 1)

            def values(h):
                pe.wait_ge(prT_ready, h + 1)
                at = (h * HD) % NC
                for t in range(T):
                    dst = ps[:, 4 + 2 * t + h * HD // NC, at:at + HD]
                    for u in range(t + 1):
                        b = (u + 1) if t else 0
                        last = mm(dst, pr_T[:, h % 2, b * P:(b + 1) * P], v_sb[:, u, h * HD:(h + 1) * HD],
                                  start=u == 0, stop=u == t)
                last.then_inc(pv_mm, 1)

            for step in range(H + 2):
                if step < H:
                    scores(step)
                if 1 <= step <= H:
                    turn_probs(step - 1)
                if step >= 2:
                    values(step - 2)

            def projection(s, cols):
                for h in range(2):
                    for half in range(2):
                        if h == 0:
                            pe.wait_ge(c_ready, cols + 2 * half + 2)
                        column_unit(s + 2 * h + half, half, 4 + 2 * h, T, tell=h == 1 and half == 1)

            turn_rows(1, 0)
            projection(U_WO, 4)

            turn_rows(2, 4)
            pe.wait_ge(c_ready, 10)
            column_unit(U_DENSE, 0, DENSE["gate"], T)
            pe.wait_ge(c_ready, 12)
            column_unit(U_DENSE + 1, 1, DENSE["gate"], T)
            pe.wait_ge(prm_in, 6 * 16)
            for b in range(3):
                last = nc.tensor.transpose(ps[:, 4, b * P:(b + 1) * P], prm[:, b, :], ident[:, :])
            last.then_inc(prm_mm, 1)
            up_products(U_DENSE + 2, 0, DENSE)
            pe.wait_ge(prm_ready, 1)
            clear(DENSE["y"], 2 * T)
            turn_hidden(0, DENSE)
            swiglu_loop(U_DENSE, 0, DENSE)
            pe.wait_ge(h_ready, CH)
            down(U_DENSE + U_PASS - 2, 0, DENSE)
            down(U_DENSE + U_PASS - 1, 1, DENSE, stop=True, tell=True)

            turn_rows(3, 4)
            for g in range(4):
                if g == 2:
                    pe.wait_ge(glu_ready, 4)
                if g == 3:
                    pe.wait_ge(sig_ready, 4)
                for half in range(2):
                    if g == 0:
                        pe.wait_ge(c_ready, 12 + 2 * half + 2)
                    feature_unit(U_PW1 + 2 * g + half, half, 4 * (g % 2))
            pe.wait_ge(sig_ready, KD)
            pe.wait_ge(glu_ready, KD)
            for i in range(KD * PE_TAPS):
                c, n = (i // PE_TAPS + KD // 2) % KD, i % PE_TAPS
                tap = DVE_TAPS + n
                pe.wait_ge(diag_ready, i + 1)
                mm(ps[:, c, 0:SEQ], diag[:, i % DIAG, :], glu[:, c, tap:tap + SEQ],
                   start=n == 0, stop=n == PE_TAPS - 1).then_inc(diag_used, 1)
            for i in range(KD):
                c = (i + KD // 2) % KD
                pe.wait_ge(conv_out, i + 1)
                last = mm(ps[:, 4, 0:SEQ], mean_w[:, :], cv[:, c, :], start=i == 0, stop=i == KD - 1)
            last.then_inc(mean_mm, 1)
            for c in range(KD):
                pe.wait_ge(sq_ready, c // 2 + 1)
                last = mm(ps[:, 5, 0:SEQ], mean_w[:, :], sq[:, c, :], start=c == 0, stop=c == KD - 1)
            last.then_inc(var_mm, 1)
            projection(U_PW2, 16)

            turn_rows(4, 0)
            pe.wait_ge(c_ready, 24)
            narrow_product(wr_cat, E)
            pe.wait_ge(narrow_out, 2)
            narrow_rows(E).then_inc(lg_mm, 1)
            pe.wait_ge(chosen_ready, 1)
            for t in range(T):
                dst = ps[:, 6, t * E:(t + 1) * E]
                for u in range(t):
                    mm(dst, ones[:, :], chosen[:, u, :], start=u == 0, stop=False)
                mm(dst, before[:, :], chosen[:, t, :], start=t == 0, stop=True)
            for t in range(T):
                last = mm(ps[:, 6, T * E:(T + 1) * E], ones[:, :], chosen[:, t, :], start=t == 0, stop=t == T - 1)
            last.then_inc(rank_mm, 1)

            def gather(p, quarter):
                src = r_hi if quarter < 2 else r_lo
                bank = quarter % 2
                for b in range(4):
                    at = (4 * (quarter % 2) + b) * P
                    for t in range(T):
                        last = mm(ps[:, bank, b * P:(b + 1) * P], src[:, t, at:at + P], pick[:, t, :],
                                  start=t == 0, stop=t == T - 1)
                last.then_inc(gather_mm, 1)

            pe.wait_ge(r_ready, T)
            pe.wait_ge(pick_ready, 1)
            gather(0, 0)
            gather(0, 1)
            pe.wait_ge(gather_a, 1)
            gather(0, 2)
            pe.wait_ge(gather_v, 1)
            gather(0, 3)
            clear(SUM, 2 * T)
            pe.wait_ge(comb_ready, 1)

            def scatter(stop=False):
                for i, (t, h) in enumerate(BY_TILE):
                    dst = ps[:, SUM + i, :]
                    mm(dst, put[:, t * P:(t + 1) * P], y_hi[:, h * NC:(h + 1) * NC], start=False, stop=False,
                       skip_group_check=True)
                    last = mm(dst, put[:, t * P:(t + 1) * P], y_lo[:, h * NC:(h + 1) * NC], start=False,
                              stop=stop, skip_group_check=True)
                    if stop:
                        last.then_inc(moe_mm, 1)
                return last

            def expert_pass(p):
                r, q = ROUNDS * p, CH + CH * p
                pe.wait_ge(gather_a, 2 * p + 2)
                pe.wait_ge(gather_v, 2 * p + 2)
                gate_products(U_EXP, q, EXPERT, r)
                up_products(U_EXP + 2, q, EXPERT, r)
                pe.wait_ge(y_ready, p + 1)
                for t in range(T):
                    last = mm(ps[:, EXPERT["y"], 0:2], pick[:, t, :],
                              comb_r[:, bass.ds(p, 1), t, :].rearrange("p a b -> p (a b)"),
                              start=t == 0, stop=t == T - 1)
                last.then_inc(slot_w_mm, 1)
                scatter().then_inc(scatter_mm, 1)
                pe.wait_ge(rank_d_ready, p + 1)
                mm(ps[:, EXPERT["y"] + 1, 0:SEQ], ones_r[:, :], rank_d[:, :, :].rearrange("p t s -> p (t s)"),
                   start=True, stop=True).then_inc(rank_row_mm, 1)
                turn_hidden(q, EXPERT)
                pe.wait_ge(slot_w_ready, p + 1)
                pe.wait_ge(put_ready, p + 1)
                clear(EXPERT["y"], 2)
                swiglu_loop(U_EXP, q, EXPERT, r)
                pe.wait_ge(pick_ready, p + 2)
                gather(p + 1, 0)
                pe.wait_ge(h_ready, q + CH)
                down(U_EXP + U_PASS - 2, 0, EXPERT, r)
                gather(p + 1, 1)
                pe.wait_ge(gather_a, 2 * p + 3)
                gather(p + 1, 2)
                down(U_EXP + U_PASS - 1, 1, EXPERT, r, stop=True)
                pe.wait_ge(gather_v, 2 * p + 3)
                gather(p + 1, 3)

            with pe.Fori(0, E) as p:
                expert_pass(p)
            pe.wait_ge(plan_ready, 1)
            extra = pe.value_load(plan[0:1, EXTRA:EXTRA + 1], min_val=0, max_val=EXTRA - 1)
            with pe.If(extra > 0):
                with pe.Fori(0, extra) as j:
                    expert_pass(j + E)
            pe.wait_ge(y_ready, extra + E + 1)
            scatter(stop=True)


_INS = ['x', 'attn_norm', 'w_qkv', 'w_fgate', 'b_fgate', 'w_attn_out', 'conv_norm', 'w_pw1', 'b_pw1', 'w_dw', 'b_dw',
        'conv_ln_g', 'conv_ln_b', 'w_pw2', 'b_pw2', 'dense_norm', 'w_dense_gate', 'w_dense_up', 'w_dense_down',
        'moe_norm', 'w_router', 'w_exp_gate', 'w_exp_up', 'w_exp_down', 'final_norm']


def kernel(**inputs):
    import numpy as _np
    import concourse.bacc as _bacc
    from concourse import mybir as _mybir
    from concourse.bass_utils import run_bass_kernel_spmd as _run

    nc = _bacc.Bacc("TRN2", target_bir_lowering=False, num_devices=1)
    arrays, args = {}, []
    for name in _INS:
        a = _np.ascontiguousarray(inputs[name])
        arrays[f"in_{name}_dram"] = a
        args.append(nc.dram_tensor(f"in_{name}_dram", a.shape, _mybir.dt.from_np(a.dtype), kind="ExternalInput").ap())
    args.append(nc.dram_tensor("out_0_dram", inputs['x'].shape, _mybir.dt.float32, kind="ExternalOutput").ap())
    build_trunk(nc, *args)
    r = _run(nc, [arrays], core_ids=[0])
    return r.results[0]["out_0_dram"]
```

```python
from contextlib import ExitStack

import concourse.bass as bass
from concourse import mybir


def build_trunk(nc, x_in, attn_norm, w_qkv, w_fgate, b_fgate, w_attn_out, conv_norm, w_pw1, b_pw1, w_dw, b_dw,
                conv_ln_g, conv_ln_b, w_pw2, b_pw2, dense_norm, w_dense_gate, w_dense_up, w_dense_down,
                moe_norm, w_router, w_exp_gate, w_exp_up, w_exp_down, final_norm, out):
    f32, f32r, i32, u32 = mybir.dt.float32, mybir.dt.float32r, mybir.dt.int32, mybir.dt.uint32
    ALU, ACT, AX = mybir.AluOpType, mybir.ActivationFunctionType, mybir.AxisListType

    P = 128
    _, SEQ, D = x_in.shape
    T = SEQ // P
    KD = D // P
    H = w_fgate.shape[2]
    HD = D // H
    F = w_dense_gate.shape[2]
    E = w_exp_gate.shape[1]
    TAPS = w_dw.shape[1]
    EPS = 1e-6
    NC = 512
    UNIT = 4 * NC
    CH = F // NC
    RAW, SPLIT = 6, 3
    MASKED = -1e30
    CAP = P
    EXTRA = 4
    PASSES = E + EXTRA

    U_QKV = 0
    U_WO = U_QKV + 2 * (3 * D // NC)
    U_DENSE = U_WO + 2 * (D // NC)
    U_PW1 = U_DENSE + 6 * CH
    U_PW2 = U_PW1 + 2 * (2 * D // NC)
    U_EXP = U_PW2 + 2 * (D // NC)
    U_PASS = 6 * CH
    ROUNDS = U_PASS // RAW
    assert U_PASS % RAW == 0 and RAW % SPLIT == 0

    ctx = ExitStack()
    with ctx:
        def sb(name, shape, dt=f32, where=ctx):
            return where.enter_context(nc.sbuf_tensor(name, shape, dt))

        def sem(name):
            return ctx.enter_context(nc.semaphore(name))

        raw = sb("raw", [P, RAW, UNIT])
        w_hi = sb("w_hi", [P, SPLIT, UNIT], f32r)
        w_lo = sb("w_lo", [P, SPLIT, UNIT], f32r)
        x = sb("x", [P, T, D])
        rows = sb("rows", [P, T, D])
        c_hi = sb("c_hi", [P, KD, SEQ], f32r)
        c_lo = sb("c_lo", [P, KD, SEQ], f32r)
        gate = sb("gate", [P, T, NC])
        hid = sb("hid", [P, T, NC])
        h_hi = sb("h_hi", [P, T, 4, P], f32r)
        h_lo = sb("h_lo", [P, T, 4, P], f32r)
        bc = sb("bc", [P, 3, D])
        ident = sb("ident", [P, P])
        ones = sb("ones", [P, P])
        mean_w = sb("mean_w", [P, P])
        upto = sb("upto", [P, P])
        before = sb("before", [P, P])
        slot_row = sb("slot_row", [P, P])
        slot_col = sb("slot_col", [P, 1])
        iota_i = hid[:, 0, 0:P].bitcast(i32)
        iota_c = sb("iota_c", [P, 1], i32)
        eight = sb("eight", [P, E])
        zero_r = sb("zero_r", [P, NC], f32r)
        ss = sb("ss", [P, T, 2])
        ones_r = sb("ones_r", [P, P], f32r)
        tick = sb("tick", [P, 2])
        narrow = sb("narrow", [P, SEQ])
        ms = sb("ms", [P, T])
        rt = sb("rt", [P, T])
        rs = sb("rs", [P, T])
        rq = sb("rq", [P, T])
        wf = sb("wf", [P, KD, H])
        wf_cat = sb("wf_cat", [P, KD * 2 * H + P], f32r)
        wr = sb("wr", [P, KD, E])
        wr_cat = sb("wr_cat", [P, KD * 2 * E + P], f32r)
        bf_bc = sb("bf_bc", [P, H])

        wf_parts = wf_cat[:, 0:KD * 2 * H].rearrange("p (k c n) -> p k c n", k=KD, c=2)
        wr_parts = wr_cat[:, 0:KD * 2 * E].rearrange("p (k c n) -> p k c n", k=KD, c=2)
        sm, pr = gate[:, :, 0:3 * P], hid[:, :, 0:3 * P]

        with ExitStack() as region:
            q_even = sb("q_even", [P, KD, SEQ], f32, region)
            q_odd = sb("q_odd", [P, KD, SEQ], f32, region)
            k_T = sb("k_T", [P, KD, SEQ], f32, region)
            v_sb = sb("v_sb", [P, T, D], f32, region)
            pr_T = sb("pr_T", [P, 2, 3 * P], f32, region)
            mask = sb("mask", [P, 2 * P], f32, region)
            c_pad = sb("c_pad", [P, T, P], f32, region)
            neg_c_hi = sb("neg_c_hi", [P, SEQ], f32r, region)
            neg_c_lo = sb("neg_c_lo", [P, SEQ], f32r, region)
            ident_r = sb("ident_r", [P, P], f32r, region)
            nm = sb("nm", [P, H, T], f32, region)
            psum_rows = sb("psum_rows", [P, T, H], f32, region)
            inv_rows = sb("inv_rows", [P, T, H], f32, region)
            z = sb("z", [P, T, H], f32, region)
            z_min = sb("z_min", [P, T, H], f32, region)
            z_abs = sb("z_abs", [P, T, H], f32, region)
            z_exp = sb("z_exp", [P, T, H], f32, region)
            z_log = sb("z_log", [P, T, H], f32, region)
            log_f = sb("log_f", [P, T, H], f32, region)
        PAD = TAPS - 1
        with ExitStack() as region:
            glu = sb("glu", [P, KD, PAD + SEQ], f32, region)
            sig = sb("sig", [P, 4, SEQ], f32, region)
            cv = sb("cv", [P, KD, SEQ], f32, region)
            sq = sb("sq", [P, KD, SEQ], f32, region)
            prm = sb("prm", [P, 3, P], f32, region)
            prm_T = sb("prm_T", [P, 3 * P], f32, region)
            var_e = sb("var_e", [P, SEQ], f32, region)
            std = sb("std", [P, SEQ], f32, region)
            rstd = sb("rstd", [P, SEQ], f32, region)
        DIAG = KD * SEQ // P
        diag = sq[:, :, :].rearrange("p c s -> p (c s)").rearrange("p (i m) -> p i m", m=P)
        r_hi = sb("r_hi", [P, T, D], f32r)
        r_lo = sb("r_lo", [P, T, D], f32r)
        rank_d = sb("rank_d", [P, T, P], f32r)
        y_hi = sb("y_hi", [P, D], f32r)
        y_lo = sb("y_lo", [P, D], f32r)
        pick = sb("pick", [P, T, P], f32r)
        put = sb("put", [P, SEQ], f32r)
        slot_w = sb("slot_w", [P, 1])
        lg = sb("lg", [P, T, E])
        top = sb("top", [P, T, E])
        below = sb("below", [P, E, E])
        better = sb("better", [P, T, E, E])
        equal = sb("equal", [P, T, E, E])
        place = sb("place", [P, T, E])
        dlt = sb("dlt", [P, T])
        ex = sb("ex", [P, T])
        p_top = sb("p_top", [P, 2, T])
        oh = sb("oh", [P, 2, T, E])
        chosen = sb("chosen", [P, T, E])
        tables = sb("tables", [P, 2, T, PASSES])
        comb_2 = sb("comb_2", [P, T, E])
        over = sb("over", [P, E])
        nth = sb("nth", [P, E])
        sel = sb("sel", [P, EXTRA, E])
        prod = sb("prod", [P, 2, T, EXTRA, E])
        plan_f = sb("plan_f", [P, EXTRA + 1])
        plan = sb("plan", [P, EXTRA + 1], i32)
        comb_r = sb("comb_r", [P, PASSES, T, 2], f32r)
        rank, comb = tables[:, 0], tables[:, 1]

        ps = ctx.enter_context(nc.psum_tensor("ps", [P, 8, NC], f32))

        raw_in = [sem(f"raw_in{i}") for i in range(RAW)]
        hi_ready = sem("hi_ready")
        split_ready = sem("split_ready")
        unit_used = sem("unit_used")
        consts_ready = sem("consts_ready")
        gp_step = sem("gp_step")
        x_in_sem = [sem(f"x_in_sem{t}") for t in range(T)]
        tick_ready = sem("tick_ready")
        bank_done = sem("bank_done")
        narrow_mm = sem("narrow_mm")
        narrow_out = sem("narrow_out")
        small_in = [sem(f"small_in{i}") for i in range(3)]
        bc_in = [sem(f"bc_in{i}") for i in range(6)]
        dve_step = sem("dve_step")
        x_ready = sem("x_ready")
        ss_ready = sem("ss_ready")
        ms_ready = sem("ms_ready")
        rt_ready = sem("rt_ready")
        rows_ready = sem("rows_ready")
        turn_mm = sem("turn_mm")
        c_hi_ready = sem("c_hi_ready")
        c_ready = sem("c_ready")
        small_hi = sem("small_hi")
        small_split = sem("small_split")
        q_out = sem("q_out")
        k_out = sem("k_out")
        v_out = sem("v_out")
        fg_mm = sem("fg_mm")
        z_ready = sem("z_ready")
        z_exp_ready = sem("z_exp_ready")
        z_log_ready = sem("z_log_ready")
        log_f_ready = sem("log_f_ready")
        c_mm = sem("c_mm")
        c_out = sem("c_out")
        cT_mm = sem("cT_mm")
        cT_out = sem("cT_out")
        s_mm = sem("s_mm")
        sm_ready = sem("sm_ready")
        max_ready = sem("max_ready")
        exp_ready = sem("exp_ready")
        prT_mm = sem("prT_mm")
        prT_ready = sem("prT_ready")
        pv_mm = sem("pv_mm")
        silu_ready = sem("silu_ready")
        hid_ready = sem("hid_ready")
        hidT_mm = sem("hidT_mm")
        h_hi_ready = sem("h_hi_ready")
        h_ready = sem("h_ready")
        prm_in = sem("prm_in")
        prm_clear = sem("prm_clear")
        prm_mm = sem("prm_mm")
        prm_ready = sem("prm_ready")
        glu_clear = sem("glu_clear")
        sig_ready = sem("sig_ready")
        glu_ready = sem("glu_ready")
        conv_step = sem("conv_step")
        diag_ready = sem("diag_ready")
        diag_used = sem("diag_used")
        base_ready = sem("base_ready")
        conv_out = sem("conv_out")
        mean_mm = sem("mean_mm")
        dev_ready = sem("dev_ready")
        sq_ready = sem("sq_ready")
        var_mm = sem("var_mm")
        var_ready = sem("var_ready")
        std_ready = sem("std_ready")
        ln_ready = sem("ln_ready")
        act_ready = sem("act_ready")
        r_hi_ready = sem("r_hi_ready")
        r_ready = sem("r_ready")
        lg_mm = sem("lg_mm")
        dlt_ready = sem("dlt_ready")
        ex_ready = sem("ex_ready")
        chosen_ready = sem("chosen_ready")
        rank_mm = sem("rank_mm")
        comb_ready = sem("comb_ready")
        rank_d_ready = sem("rank_d_ready")
        rank_row_mm = sem("rank_row_mm")
        zeros_ready = sem("zeros_ready")
        plan_ready = sem("plan_ready")
        pick_ready = sem("pick_ready")
        put_ready = sem("put_ready")
        gather_mm = sem("gather_mm")
        gather_a = sem("gather_a")
        gather_v = sem("gather_v")
        slot_w_mm = sem("slot_w_mm")
        slot_w_ready = sem("slot_w_ready")
        y_hi_ready = sem("y_hi_ready")
        y_ready = sem("y_ready")
        scatter_mm = sem("scatter_mm")
        moe_mm = sem("moe_mm")
        stored = sem("stored")

        PE_TAPS = 14
        DVE_TAPS = TAPS - PE_TAPS
        PE_BLOCKS = (0, 1, 4, 5, 6, 7, 2, 3)
        CONV_DONE = (4, 5, 0, 1, 2, 3, 6, 7)
        BY_HALF = ((0, 0), (1, 0), (0, 1), (1, 1))
        BY_TILE = ((0, 0), (0, 1), (1, 0), (1, 1))

        DENSE = dict(tiles=T, gate=0, up=2, y=4)
        EXPERT = dict(tiles=1, gate=0, up=1, y=2)
        SUM = 4
        WD = w_dw.shape[1] * KD
        A_PW1, A_DW, A_G, A_B = 2 * P, 2 * P + 2 * KD, 2 * P + 3 * KD, 2 * P + 4 * KD

        block = ctx.enter_context(nc.Block())

        @block.sync
        def _(sp):
            def load(s, src, r=0):
                if s >= RAW or not isinstance(r, int):
                    sp.wait_ge(split_ready, s - RAW + 1 + RAW * r)
                k = src.shape[0] // P
                sp.dma_start(raw[:, s % RAW, :].rearrange("p (k n) -> p k n", k=k),
                             src.rearrange("(k p) n -> p k n", p=P)).then_inc(raw_in[s % RAW], 16)

            def load_columns(s, w, c, r=0):
                for half in range(2):
                    load(s + half, w[half * D // 2:(half + 1) * D // 2, bass.ds(c * NC, NC)], r)

            def load_swiglu(s, wg, wu, wd, r=0):
                def down(s, c, r):
                    for half in range(2):
                        load(s + half, wd[bass.ds(c * NC + half * (NC // 2), NC // 2), :], r)
                load_columns(s, wg, 0, r)
                load_columns(s + 2, wu, 0, r)
                with sp.Fori(0, CH - 1) as i:
                    load_columns(s + 4, wg, i + 1, r + i)
                    load_columns(s + 6, wu, i + 1, r + i)
                    down(s + 8, i, r + i)
                down(s + 6 * CH - 2, CH - 1, r)

            for t in range(T):
                sp.dma_start(x[:, t, :], x_in[0, t * P:(t + 1) * P, :]).then_inc(x_in_sem[t], 16)
            sp.dma_start(bc[:, 0, :], attn_norm[0].partition_broadcast(P)).then_inc(bc_in[0], 16)
            for c in range(3 * D // NC):
                load_columns(U_QKV + 2 * c, w_qkv[0], c)
            for c in range(D // NC):
                load_columns(U_WO + 2 * c, w_attn_out[0], c)
            load_swiglu(U_DENSE, w_dense_gate[0], w_dense_up[0], w_dense_down[0])
            for g, c in enumerate((2, 0, 3, 1)):
                load_columns(U_PW1 + 2 * g, w_pw1[0], c)
            for c in range(D // NC):
                load_columns(U_PW2 + 2 * c, w_pw2[0], c)

            def load_expert(e, p):
                load_swiglu(U_EXP, w_exp_gate[0, e], w_exp_up[0, e], w_exp_down[0, e], ROUNDS * p)

            with sp.Fori(0, E) as p:
                load_expert(p, p)
            sp.wait_ge(plan_ready, 1)
            extra = sp.value_load(plan[0:1, EXTRA:EXTRA + 1], min_val=0, max_val=EXTRA - 1)
            with sp.If(extra > 0):
                with sp.Fori(0, extra) as j:
                    e = sp.value_load(plan[0:1, bass.ds(j, 1)], min_val=0, max_val=E - 1)
                    load_expert(e, j + E)

            for i, (t, h) in enumerate(BY_HALF):
                sp.wait_ge(rows_ready, 20 + i + 1)
                sp.dma_start(out[0, t * P:(t + 1) * P, h * NC:(h + 1) * NC],
                             rows[:, t, h * NC:(h + 1) * NC]).then_inc(stored, 16)
            sp.wait_ge(stored, 16 * 4)

        @block.gpsimd
        def _(gp):
            def triangle(tile, fill, op, row=-1, column=1):
                return nc.gpsimd.affine_select(out=tile, in_=tile, compare_op=op, fill=fill, base=0,
                                               pattern=[[column, P]], channel_multiplier=row)
            nc.gpsimd.memset(ident[:, :], 0.0).then_inc(gp_step, 1)
            gp.wait_ge(gp_step, 1)
            triangle(ident[:, :], 1.0, ALU.not_equal).then_inc(consts_ready, 1)
            for i, row in ((1, dense_norm[0]), (2, conv_norm[0])):
                gp.dma_start(bc[:, i, :], row.partition_broadcast(P)).then_inc(bc_in[i], 16)
            gp.dma_start(wf[:, :, :], w_fgate[0].rearrange("(k p) n -> p k n", p=P)).then_inc(small_in[0], 16)
            gp.dma_start(bf_bc[:, :], b_fgate[0].partition_broadcast(P)).then_inc(small_in[1], 16)
            gp.dma_start(wr[:, :, :], w_router[0].rearrange("(k p) n -> p k n", p=P)).then_inc(small_in[2], 16)
            for i, (tile, value) in enumerate((
                    (ones[:, :], 1.0), (mean_w[:, :], 1.0 / D), (upto[:, :], 1.0),
                    (before[:, :], 1.0), (mask[:, :], 0.0), (c_pad[:, :, :], 0.0), (zero_r[:, :].bitcast(f32), 0.0),
                    (ones_r[:, :].bitcast(f32), 1.0), (wf_cat[:, KD * 2 * H:].bitcast(f32), 0.0),
                    (wr_cat[:, KD * 2 * E:].bitcast(f32), 0.0),
                    (q_even[P // 2:P, :, :], 0.0), (q_odd[0:P // 2, :, :], 0.0))):
                if i:
                    gp.wait_ge(gp_step, i + 1)
                else:
                    gp.wait_ge(consts_ready, 1)
                nc.gpsimd.memset(tile, value).then_inc(gp_step, 1)
            gp.wait_ge(gp_step, 13)
            nc.gpsimd.iota(iota_i[:, :], [[1, P]], base=1, channel_multiplier=0).then_inc(gp_step, 1)
            gp.wait_ge(gp_step, 14)
            nc.gpsimd.iota(iota_c[:, :], [[0, 1]], base=1, channel_multiplier=1).then_inc(gp_step, 1)
            gp.wait_ge(gp_step, 15)
            triangle(upto[:, :], 0.0, ALU.is_ge).then_inc(consts_ready, 1)
            gp.wait_ge(consts_ready, 2)
            triangle(before[:, :], 0.0, ALU.is_gt).then_inc(consts_ready, 1)
            gp.wait_ge(consts_ready, 3)
            triangle(mask[:, P:2 * P], MASKED, ALU.is_ge, row=1, column=-1).then_inc(consts_ready, 1)
            gp.wait_ge(consts_ready, 4)
            nc.gpsimd.tensor_copy(slot_row[:, :], iota_i[:, :]).then_inc(consts_ready, 1)
            gp.wait_ge(consts_ready, 5)
            nc.gpsimd.tensor_copy(slot_col[:, :], iota_c[:, :]).then_inc(consts_ready, 1)
            gp.wait_ge(consts_ready, 6)

            gp.wait_ge(rows_ready, 8)
            nc.gpsimd.memset(prm[:, :, :], 0.0).then_inc(prm_clear, 1)
            gp.wait_ge(prm_clear, 1)
            nc.gpsimd.memset(glu[:, :, 0:PAD], 0.0).then_inc(glu_clear, 1)
            taps = w_dw[0].rearrange("a (b c) -> (a b) c", c=P)
            gp.dma_start(prm[:, 0, :], taps[0:P, :]).then_inc(prm_in, 16)
            gp.dma_start(prm[0:WD - P, 1, :], taps[P:WD, :]).then_inc(prm_in, 16)
            at = 0
            for v, n in ((b_pw1, 2 * KD), (b_dw, KD), (conv_ln_g, KD), (conv_ln_b, KD)):
                gp.dma_start(prm[at:at + n, 2, :], v[0].rearrange("(b c) -> b c", c=P)).then_inc(prm_in, 16)
                at += n
            gp.dma_start(bc[:, 0, :], moe_norm[0].partition_broadcast(P)).then_inc(bc_in[3], 16)
            gp.wait_ge(rows_ready, 12)
            gp.dma_start(bc[:, 1, :], final_norm.partition_broadcast(P)).then_inc(bc_in[4], 16)
            gp.wait_ge(rows_ready, 16)
            gp.dma_start(bc[:, 2, :], b_pw2[0].partition_broadcast(P)).then_inc(bc_in[5], 16)

            gp.wait_ge(c_ready, 20)
            gp.wait_ge(glu_clear, 1)
            nc.gpsimd.memset(y_hi[:, :].bitcast(f32), 0.0).then_inc(zeros_ready, 1)
            gp.wait_ge(zeros_ready, 1)
            nc.gpsimd.memset(y_lo[:, :].bitcast(f32), 0.0).then_inc(zeros_ready, 1)
            gp.wait_ge(zeros_ready, 2)
            nc.gpsimd.memset(put[:, :].bitcast(f32), 0.0).then_inc(y_ready, 1)

        @block.scalar
        def _(act):
            def high(s, r=0):
                act.wait_ge(raw_in[s % RAW], 16 * (s // RAW + 1) + 16 * r)
                if s >= SPLIT or not isinstance(r, int):
                    act.wait_ge(unit_used, s - SPLIT + 1 + RAW * r)
                nc.scalar.copy(w_hi[:, s % SPLIT, :], raw[:, s % RAW, :]).then_inc(hi_ready, 1)

            def norm_sums(k, order):
                nc.scalar.activation(tick[:, 1:2], tick[:, 0:1], ACT.Sqrt)
                for i, (t, h) in enumerate(order):
                    if k == 0:
                        act.wait_ge(x_in_sem[t], 16)
                    else:
                        act.wait_ge(x_ready, 4 * (k - 1) + i + 1)
                    nc.scalar.activation(rows[:, t, h * NC:(h + 1) * NC], x[:, t, h * NC:(h + 1) * NC], ACT.Square,
                                         accum_out=ss[:, t, h:h + 1]).then_inc(ss_ready, 1)
                act.wait_ge(ms_ready, k + 1)
                nc.scalar.activation(rt[:, :], ms[:, :], ACT.Sqrt).then_inc(rt_ready, 1)

            def turned_high(k, bank):
                for g, (t, half) in enumerate(BY_HALF):
                    act.wait_ge(turn_mm, 4 * k + g + 1)
                    nc.scalar.copy(c_hi[:, 4 * half:4 * half + 4, t * P:(t + 1) * P],
                                   ps[:, bank + g, :].rearrange("p (b m) -> p b m", b=4)).then_inc(c_hi_ready, 1)

            def hid_high(q, tiles, up):
                act.wait_ge(hidT_mm, q + 1)
                nc.scalar.copy(h_hi[:, 0:tiles].rearrange("p t b m -> p t (b m)"),
                               ps[:, up:up + tiles, :]).then_inc(h_hi_ready, 1)

            def silu(s, tiles, gate_bank, r):
                act.wait_ge(unit_used, s + 2 + RAW * r)
                nc.scalar.activation(gate[:, 0:tiles, :], ps[:, gate_bank:gate_bank + tiles, :],
                                     ACT.Silu).then_inc(silu_ready, 1)

            def swiglu_first(s, q, L, r=0):
                high(s + 2, r)
                high(s + 3, r)
                silu(s, L["tiles"], L["gate"], r)
                high(s + 4, r)
                high(s + 5, r)

            def swiglu_loop(s, q, L, r=0):
                with act.Fori(0, CH - 1) as i:
                    hid_high(q + i, L["tiles"], L["up"])
                    high(s + 6, r + i)
                    high(s + 7, r + i)
                    silu(s + 4, L["tiles"], L["gate"], r + i)
                    for j in range(8, 12):
                        high(s + j, r + i)

            act.wait_ge(tick_ready, 1)
            norm_sums(0, BY_TILE)
            high(0)
            turned_high(0, 4)
            high(1)
            high(2)
            act.wait_ge(small_in[0], 16)
            nc.scalar.copy(wf_parts[:, :, 0, :], wf[:, :, :]).then_inc(small_hi, 1)
            act.wait_ge(small_in[2], 16)
            nc.scalar.copy(wr_parts[:, :, 0, :], wr[:, :, :]).then_inc(small_hi, 1)

            for g in range(4):
                high(2 * g + 3)
                if g < 2:
                    act.wait_ge(unit_used, U_QKV + 2 * g + 2)
                    if g == 0:
                        act.wait_ge(gp_step, 15)
                    cols = slice(4 * g, 4 * g + 4)
                    banks = slice(4 * g, 4 * g + 4)
                    nc.scalar.activation(q_even[0:HD, cols, :], ps[0:HD, banks, 0:SEQ], ACT.Copy,
                                         scale=HD ** -0.5)
                    nc.scalar.activation(q_odd[HD:P, cols, :], ps[HD:P, banks, 0:SEQ], ACT.Copy,
                                         scale=HD ** -0.5).then_inc(q_out, 1)
                high(2 * g + 4)
            high(U_QKV + 11)
            act.wait_ge(z_ready, 1)
            nc.scalar.activation(z_exp[:, :, :], z_abs[:, :, :], ACT.Exp, scale=-1.0).then_inc(z_exp_ready, 1)
            act.wait_ge(z_exp_ready, 1)
            nc.scalar.activation(z_log[:, :, :], z_exp[:, :, :], ACT.Ln, bias=1.0).then_inc(z_log_ready, 1)
            for h in range(2):
                act.wait_ge(unit_used, U_QKV + 10 + 2 * h)
                nc.scalar.copy(v_sb[:, :, h * NC:(h + 1) * NC], ps[:, 2 * h:2 * h + 2, :]).then_inc(v_out, 1)
                if h == 0:
                    high(U_WO)
                    high(U_WO + 1)

            def prob_T(h):
                act.wait_ge(prT_mm, h + 1)
                if h >= 2:
                    act.wait_ge(pv_mm, h - 1)
                nc.scalar.copy(pr_T[:, h % 2, :], ps[:, 2 + h % 2, 0:3 * P]).then_inc(prT_ready, 1)

            for h in range(H):
                if h >= 2:
                    prob_T(h - 2)
                if h == 4:
                    high(U_WO + 2)
                act.wait_ge(max_ready, h + 1)
                if h >= 2:
                    act.wait_ge(prT_mm, h - 1)
                nc.scalar.activation(pr[:, h % 2, 0:P], sm[:, h % 2, 0:P], ACT.Exp, bias=nm[:, h, 0:1],
                                     accum_out=psum_rows[:, 0, h:h + 1])
                nc.scalar.activation(pr[:, h % 2, P:3 * P], sm[:, h % 2, P:3 * P], ACT.Exp, bias=nm[:, h, 1:2],
                                     accum_out=psum_rows[:, 1, h:h + 1]).then_inc(exp_ready, 1)
            prob_T(H - 2)
            prob_T(H - 1)
            turned_high(1, 0)
            high(U_WO + 3)
            for s in range(U_WO + 4, U_WO + 6):
                high(s)

            norm_sums(1, BY_HALF)
            turned_high(2, 4)
            swiglu_first(U_DENSE, 0, DENSE)
            swiglu_loop(U_DENSE, 0, DENSE)
            hid_high(CH - 1, T, DENSE["up"])
            high(U_PW1)
            high(U_PW1 + 1)

            norm_sums(2, BY_TILE)
            turned_high(3, 4)
            high(U_PW1 + 2)

            def tap_diagonals(first, count):
                for i in range(first, first + count):
                    c = PE_BLOCKS[i // PE_TAPS]
                    col = (DVE_TAPS + i % PE_TAPS) * KD + c
                    if i >= DIAG:
                        act.wait_ge(diag_used, i - DIAG + 1)
                    nc.scalar.activation(diag[:, i % DIAG, :], ident[:, :], ACT.Copy,
                                         scale=prm_T[:, col:col + 1]).then_inc(diag_ready, 1)

            for j in range(2):
                high(U_PW1 + 4 * j + 3)
                high(U_PW1 + 4 * j + 4)
                act.wait_ge(unit_used, U_PW1 + 4 * j + 2)
                if j == 0:
                    act.wait_ge(prm_ready, 1)
                else:
                    act.wait_ge(glu_ready, 4)
                for c in range(4):
                    ch = A_PW1 + KD + 4 * j + c
                    nc.scalar.activation(sig[:, c, :], ps[:, c, 0:SEQ], ACT.Sigmoid,
                                         bias=prm_T[:, ch:ch + 1]).then_inc(sig_ready, 1)
                high(U_PW1 + 4 * j + 5)
                if j == 1:
                    tap_diagonals(0, 12)
                high(U_PW1 + 4 * j + 6)
            tap_diagonals(12, PE_TAPS - 12)
            for b in range(1, KD):
                tap_diagonals(b * PE_TAPS, PE_TAPS)
                c = PE_BLOCKS[b - 1]
                if c >= KD // 2:
                    act.wait_ge(diag_used, b * PE_TAPS)
                    nc.scalar.activation(cv[:, c, :], ps[:, c, 0:SEQ], ACT.Identity,
                                         bias=prm_T[:, A_DW + c:A_DW + c + 1]).then_inc(base_ready, 1)
            nc.scalar.activation(tick[:, 1:2], tick[:, 0:1], ACT.Sqrt)
            for i in range(KD // 2):
                act.wait_ge(dev_ready, i + 1)
                nc.scalar.activation(sq[:, 2 * i:2 * i + 2, :], cv[:, 2 * i:2 * i + 2, :],
                                     ACT.Square).then_inc(sq_ready, 1)
            act.wait_ge(var_ready, 1)
            nc.scalar.activation(std[:, :], var_e[:, :], ACT.Sqrt).then_inc(std_ready, 1)
            for c in range(KD):
                act.wait_ge(ln_ready, c // 2 + 1)
                nc.scalar.activation(sq[:, c, :], cv[:, c, :], ACT.Silu, bias=prm_T[:, A_B + c:A_B + c + 1],
                                     scale=prm_T[:, A_G + c:A_G + c + 1]).then_inc(act_ready, 1)
                if c % 2:
                    act.wait_ge(act_ready, c + 1)
                    nc.scalar.copy(c_hi[:, c - 1:c + 1, :], sq[:, c - 1:c + 1, :]).then_inc(c_hi_ready, 1)
            for s in range(U_PW2 + 3, U_EXP + 2):
                high(s)

            norm_sums(3, BY_HALF)
            turned_high(4, 0)
            for t in range(T):
                act.wait_ge(rows_ready, 20)
                nc.scalar.copy(r_hi[:, t, :], rows[:, t, :]).then_inc(r_hi_ready, 1)
            high(U_EXP + 2)
            act.wait_ge(dlt_ready, 1)
            nc.scalar.activation(ex[:, :], dlt[:, :], ACT.Exp).then_inc(ex_ready, 1)

            def gathered(n, quarter, bank):
                act.wait_ge(gather_mm, n)
                dst = c_hi if quarter == 0 else c_lo
                nc.scalar.copy(dst[:, 0:4, 0:P],
                               ps[:, bank, :].rearrange("p (b m) -> p b m", b=4)).then_inc(gather_a, 1)

            gathered(1, 0, 0)
            gathered(2, 2, 2)

            def expert_pass(p, more=True):
                r, q = ROUNDS * p, CH + CH * p
                high(U_EXP + 3, r)
                silu(U_EXP, 1, EXPERT["gate"], r)
                high(U_EXP + 4, r)
                high(U_EXP + 5, r)
                swiglu_loop(U_EXP, q, EXPERT, r)
                hid_high(q + CH - 1, 1, EXPERT["up"])
                if more:
                    gathered(4 * p + 5, 0, 0)
                    high(U_EXP + U_PASS, r)
                    gathered(4 * p + 7, 2, 0)
                    high(U_EXP + U_PASS + 1, r)
                act.wait_ge(unit_used, U_EXP + U_PASS + RAW * r)
                act.wait_ge(slot_w_ready, p + 1)
                nc.scalar.activation(y_hi[:, :], ps[:, 2:4, :].rearrange("p b n -> p (b n)"), ACT.Copy,
                                     scale=slot_w[:, 0:1]).then_inc(y_hi_ready, 1)
                if more:
                    high(U_EXP + U_PASS + 2, r)

            with act.Fori(0, E - 1) as p:
                expert_pass(p)
            act.wait_ge(plan_ready, 1)
            extra = act.value_load(plan[0:1, EXTRA:EXTRA + 1], min_val=0, max_val=EXTRA - 1)
            with act.If(extra > 0):
                with act.Fori(0, extra) as j:
                    expert_pass(j + (E - 1))
            expert_pass(extra + (E - 1), more=False)
            norm_sums(4, BY_TILE)

        @block.vector
        def _(dve):
            chain = [0]

            def link(ins):
                chain[0] += 1
                ins.then_inc(dve_step, 1)
                dve.wait_ge(dve_step, chain[0])

            def low(s, r=0):
                dve.wait_ge(hi_ready, s + 1 + RAW * r)
                nc.vector.tensor_tensor(w_lo[:, s % SPLIT, :], raw[:, s % RAW, :], w_hi[:, s % SPLIT, :],
                                        ALU.subtract).then_inc(split_ready, 1)

            def norm(k, slot, gain_in):
                dve.wait_ge(ss_ready, 4 * (k + 1))
                link(nc.vector.tensor_tensor(ms[:, :], ss[:, :, 0], ss[:, :, 1], ALU.add))
                nc.vector.tensor_scalar(ms[:, :], ms[:, :], 1.0 / D, EPS, ALU.mult, ALU.add).then_inc(ms_ready, 1)
                dve.wait_ge(rt_ready, k + 1)
                dve.wait_ge(ms_ready, k + 1)
                link(nc.vector.reciprocal(rs[:, :], rt[:, :]))
                link(nc.vector.scalar_tensor_tensor(rq[:, :], rs[:, :], -0.5, rs[:, :], ALU.mult, ALU.mult))
                link(nc.vector.tensor_tensor(rq[:, :], rq[:, :], ms[:, :], ALU.mult))
                link(nc.vector.scalar_tensor_tensor(rs[:, :], rq[:, :], 1.5, rs[:, :], ALU.add, ALU.mult))
                dve.wait_ge(gain_in, 16)
                for t, h in BY_HALF:
                    at = slice(h * NC, (h + 1) * NC)
                    nc.vector.scalar_tensor_tensor(rows[:, t, at], x[:, t, at], rs[:, t:t + 1], bc[:, slot, at],
                                                   ALU.mult, ALU.mult).then_inc(rows_ready, 1)

            def turned_low(k, bank, base):
                for g, (t, half) in enumerate(BY_HALF):
                    dve.wait_ge(c_hi_ready, base + g + 1)
                    nc.vector.tensor_tensor(c_lo[:, 4 * half:4 * half + 4, t * P:(t + 1) * P],
                                            ps[:, bank + g, :].rearrange("p (b m) -> p b m", b=4),
                                            c_hi[:, 4 * half:4 * half + 4, t * P:(t + 1) * P],
                                            ALU.subtract).then_inc(c_ready, 1)

            def add_quarter(t, h, bank):
                nc.vector.tensor_tensor(x[:, t, h * NC:(h + 1) * NC], x[:, t, h * NC:(h + 1) * NC], ps[:, bank, :],
                                        ALU.add).then_inc(x_ready, 1)

            def add_projection(s, h, done):
                if h == 0:
                    dve.wait_ge(unit_used, s + 2)
                    add_quarter(0, 0, 4)
                    add_quarter(1, 0, 5)
                else:
                    dve.wait_ge(bank_done, done)
                    add_quarter(0, 1, 6)
                    dve.wait_ge(unit_used, s + 4)
                    add_quarter(1, 1, 7)

            def hid_low(q, tiles, up):
                dve.wait_ge(h_hi_ready, q + 1)
                nc.vector.tensor_tensor(h_lo[:, 0:tiles].rearrange("p t b m -> p t (b m)"),
                                        ps[:, up:up + tiles, :],
                                        h_hi[:, 0:tiles].rearrange("p t b m -> p t (b m)"),
                                        ALU.subtract).then_inc(h_ready, 1)

            def hidden(s, q, tiles, up, r):
                dve.wait_ge(unit_used, s + 2 + RAW * r)
                dve.wait_ge(silu_ready, q + 1)
                nc.vector.tensor_tensor(hid[:, 0:tiles, :], gate[:, 0:tiles, :], ps[:, up:up + tiles, :],
                                        ALU.mult).then_inc(hid_ready, 1)

            def swiglu_first(s, q, L, r=0):
                for j in range(2, 6):
                    low(s + j, r)
                hidden(s + 2, q, L["tiles"], L["up"], r)

            def swiglu_loop(s, q, L, r=0):
                with dve.Fori(0, CH - 1) as i:
                    hid_low(q + i, L["tiles"], L["up"])
                    for j in range(6, 10):
                        low(s + j, r + i)
                    hidden(s + 6, q + 1 + i, L["tiles"], L["up"], r + i)
                    low(s + 10, r + i)
                    low(s + 11, r + i)
                hid_low(q + CH - 1, L["tiles"], L["up"])

            nc.vector.memset(tick[:, :], 1.0).then_inc(tick_ready, 1)
            norm(0, 0, bc_in[0])
            low(0)
            turned_low(0, 4, 0)
            low(1)
            low(2)
            dve.wait_ge(small_hi, 1)
            nc.vector.tensor_tensor(wf_parts[:, :, 1, :], wf[:, :, :], wf_parts[:, :, 0, :],
                                    ALU.subtract).then_inc(small_split, 1)
            dve.wait_ge(small_hi, 2)
            nc.vector.tensor_tensor(wr_parts[:, :, 1, :], wr[:, :, :], wr_parts[:, :, 0, :],
                                    ALU.subtract).then_inc(small_split, 1)

            for g in range(4):
                low(2 * g + 3)
                if g in (2, 3):
                    dve.wait_ge(unit_used, U_QKV + 2 * g + 2)
                    banks = slice(4 * (g % 2), 4 * (g % 2) + 4)
                    nc.vector.tensor_copy(k_T[:, 4 * (g - 2):4 * (g - 2) + 4, :],
                                          ps[:, banks, 0:SEQ]).then_inc(k_out, 1)
                low(2 * g + 4)

            dve.wait_ge(consts_ready, 6)
            nc.vector.tensor_copy(ident_r[:, :], ident[:, :])
            dve.wait_ge(narrow_mm, 1)
            nc.vector.tensor_copy(narrow[0:2 * H, :], ps[0:2 * H, 4, 0:SEQ]).then_inc(narrow_out, 1)
            low(U_QKV + 11)
            dve.wait_ge(fg_mm, 1)
            dve.wait_ge(small_in[1], 16)
            link(nc.vector.tensor_tensor(z[:, :, :], ps[:, 5, 0:T * H].rearrange("p (t h) -> p t h", t=T),
                                         bf_bc[:, None, :].to_broadcast([P, T, H]), ALU.add))
            nc.vector.tensor_scalar(z_min[:, :, :], z[:, :, :], 0.0, None, ALU.min)
            nc.vector.scalar_tensor_tensor(z_abs[:, :, :], z[:, :, :], -1.0, z[:, :, :],
                                           ALU.mult, ALU.max).then_inc(z_ready, 1)
            dve.wait_ge(z_log_ready, 1)
            dve.wait_ge(z_ready, 1)
            nc.vector.tensor_tensor(log_f[:, :, :], z_min[:, :, :], z_log[:, :, :],
                                    ALU.subtract).then_inc(log_f_ready, 1)
            dve.wait_ge(c_mm, 1)
            dve.wait_ge(gp_step, 15)
            nc.vector.tensor_copy(c_pad[:, :, 0:H], ps[:, 6, 0:T * H].rearrange("p (t h) -> p t h", t=T))\
              .then_inc(c_out, 1)
            low(U_WO)
            dve.wait_ge(cT_mm, 1)
            link(nc.vector.tensor_scalar(narrow[:, :], ps[:, 7, 0:SEQ], -1.0, None, ALU.mult))
            link(nc.vector.tensor_copy(neg_c_hi[:, :], narrow[:, :]))
            nc.vector.tensor_tensor(neg_c_lo[:, :], narrow[:, :], neg_c_hi[:, :], ALU.subtract).then_inc(cT_out, 1)
            low(U_WO + 1)
            dve.wait_ge(c_out, 1)
            dve.wait_ge(consts_ready, 6)
            for h in range(H):
                if h == 6:
                    low(U_WO + 2)
                dve.wait_ge(s_mm, h + 1)
                if h >= 2:
                    dve.wait_ge(exp_ready, h - 1)
                nc.vector.scalar_tensor_tensor(sm[:, h % 2, 0:P], ps[:, h % 2, 0:P], c_pad[:, 0, h:h + 1],
                                               mask[:, P:2 * P], ALU.add, ALU.add)
                nc.vector.scalar_tensor_tensor(sm[:, h % 2, P:3 * P], ps[:, h % 2, P:3 * P], c_pad[:, 1, h:h + 1],
                                               mask[:, :], ALU.add, ALU.add).then_inc(sm_ready, 1)
                dve.wait_ge(sm_ready, h + 1)
                nc.vector.tensor_reduce(nm[:, h, 0:1], sm[:, h % 2, 0:P], AX.X, ALU.max, negate=True)
                nc.vector.tensor_reduce(nm[:, h, 1:2], sm[:, h % 2, P:3 * P], AX.X, ALU.max,
                                        negate=True).then_inc(max_ready, 1)
            dve.wait_ge(exp_ready, H)
            link(nc.vector.reciprocal(inv_rows[:, :, :], psum_rows[:, :, :]))
            dve.wait_ge(pv_mm, H)
            for t, h in BY_HALF:
                heads = slice(h * H // 2, (h + 1) * H // 2)
                nc.vector.tensor_tensor(rows[:, t, h * NC:(h + 1) * NC].rearrange("p (h d) -> p h d", d=HD),
                                        ps[:, 4 + 2 * t + h, :].rearrange("p (h d) -> p h d", d=HD),
                                        inv_rows[:, t, heads, None].to_broadcast([P, H // 2, HD]),
                                        ALU.mult).then_inc(rows_ready, 1)
            turned_low(1, 0, 4)
            low(U_WO + 3)
            low(U_WO + 4)
            add_projection(U_WO, 0, 0)
            low(U_WO + 5)
            add_projection(U_WO, 1, 1)

            norm(1, 1, bc_in[1])
            turned_low(2, 4, 8)
            low(U_DENSE + 2)
            dve.wait_ge(prm_mm, 1)
            nc.vector.tensor_copy(prm_T[:, :], ps[:, 4, 0:3 * P]).then_inc(prm_ready, 1)
            for s in range(U_DENSE + 3, U_DENSE + 6):
                low(s)
            hidden(U_DENSE + 2, 0, T, DENSE["up"], 0)
            swiglu_loop(U_DENSE, 0, DENSE)
            low(U_PW1)
            low(U_PW1 + 1)
            for i, (t, h) in enumerate(BY_TILE):
                if i < 3:
                    dve.wait_ge(bank_done, 1 + i + 1)
                else:
                    dve.wait_ge(unit_used, U_DENSE + U_PASS)
                add_quarter(t, h, DENSE["y"] + i)

            norm(2, 2, bc_in[2])
            turned_low(3, 4, 12)
            low(U_PW1 + 2)
            dve.wait_ge(prm_ready, 1)
            dve.wait_ge(glu_clear, 1)
            steps, step_of = [0], {}

            def conv_tap(c, tap):
                src = glu[:, c, tap:tap + SEQ]
                wt = prm_T[:, tap * KD + c:tap * KD + c + 1]
                if tap:
                    dve.wait_ge(conv_step, step_of[c])
                elif c >= KD // 2:
                    dve.wait_ge(base_ready, c - KD // 2 + 1)
                if tap == 0 and c < KD // 2:
                    ins = nc.vector.tensor_scalar(cv[:, c, :], src, wt, prm_T[:, A_DW + c:A_DW + c + 1],
                                                  ALU.mult, ALU.add)
                else:
                    ins = nc.vector.scalar_tensor_tensor(cv[:, c, :], src, wt, cv[:, c, :], ALU.mult, ALU.add)
                if c >= KD // 2 and tap == DVE_TAPS - 1:
                    ins.then_inc(conv_out, 1)
                else:
                    ins.then_inc(conv_step, 1)
                    steps[0] += 1
                    step_of[c] = steps[0]

            def conv_taps(blocks, first, last):
                for tap in range(first, last):
                    for c in blocks:
                        conv_tap(c, tap)

            for j in range(2):
                for i, s in enumerate(range(U_PW1 + 4 * j + 3, U_PW1 + 4 * j + 6)):
                    low(s)
                    if j == 1:
                        if i == 0:
                            dve.wait_ge(glu_ready, KD // 2)
                        conv_taps(range(KD // 2), 2 * i, 2 * i + 2)
                dve.wait_ge(unit_used, U_PW1 + 4 * j + 4)
                for c in range(4):
                    ch = A_PW1 + 4 * j + c
                    dve.wait_ge(sig_ready, 4 * j + c + 1)
                    nc.vector.scalar_tensor_tensor(glu[:, 4 * j + c, PAD:PAD + SEQ], ps[:, 4 + c, 0:SEQ],
                                                   prm_T[:, ch:ch + 1], sig[:, c, :],
                                                   ALU.add, ALU.mult).then_inc(glu_ready, 1)
                low(U_PW1 + 4 * j + 6)
            conv_taps(range(KD // 2), 6, DVE_TAPS)
            dve.wait_ge(glu_ready, KD)
            def add_taps(c):
                dve.wait_ge(diag_used, (PE_BLOCKS.index(c) + 1) * PE_TAPS)
                dve.wait_ge(conv_step, step_of[c])
                nc.vector.tensor_tensor(cv[:, c, :], cv[:, c, :], ps[:, c, 0:SEQ], ALU.add).then_inc(conv_out, 1)

            conv_taps((4, 5), 0, DVE_TAPS)
            add_taps(0)
            add_taps(1)
            conv_taps((6, 7), 0, DVE_TAPS - 3)
            add_taps(2)
            add_taps(3)
            conv_taps((6, 7), DVE_TAPS - 3, DVE_TAPS)

            dve.wait_ge(mean_mm, 1)
            dve.wait_ge(conv_out, KD)
            for i in range(KD // 2):
                two = cv[:, 2 * i:2 * i + 2, :]
                nc.vector.tensor_tensor(two, two, ps[:, 4:5, 0:SEQ].to_broadcast([P, 2, SEQ]),
                                        ALU.subtract).then_inc(dev_ready, 1)
            dve.wait_ge(var_mm, 1)
            nc.vector.tensor_scalar(var_e[:, :], ps[:, 5, 0:SEQ], EPS, None, ALU.add).then_inc(var_ready, 1)
            dve.wait_ge(std_ready, 1)
            link(nc.vector.reciprocal(rstd[:, :], std[:, :]))
            dve.wait_ge(dev_ready, KD // 2)
            for i in range(KD // 2):
                two = cv[:, 2 * i:2 * i + 2, :]
                nc.vector.tensor_tensor(two, two, rstd[:, None, :].to_broadcast([P, 2, SEQ]),
                                        ALU.mult).then_inc(ln_ready, 1)
            for i in range(KD // 2):
                dve.wait_ge(c_hi_ready, 16 + i + 1)
                nc.vector.tensor_tensor(c_lo[:, 2 * i:2 * i + 2, :], sq[:, 2 * i:2 * i + 2, :],
                                        c_hi[:, 2 * i:2 * i + 2, :], ALU.subtract).then_inc(c_ready, 1)
            dve.wait_ge(bc_in[5], 16)
            link(nc.vector.tensor_tensor(x[:, :, :], x[:, :, :], bc[:, 2:3, :].to_broadcast([P, T, D]), ALU.add))
            low(U_PW2 + 3)
            low(U_PW2 + 4)
            add_projection(U_PW2, 0, 0)
            low(U_PW2 + 5)
            add_projection(U_PW2, 1, 5)

            dve.wait_ge(consts_ready, 6)
            nc.vector.tensor_scalar(eight[:, :], slot_row[:, 0:E], -1.0, None, ALU.add)
            link(nc.vector.tensor_tensor(below[:, :, :], slot_row[:, None, 0:E].to_broadcast([P, E, E]),
                                         slot_row[:, 0:E, None].to_broadcast([P, E, E]), ALU.is_lt))

            norm(3, 0, bc_in[3])
            turned_low(4, 0, 20)
            for t in range(T):
                dve.wait_ge(r_hi_ready, t + 1)
                nc.vector.tensor_tensor(r_lo[:, t, :], rows[:, t, :], r_hi[:, t, :], ALU.subtract).then_inc(r_ready, 1)
                if t == 0:
                    dve.wait_ge(narrow_mm, 2)
                    nc.vector.tensor_copy(narrow[0:2 * E, :], ps[0:2 * E, 4, 0:SEQ]).then_inc(narrow_out, 1)
            dve.wait_ge(lg_mm, 1)
            link(nc.vector.tensor_copy(lg[:, :, :], ps[:, 1, 0:T * E].rearrange("p (t e) -> p t e", t=T)))
            for t in range(T):
                one, other = (lg[:, t, None, :].to_broadcast([P, E, E]), lg[:, t, :, None].to_broadcast([P, E, E]))
                nc.vector.tensor_tensor(better[:, t], one, other, ALU.is_gt)
                ins = nc.vector.tensor_tensor(equal[:, t], one, other, ALU.is_equal)
            link(ins)
            for t in range(T):
                ins = nc.vector.tensor_tensor(equal[:, t], equal[:, t], below[:, :, :], ALU.mult)
            link(ins)
            for t in range(T):
                ins = nc.vector.tensor_tensor(better[:, t], better[:, t], equal[:, t], ALU.add)
            link(ins)
            link(nc.vector.tensor_reduce(place[:, :, :], better[:, :, :, :], AX.X, ALU.add))
            nc.vector.tensor_scalar(chosen[:, :, :], place[:, :, :], 2.0, None, ALU.is_lt).then_inc(chosen_ready, 1)
            for j in range(2):
                nc.vector.tensor_scalar(oh[:, j], place[:, :, :], float(j), None, ALU.is_equal)
            for t in range(T):
                ins = nc.vector.max(top[:, t, :], lg[:, t, :])
            link(ins)
            nc.vector.tensor_tensor(dlt[:, :], top[:, :, 1], top[:, :, 0], ALU.subtract).then_inc(dlt_ready, 1)
            dve.wait_ge(rank_mm, 1)
            dve.wait_ge(chosen_ready, 1)
            nc.vector.tensor_scalar(over[:, :], ps[:, 3, T * E:(T + 1) * E], float(CAP), None, ALU.is_gt)
            link(nc.vector.scalar_tensor_tensor(rank[:, :, 0:E],
                                                ps[:, 3, 0:T * E].rearrange("p (t e) -> p t e", t=T), 1.0,
                                                chosen[:, :, :], ALU.add, ALU.mult))

            def make_pick(p):
                for t in range(T):
                    ins = nc.vector.tensor_scalar(pick[:, t, :], slot_row[:, :], rank[:, t, bass.ds(p, 1)], None,
                                                  ALU.is_equal)
                ins.then_inc(pick_ready, 1)

            def make_rank_diagonals(p):
                for t in range(T):
                    ins = nc.vector.tensor_scalar(rank_d[:, t, :], ident[:, :], rank[:, t, bass.ds(p, 1)], None,
                                                  ALU.mult)
                ins.then_inc(rank_d_ready, 1)

            def make_put(p):
                dve.wait_ge(rank_row_mm, p + 1)
                nc.vector.tensor_scalar(put[:, :], ps[:, EXPERT["y"] + 1, 0:SEQ],
                                        slot_col[:, 0:1], None, ALU.is_equal).then_inc(put_ready, 1)

            def gathered(n, quarter, bank):
                dve.wait_ge(gather_mm, n)
                dst = c_hi if quarter == 1 else c_lo
                nc.vector.tensor_copy(dst[:, 4:8, 0:P],
                                      ps[:, bank, :].rearrange("p (b m) -> p b m", b=4)).then_inc(gather_v, 1)

            make_pick(0)
            low(U_EXP + 2)
            dve.wait_ge(ex_ready, 1)
            link(nc.vector.tensor_scalar(p_top[:, 1, :], ex[:, :], 1.0, None, ALU.add))
            link(nc.vector.reciprocal(p_top[:, 0, :], p_top[:, 1, :]))
            link(nc.vector.tensor_tensor(p_top[:, 1, :], p_top[:, 0, :], ex[:, :], ALU.mult))
            nc.vector.tensor_tensor(comb[:, :, 0:E], oh[:, 0], p_top[:, 0, :, None].to_broadcast([P, T, E]), ALU.mult)
            link(nc.vector.tensor_tensor(comb_2[:, :, :], oh[:, 1], p_top[:, 1, :, None].to_broadcast([P, T, E]),
                                         ALU.mult))
            link(nc.vector.tensor_tensor(comb[:, :, 0:E], comb[:, :, 0:E], comb_2[:, :, :], ALU.add))
            gathered(3, 1, 1)
            link(nc.vector.tensor_tensor_scan(nth[:, :], ones[:, 0:E], over[:, :], 0.0, ALU.mult, ALU.add))
            for j in range(EXTRA):
                nc.vector.scalar_tensor_tensor(sel[:, j, :], nth[:, :], float(j + 1), over[:, :],
                                               ALU.is_equal, ALU.mult)
            link(nc.vector.tensor_reduce(plan_f[:, EXTRA:EXTRA + 1], over[:, :], AX.X, ALU.add))
            link(nc.vector.tensor_tensor(prod[:, 0, 0], sel[:, :, :], eight[:, None, :].to_broadcast([P, EXTRA, E]),
                                         ALU.mult))
            link(nc.vector.tensor_reduce(plan_f[:, 0:EXTRA], prod[:, 0, 0], AX.X, ALU.add))
            nc.vector.tensor_copy(plan[:, :], plan_f[:, :]).then_inc(plan_ready, 1)
            gathered(4, 3, 3)
            for i in range(2):
                for t in range(T):
                    ins = nc.vector.tensor_tensor(prod[:, i, t], sel[:, :, :],
                                                  tables[:, i, t, None, 0:E].to_broadcast([P, EXTRA, E]), ALU.mult)
            link(ins)
            link(nc.vector.tensor_reduce(tables[:, :, :, E:PASSES], prod[:, :, :, :, :], AX.X, ALU.add))
            nc.vector.tensor_scalar(rank[:, :, E:PASSES], rank[:, :, E:PASSES], -float(CAP), None, ALU.add)
            link(nc.vector.tensor_copy(comb_r[:, :, :, 0].rearrange("p e t -> p t e"), comb[:, :, :]))
            nc.vector.tensor_tensor(comb_r[:, :, :, 1].rearrange("p e t -> p t e"), comb[:, :, :],
                                    comb_r[:, :, :, 0].rearrange("p e t -> p t e"),
                                    ALU.subtract).then_inc(comb_ready, 1)

            def expert_pass(p, more=True):
                r, q = ROUNDS * p, CH + CH * p
                for s in range(U_EXP + 3, U_EXP + 6):
                    low(s, r)
                hidden(U_EXP + 2, q, 1, EXPERT["up"], r)
                make_rank_diagonals(p)
                dve.wait_ge(slot_w_mm, p + 1)
                nc.vector.tensor_reduce(slot_w[:, 0:1], ps[:, 2, 0:2], AX.X, ALU.add).then_inc(slot_w_ready, 1)
                if more:
                    make_pick(p + 1)
                dve.wait_ge(scatter_mm, p + 1)
                make_put(p)
                swiglu_loop(U_EXP, q, EXPERT, r)
                if more:
                    low(U_EXP + U_PASS, r)
                    gathered(4 * p + 6, 1, 1)
                    low(U_EXP + U_PASS + 1, r)
                    gathered(4 * p + 8, 3, 1)
                dve.wait_ge(y_hi_ready, p + 1)
                nc.vector.scalar_tensor_tensor(y_lo[:, :], ps[:, 2:4, :].rearrange("p b n -> p (b n)"),
                                               slot_w[:, 0:1], y_hi[:, :], ALU.mult, ALU.subtract)\
                  .then_inc(y_ready, 1)
                if more:
                    low(U_EXP + U_PASS + 2, r)

            with dve.Fori(0, E - 1) as p:
                expert_pass(p)
            dve.wait_ge(plan_ready, 1)
            extra = dve.value_load(plan[0:1, EXTRA:EXTRA + 1], min_val=0, max_val=EXTRA - 1)
            with dve.If(extra > 0):
                with dve.Fori(0, extra) as j:
                    expert_pass(j + (E - 1))
            expert_pass(extra + (E - 1), more=False)
            for i, (t, h) in enumerate(BY_TILE):
                dve.wait_ge(moe_mm, i + 1)
                add_quarter(t, h, SUM + i)
            norm(4, 1, bc_in[4])

        @block.tensor
        def _(pe):
            mm = nc.tensor.matmul

            def moving(dst, hi, lo, s, at, start, stop):
                wh, wl = w_hi[:, s % SPLIT, at:at + NC], w_lo[:, s % SPLIT, at:at + NC]
                mm(dst, hi, wh, start=start, stop=False, skip_group_check=True)
                mm(dst, hi, wl, start=False, stop=False, skip_group_check=True)
                return mm(dst, lo, wh, start=False, stop=stop, skip_group_check=True)

            def turn_rows(k, bank):
                for g, (t, half) in enumerate(BY_HALF):
                    pe.wait_ge(rows_ready, 4 * k + g + 1)
                    for b in range(4):
                        at = (4 * half + b) * P
                        last = nc.tensor.transpose(ps[:, bank + g, b * P:(b + 1) * P],
                                                   rows[:, t, at:at + P], ident[:, :])
                    last.then_inc(turn_mm, 1)

            def column_unit(s, half, bank, tiles, r=0, tell=False):
                pe.wait_ge(split_ready, s + 1 + RAW * r)
                for t in range(tiles):
                    for k in range(4):
                        kk = 4 * half + k
                        last = moving(ps[:, bank + t, :], c_hi[:, kk, t * P:(t + 1) * P],
                                      c_lo[:, kk, t * P:(t + 1) * P], s, k * NC, kk == 0, kk == KD - 1)
                    if tell and t < tiles - 1:
                        last.then_inc(bank_done, 1)
                return last.then_inc(unit_used, 1)

            def feature_unit(s, half, bank):
                pe.wait_ge(split_ready, s + 1)
                for k in range(4):
                    kk = 4 * half + k
                    for b in range(4):
                        at = k * NC + b * P
                        wh, wl = w_hi[:, s % SPLIT, at:at + P], w_lo[:, s % SPLIT, at:at + P]
                        dst = ps[:, bank + b, 0:SEQ]
                        mm(dst, wh, c_hi[:, kk, :], start=kk == 0, stop=False)
                        mm(dst, wh, c_lo[:, kk, :], start=False, stop=False)
                        last = mm(dst, wl, c_hi[:, kk, :], start=False, stop=kk == KD - 1)
                return last.then_inc(unit_used, 1)

            def narrow_product(cat, n, cols):
                for k in range(KD):
                    if k % 4 == 0:
                        pe.wait_ge(c_ready, cols + k // 2 + 2)
                    for part in (c_hi, c_lo):
                        last = mm(ps[:, 4, 0:SEQ], cat[:, 2 * n * k:2 * n * k + P], part[:, k, :],
                                  start=k == 0 and part is c_hi, stop=k == KD - 1 and part is c_lo)
                last.then_inc(narrow_mm, 1)

            def narrow_rows(n, bank):
                for t in range(T):
                    for part in range(2):
                        last = mm(ps[:, bank, t * n:(t + 1) * n], narrow[0:2 * n, t * P:(t + 1) * P],
                                  ident[0:2 * n, part * n:(part + 1) * n], start=part == 0, stop=part == 1)
                return last

            def clear(bank, n):
                for b in range(n):
                    last = mm(ps[:, bank + b, :], zero_r[:, 0:P], zero_r[:, :], start=True, stop=False,
                              skip_group_check=True)
                return last

            def keep_warm(n, bank):
                for _ in range(n):
                    mm(ps[:, bank, :], zero_r[:, 0:P], zero_r[:, :], start=True, stop=True, skip_group_check=True)

            def gate_products(s, q, L, r=0):
                column_unit(s, 0, L["gate"], L["tiles"], r)
                column_unit(s + 1, 1, L["gate"], L["tiles"], r)

            def up_products(s, q, L, r=0):
                column_unit(s, 0, L["up"], L["tiles"], r)
                column_unit(s + 1, 1, L["up"], L["tiles"], r)

            def down(s, half, L, r=0, stop=False, tell=False):
                pe.wait_ge(split_ready, s + 1 + RAW * r)
                for i, (t, n) in enumerate(BY_TILE[0:2 * L["tiles"]]):
                    for k in range(2):
                        hi, lo = h_hi[:, t, 2 * half + k, :], h_lo[:, t, 2 * half + k, :]
                        last = moving(ps[:, L["y"] + i, :], hi, lo, s, k * D + n * NC, False, stop and k == 1)
                    if tell and i < 2 * L["tiles"] - 1:
                        last.then_inc(bank_done, 1)
                return last.then_inc(unit_used, 1)

            def turn_hidden(q, L):
                pe.wait_ge(hid_ready, q + 1)
                for t in range(L["tiles"]):
                    for b in range(4):
                        last = nc.tensor.transpose(ps[:, L["up"] + t, b * P:(b + 1) * P],
                                                   hid[:, t, b * P:(b + 1) * P], ident[:, :])
                last.then_inc(hidT_mm, 1)

            def swiglu_loop(s, q, L, r=0):
                with pe.Fori(0, CH - 1) as i:
                    gate_products(s + 4, q + 1 + i, L, r + i)
                    pe.wait_ge(h_ready, q + 1 + i)
                    up_products(s + 6, q + 1 + i, L, r + i)
                    down(s + 8, 0, L, r + i)
                    down(s + 9, 1, L, r + i)
                    turn_hidden(q + 1 + i, L)

            pe.wait_ge(consts_ready, 1)
            for _ in range(26):
                mm(ps[:, 0, 0:P], ident[:, :], ident[:, :], start=True, stop=True, skip_group_check=True)
            turn_rows(0, 4)
            for g in range(4):
                if g >= 2:
                    pe.wait_ge(q_out, g - 1)
                for half in range(2):
                    if g == 0:
                        pe.wait_ge(c_ready, 2 * half + 2)
                    feature_unit(U_QKV + 2 * g + half, half, 4 * (g % 2))
            pe.wait_ge(k_out, 1)
            column_unit(U_QKV + 8, 0, 0, T)
            pe.wait_ge(consts_ready, 6)
            pe.wait_ge(gp_step, 15)
            pe.wait_ge(k_out, 2)
            pe.wait_ge(small_split, 2)
            narrow_product(wf_cat, H, 0)
            column_unit(U_QKV + 9, 1, 0, T)
            pe.wait_ge(narrow_out, 1)
            narrow_rows(H, 5).then_inc(fg_mm, 1)
            column_unit(U_QKV + 10, 0, 2, T)
            pe.wait_ge(log_f_ready, 1)
            for t in range(T):
                dst = ps[:, 6, t * H:(t + 1) * H]
                for u in range(t):
                    mm(dst, ones[:, :], log_f[:, u, :], start=u == 0, stop=False)
                last = mm(dst, upto[:, :], log_f[:, t, :], start=t == 0, stop=True)
            last.then_inc(c_mm, 1)
            pe.wait_ge(c_out, 1)
            for t in range(T):
                last = nc.tensor.transpose(ps[:, 7, t * P:(t + 1) * P], c_pad[:, t, :], ident[:, :])
            last.then_inc(cT_mm, 1)
            column_unit(U_QKV + 11, 1, 2, T)
            pe.wait_ge(cT_out, 1)
            pe.wait_ge(v_out, 1)

            def scores(h):
                q = (q_even, q_odd)[h % 2]
                if h >= 2:
                    pe.wait_ge(sm_ready, h - 1)
                pick_c = ident_r[:, h:h + 1].to_broadcast([P, P])
                for t in range(T):
                    at = P if t else 0
                    n = (t + 1) * P
                    dst = ps[:, h % 2, at:at + n]
                    mm(dst, q[:, h // 2, t * P:(t + 1) * P], k_T[:, h // 2, 0:n], start=True, stop=False)
                    mm(dst, pick_c, neg_c_hi[:, 0:n], start=False, stop=False)
                    last = mm(dst, pick_c, neg_c_lo[:, 0:n], start=False, stop=True)
                last.then_inc(s_mm, 1)

            def turn_probs(h):
                pe.wait_ge(exp_ready, h + 1)
                if h >= 2:
                    pe.wait_ge(prT_ready, h - 1)
                for b in range(3):
                    last = nc.tensor.transpose(ps[:, 2 + h % 2, b * P:(b + 1) * P],
                                               pr[:, h % 2, b * P:(b + 1) * P], ident[:, :])
                last.then_inc(prT_mm, 1)

            def values(h):
                pe.wait_ge(prT_ready, h + 1)
                at = (h * HD) % NC
                for t in range(T):
                    dst = ps[:, 4 + 2 * t + h * HD // NC, at:at + HD]
                    for u in range(t + 1):
                        b = (u + 1) if t else 0
                        last = mm(dst, pr_T[:, h % 2, b * P:(b + 1) * P], v_sb[:, u, h * HD:(h + 1) * HD],
                                  start=u == 0, stop=u == t)
                last.then_inc(pv_mm, 1)

            for step in range(H + 3):
                if step == 2:
                    pe.wait_ge(v_out, 2)
                if step < H:
                    scores(step)
                if 2 <= step < H + 2:
                    turn_probs(step - 2)
                if step >= 3:
                    values(step - 3)

            def projection(s, cols):
                for h in range(2):
                    for half in range(2):
                        if h == 0:
                            pe.wait_ge(c_ready, cols + 2 * half + 2)
                        column_unit(s + 2 * h + half, half, 4 + 2 * h, T, tell=h == 1 and half == 1)

            turn_rows(1, 0)
            projection(U_WO, 4)
            keep_warm(17, 0)

            turn_rows(2, 4)
            pe.wait_ge(c_ready, 10)
            column_unit(U_DENSE, 0, DENSE["gate"], T)
            pe.wait_ge(c_ready, 12)
            column_unit(U_DENSE + 1, 1, DENSE["gate"], T)
            pe.wait_ge(prm_in, 6 * 16)
            for b in range(3):
                last = nc.tensor.transpose(ps[:, 4, b * P:(b + 1) * P], prm[:, b, :], ident[:, :])
            last.then_inc(prm_mm, 1)
            up_products(U_DENSE + 2, 0, DENSE)
            pe.wait_ge(prm_ready, 1)
            clear(DENSE["y"], 2 * T)
            turn_hidden(0, DENSE)
            swiglu_loop(U_DENSE, 0, DENSE)
            pe.wait_ge(h_ready, CH)
            down(U_DENSE + U_PASS - 2, 0, DENSE)
            down(U_DENSE + U_PASS - 1, 1, DENSE, stop=True, tell=True)
            keep_warm(17, 0)

            turn_rows(3, 4)
            for g in range(4):
                if g >= 2:
                    pe.wait_ge((sig_ready, glu_ready)[g % 2], 4)
                for half in range(2):
                    if g == 0:
                        pe.wait_ge(c_ready, 12 + 2 * half + 2)
                    feature_unit(U_PW1 + 2 * g + half, half, 4 * (g % 2))
            pe.wait_ge(sig_ready, KD)
            for i in range(KD * PE_TAPS):
                c, n = PE_BLOCKS[i // PE_TAPS], i % PE_TAPS
                tap = DVE_TAPS + n
                if n == 0:
                    pe.wait_ge(glu_ready, c + 1)
                pe.wait_ge(diag_ready, i + 1)
                mm(ps[:, c, 0:SEQ], diag[:, i % DIAG, :], glu[:, c, tap:tap + SEQ],
                   start=n == 0, stop=n == PE_TAPS - 1).then_inc(diag_used, 1)
            for i, c in enumerate(CONV_DONE):
                pe.wait_ge(conv_out, i + 1)
                last = mm(ps[:, 4, 0:SEQ], mean_w[:, :], cv[:, c, :], start=i == 0, stop=i == KD - 1)
            last.then_inc(mean_mm, 1)
            for c in range(KD):
                pe.wait_ge(sq_ready, c // 2 + 1)
                last = mm(ps[:, 5, 0:SEQ], mean_w[:, :], sq[:, c, :], start=c == 0, stop=c == KD - 1)
            last.then_inc(var_mm, 1)
            keep_warm(28, 0)
            projection(U_PW2, 16)
            keep_warm(17, 0)

            turn_rows(4, 0)
            narrow_product(wr_cat, E, 20)
            pe.wait_ge(c_ready, 24)
            pe.wait_ge(narrow_out, 2)
            narrow_rows(E, 1).then_inc(lg_mm, 1)
            clear(SUM, 2 * T)
            keep_warm(6, 0)
            pe.wait_ge(chosen_ready, 1)
            both = chosen[:, :, :].rearrange("p t e -> p (t e)")
            mm(ps[:, 3, 0:T * E], before[:, :], both, start=True, stop=False, skip_group_check=True)
            mm(ps[:, 3, E:3 * E].rearrange("p (a e) -> p a e", a=2), ones[:, :],
               chosen[:, 0:1, :].to_broadcast([P, 2, E]), start=False, stop=False, skip_group_check=True)
            last = mm(ps[:, 3, 2 * E:3 * E], ones[:, :], chosen[:, 1, :], start=False, stop=True,
                      skip_group_check=True)
            last.then_inc(rank_mm, 1)
            keep_warm(5, 0)

            def gather(quarter, bank):
                src = r_hi if quarter < 2 else r_lo
                for b in range(4):
                    at = (4 * (quarter % 2) + b) * P
                    for t in range(T):
                        last = mm(ps[:, bank, b * P:(b + 1) * P], src[:, t, at:at + P], pick[:, t, :],
                                  start=t == 0, stop=t == T - 1)
                last.then_inc(gather_mm, 1)

            pe.wait_ge(r_ready, T)
            pe.wait_ge(pick_ready, 1)
            for quarter in (0, 2, 1, 3):
                gather(quarter, quarter)

            def scatter(stop=False):
                for i, (t, h) in enumerate(BY_TILE):
                    dst = ps[:, SUM + i, :]
                    mm(dst, put[:, t * P:(t + 1) * P], y_hi[:, h * NC:(h + 1) * NC], start=False, stop=False,
                       skip_group_check=True)
                    last = mm(dst, put[:, t * P:(t + 1) * P], y_lo[:, h * NC:(h + 1) * NC], start=False,
                              stop=stop, skip_group_check=True)
                    if stop:
                        last.then_inc(moe_mm, 1)
                return last

            def expert_pass(p, more=True):
                r, q = ROUNDS * p, CH + CH * p
                pe.wait_ge(gather_a, 2 * p + 2)
                column_unit(U_EXP, 0, EXPERT["gate"], 1, r)
                pe.wait_ge(gather_v, 2 * p + 2)
                column_unit(U_EXP + 1, 1, EXPERT["gate"], 1, r)
                up_products(U_EXP + 2, q, EXPERT, r)
                pe.wait_ge(y_ready, p + 1)
                pe.wait_ge(comb_ready, 1)
                for t in range(T):
                    last = mm(ps[:, EXPERT["y"], 0:2], pick[:, t, :],
                              comb_r[:, bass.ds(p, 1), t, :].rearrange("p a b -> p (a b)"),
                              start=t == 0, stop=t == T - 1)
                last.then_inc(slot_w_mm, 1)
                scatter().then_inc(scatter_mm, 1)
                pe.wait_ge(rank_d_ready, p + 1)
                mm(ps[:, EXPERT["y"] + 1, 0:SEQ], ones_r[:, :], rank_d[:, :, :].rearrange("p t s -> p (t s)"),
                   start=True, stop=True).then_inc(rank_row_mm, 1)
                turn_hidden(q, EXPERT)
                pe.wait_ge(slot_w_ready, p + 1)
                pe.wait_ge(put_ready, p + 1)
                clear(EXPERT["y"], 2)
                swiglu_loop(U_EXP, q, EXPERT, r)
                if more:
                    pe.wait_ge(pick_ready, p + 2)
                    gather(0, 0)
                else:
                    keep_warm(12, EXPERT["gate"])
                pe.wait_ge(h_ready, q + CH)
                down(U_EXP + U_PASS - 2, 0, EXPERT, r)
                if more:
                    gather(1, 1)
                    pe.wait_ge(gather_a, 2 * p + 3)
                    gather(2, 0)
                down(U_EXP + U_PASS - 1, 1, EXPERT, r, stop=True)
                if more:
                    pe.wait_ge(gather_v, 2 * p + 3)
                    gather(3, 1)

            with pe.Fori(0, E - 1) as p:
                expert_pass(p)
            pe.wait_ge(plan_ready, 1)
            extra = pe.value_load(plan[0:1, EXTRA:EXTRA + 1], min_val=0, max_val=EXTRA - 1)
            with pe.If(extra > 0):
                with pe.Fori(0, extra) as j:
                    expert_pass(j + (E - 1))
            expert_pass(extra + (E - 1), more=False)
            keep_warm(10, EXPERT["gate"])
            pe.wait_ge(y_ready, extra + E + 1)
            scatter(stop=True)


_INS = ['x', 'attn_norm', 'w_qkv', 'w_fgate', 'b_fgate', 'w_attn_out', 'conv_norm', 'w_pw1', 'b_pw1', 'w_dw', 'b_dw',
        'conv_ln_g', 'conv_ln_b', 'w_pw2', 'b_pw2', 'dense_norm', 'w_dense_gate', 'w_dense_up', 'w_dense_down',
        'moe_norm', 'w_router', 'w_exp_gate', 'w_exp_up', 'w_exp_down', 'final_norm']


def kernel(**inputs):
    import numpy as _np
    import concourse.bacc as _bacc
    from concourse import mybir as _mybir
    from concourse.bass_utils import run_bass_kernel_spmd as _run

    nc = _bacc.Bacc("TRN2", target_bir_lowering=False, num_devices=1)
    arrays, args = {}, []
    for name in _INS:
        a = _np.ascontiguousarray(inputs[name])
        arrays[f"in_{name}_dram"] = a
        args.append(nc.dram_tensor(f"in_{name}_dram", a.shape, _mybir.dt.from_np(a.dtype), kind="ExternalInput").ap())
    args.append(nc.dram_tensor("out_0_dram", inputs['x'].shape, _mybir.dt.float32, kind="ExternalOutput").ap())
    build_trunk(nc, *args)
    r = _run(nc, [arrays], core_ids=[0])
    return r.results[0]["out_0_dram"]
```
